# Optimizing a Trainium2 kernel written in Bass

```python
import math
import jax, jax.numpy as jnp
from jax import lax
import numpy as np

D_MODEL = 1024
BATCH = 1
SEQ = 256
DEPTH = 2

N_MIXERS = 2
EPS = 1e-6

NSA_HEADS = 16
NSA_KV_GROUPS = 4
NSA_HEAD_DIM = 64
NSA_Q_DIM = NSA_HEADS * NSA_HEAD_DIM
NSA_KV_DIM = NSA_KV_GROUPS * NSA_HEAD_DIM
NSA_IN_COLS = NSA_Q_DIM + 6 * NSA_KV_DIM + 3 * NSA_HEADS
CMP_BLOCK = 32
CMP_STRIDE = 16
CMP_HIDDEN = 256
SEL_BLOCK = 64
SEL_TOP_N = 16
WINDOW = 512
Q_BLOCK = 128
SEL_Q_CHUNK = 16

REL_BUCKETS = 32
REL_MAX_DIST = 128

SSD_EXPAND = 2
SSD_D_INNER = SSD_EXPAND * D_MODEL
SSD_HEAD_DIM = 64
SSD_HEADS = SSD_D_INNER // SSD_HEAD_DIM
SSD_GROUPS = 8
SSD_STATE = 128
SSD_CONV = 4
SSD_CHUNK = 128
SSD_CONV_DIM = SSD_D_INNER + 2 * SSD_GROUPS * SSD_STATE
SSD_IN_COLS = SSD_D_INNER + SSD_CONV_DIM + SSD_HEADS
DT_MIN = 1e-3
DT_MAX = 1e-1

MLP_HIDDEN = 4 * D_MODEL

N_NSA_LAYERS = (DEPTH + 1) // 2
N_SSD_LAYERS = DEPTH // 2

kernel_name = 'nsa_mamba2_interleaved_trunk'

def rmsnorm(x, w):
    x32 = x.astype(jnp.float32)
    y = x32 * lax.rsqrt(jnp.mean(x32 * x32, axis=-1, keepdims=True) + EPS)
    return (y * w.astype(jnp.float32)).astype(x.dtype)

def rel_bucket(dist):
    max_exact = REL_BUCKETS // 2
    d = jnp.maximum(dist, 0)
    df = jnp.maximum(d, 1).astype(jnp.float32)
    large = max_exact + (jnp.log(df / max_exact) / math.log(REL_MAX_DIST / max_exact)
                         * (REL_BUCKETS - max_exact)).astype(jnp.int32)
    large = jnp.minimum(large, REL_BUCKETS - 1)
    return jnp.where(d < max_exact, d, large)

def masked_softmax(s, mask, axis=-1):
    s = jnp.where(mask, s, -jnp.inf)
    m = jnp.max(s, axis=axis, keepdims=True)
    m = jnp.where(jnp.isfinite(m), m, 0.0)
    e = jnp.exp(s - m)
    den = jnp.sum(e, axis=axis, keepdims=True)
    return e / jnp.where(den > 0, den, 1.0)

def compress_blocks(t, idx, pe, w1, w2):
    blocks = t[:, idx] + pe[:, None, :]
    hid = jax.nn.silu(jnp.einsum('bnlgd,lde->bnge', blocks, w1))
    return jnp.einsum('bnge,ed->bngd', hid, w2)

def nsa_mixer(h, w_in, q_gain, k_gain, pe_k, w1_k, w2_k, pe_v, w1_v, w2_v, rel_table, w_out):
    B, S, _ = h.shape
    G, Dh = NSA_KV_GROUPS, NSA_HEAD_DIM
    R = NSA_HEADS // G
    dt = h.dtype
    proj = h @ w_in
    q = rmsnorm(proj[..., :NSA_Q_DIM].reshape(B, S, G, R, Dh), q_gain) * (Dh ** -0.5)
    kv = proj[..., NSA_Q_DIM:NSA_Q_DIM + 6 * NSA_KV_DIM].reshape(B, S, 6, G, Dh)
    k_c, v_c, k_s, v_s, k_w, v_w = (kv[:, :, i] for i in range(6))
    gates = jax.nn.sigmoid(proj[..., NSA_Q_DIM + 6 * NSA_KV_DIM:]).reshape(B, S, 3, G, R)
    table = rel_table.reshape(REL_BUCKETS, G, R)

    n_cmp = (S - CMP_BLOCK) // CMP_STRIDE + 1
    cmp_start = jnp.arange(n_cmp) * CMP_STRIDE
    cmp_idx = cmp_start[:, None] + jnp.arange(CMP_BLOCK)[None, :]
    cmp_end = cmp_start + CMP_BLOCK - 1
    k_cmp = rmsnorm(compress_blocks(k_c, cmp_idx, pe_k, w1_k, w2_k), k_gain)
    v_cmp = compress_blocks(v_c, cmp_idx, pe_v, w1_v, w2_v)

    n_sel = S // SEL_BLOCK
    sel_start = jnp.arange(n_sel) * SEL_BLOCK
    overlap = ((cmp_start[:, None] < sel_start[None, :] + SEL_BLOCK)
               & (cmp_start[:, None] + CMP_BLOCK > sel_start[None, :])).astype(jnp.float32)
    top_n = min(SEL_TOP_N, n_sel)
    ks_blocks = rmsnorm(k_s, k_gain).reshape(B, n_sel, SEL_BLOCK, G, Dh).transpose(0, 3, 1, 2, 4)
    vs_blocks = v_s.reshape(B, n_sel, SEL_BLOCK, G, Dh).transpose(0, 3, 1, 2, 4)
    b_idx = jnp.arange(B)[:, None, None, None]
    g_idx = jnp.arange(G)[None, :, None, None]
    g_idx5 = jnp.arange(G)[None, :, None, None, None]
    blk_ids = jnp.arange(n_sel)

    def cmp_sel_chunk(args):
        q_c, t_c = args
        s = jnp.einsum('bqgrd,bngd->bgrqn', q_c, k_cmp).astype(jnp.float32)
        dist = t_c[:, None] - cmp_end[None, :]
        bias = jnp.transpose(table[rel_bucket(dist)], (2, 3, 0, 1))
        p = masked_softmax(s + bias, dist >= 0)
        o_cmp = jnp.einsum('bgrqn,bngd->bqgrd', p.astype(dt), v_cmp)
        imp = jnp.einsum('bgrqn,nj->bgqj', p, overlap)
        cur = t_c // SEL_BLOCK
        blk_valid = sel_start[None, :] <= t_c[:, None]
        forced = ((blk_ids[None, :] == 0) | (blk_ids[None, :] == cur[:, None])
                  | (blk_ids[None, :] == cur[:, None] - 1))
        score = jnp.where(forced, jnp.inf, imp)
        score = jnp.where(blk_valid, score, -jnp.inf)
        _, sel_idx = lax.top_k(score, top_n)
        k_sel = ks_blocks[b_idx, g_idx, sel_idx]
        v_sel = vs_blocks[b_idx, g_idx, sel_idx]
        key_pos = sel_idx[..., None] * SEL_BLOCK + jnp.arange(SEL_BLOCK)
        dist2 = t_c[None, None, :, None, None] - key_pos
        bias2 = jnp.moveaxis(table[rel_bucket(dist2), g_idx5], -1, 2)
        s2 = jnp.einsum('bqgrd,bgqnld->bgrqnl', q_c, k_sel).astype(jnp.float32)
        p2 = masked_softmax(s2 + bias2, (dist2 >= 0)[:, :, None], axis=(-2, -1))
        o_slc = jnp.einsum('bgrqnl,bgqnld->bqgrd', p2.astype(dt), v_sel)
        return o_cmp, o_slc

    nq = S // SEL_Q_CHUNK
    q_chunks = jnp.swapaxes(q.reshape(B, nq, SEL_Q_CHUNK, G, R, Dh), 0, 1)
    t_chunks = jnp.arange(S).reshape(nq, SEL_Q_CHUNK)
    o_cmp, o_slc = lax.map(cmp_sel_chunk, (q_chunks, t_chunks))
    o_cmp = jnp.swapaxes(o_cmp, 0, 1).reshape(B, S, G, R, Dh)
    o_slc = jnp.swapaxes(o_slc, 0, 1).reshape(B, S, G, R, Dh)

    span = WINDOW + Q_BLOCK
    kw_pad = jnp.pad(rmsnorm(k_w, k_gain), ((0, 0), (WINDOW, 0), (0, 0), (0, 0)))
    vw_pad = jnp.pad(v_w, ((0, 0), (WINDOW, 0), (0, 0), (0, 0)))

    def window_block(args):
        q_b, start = args
        k_b = lax.dynamic_slice_in_dim(kw_pad, start, span, axis=1)
        v_b = lax.dynamic_slice_in_dim(vw_pad, start, span, axis=1)
        t_b = start + jnp.arange(Q_BLOCK)
        key_pos = start - WINDOW + jnp.arange(span)
        dist = t_b[:, None] - key_pos[None, :]
        mask = (dist >= 0) & (dist < WINDOW) & (key_pos[None, :] >= 0)
        s = jnp.einsum('bqgrd,bkgd->bgrqk', q_b, k_b).astype(jnp.float32)
        bias = jnp.transpose(table[rel_bucket(dist)], (2, 3, 0, 1))
        p = masked_softmax(s + bias, mask)
        return jnp.einsum('bgrqk,bkgd->bqgrd', p.astype(dt), v_b)

    nb = S // Q_BLOCK
    q_blocks = jnp.swapaxes(q.reshape(B, nb, Q_BLOCK, G, R, Dh), 0, 1)
    o_win = lax.map(window_block, (q_blocks, jnp.arange(nb) * Q_BLOCK))
    o_win = jnp.swapaxes(o_win, 0, 1).reshape(B, S, G, R, Dh)

    o = (gates[:, :, 0][..., None] * o_cmp + gates[:, :, 1][..., None] * o_slc
         + gates[:, :, 2][..., None] * o_win)
    return o.reshape(B, S, NSA_Q_DIM).astype(dt) @ w_out

def ssd_scan(X, A, Bm, Cm):
    b, S, NH, P = X.shape
    G, N = Bm.shape[-2], Bm.shape[-1]
    J = NH // G
    L = SSD_CHUNK
    c = S // L
    X = X.reshape(b, c, L, G, J, P)
    A = jnp.transpose(A.reshape(b, c, L, G, J), (0, 3, 4, 1, 2))
    Bm = Bm.reshape(b, c, L, G, N)
    Cm = Cm.reshape(b, c, L, G, N)
    A_cs = jnp.cumsum(A, axis=-1)
    tril = jnp.tril(jnp.ones((L, L), dtype=bool))
    decay_in = jnp.exp(jnp.where(tril, A_cs[..., :, None] - A_cs[..., None, :], -jnp.inf))
    cb = jnp.einsum('bclgn,bcsgn->bcgls', Cm, Bm)
    y_diag = jnp.einsum('bcgls,bgjcls,bcsgjp->bclgjp', cb, decay_in, X)
    decay_to_end = jnp.exp(A_cs[..., -1:] - A_cs)
    states = jnp.einsum('bcsgn,bgjcs,bcsgjp->bcgjpn', Bm, decay_to_end, X)
    chunk_decay = jnp.exp(A_cs[..., -1])

    def step(carry, inp):
        st, dec = inp
        return carry * dec[..., None, None] + st, carry

    init = jnp.zeros((b, G, J, P, N), states.dtype)
    _, prev = lax.scan(step, init, (jnp.moveaxis(states, 1, 0), jnp.moveaxis(chunk_decay, -1, 0)))
    prev = jnp.moveaxis(prev, 0, 1)
    y_off = jnp.einsum('bclgn,bcgjpn,bgjcl->bclgjp', Cm, prev, jnp.exp(A_cs))
    return (y_diag + y_off).reshape(b, S, NH, P)

def ssd_mixer(h, w_in, conv_w, conv_b, dt_bias, a_log, d_skip, norm_w, w_out):
    B, S, _ = h.shape
    DI, G, N, NH, P = SSD_D_INNER, SSD_GROUPS, SSD_STATE, SSD_HEADS, SSD_HEAD_DIM
    f32 = jnp.float32
    proj = h @ w_in
    z = proj[..., :DI]
    xbc = proj[..., DI:DI + SSD_CONV_DIM]
    dt_raw = proj[..., DI + SSD_CONV_DIM:]
    xbc = lax.conv_general_dilated(xbc, conv_w[:, None, :], window_strides=(1,),
                                   padding=[(SSD_CONV - 1, 0)],
                                   dimension_numbers=('NWC', 'WIO', 'NWC'),
                                   feature_group_count=SSD_CONV_DIM)
    xbc = jax.nn.silu(xbc + conv_b)
    xs = xbc[..., :DI].reshape(B, S, NH, P).astype(f32)
    Bm = xbc[..., DI:DI + G * N].reshape(B, S, G, N).astype(f32)
    Cm = xbc[..., DI + G * N:].reshape(B, S, G, N).astype(f32)
    dt = jax.nn.softplus((dt_raw + dt_bias).astype(f32))
    A = -jnp.exp(a_log.astype(f32))
    y = ssd_scan(xs * dt[..., None], dt * A, Bm, Cm)
    y = y + xs * d_skip.astype(f32)[:, None]
    y = y.reshape(B, S, DI) * jax.nn.silu(z.astype(f32))
    y = rmsnorm(y.reshape(B, S, G, DI // G), norm_w.reshape(G, DI // G)).reshape(B, S, DI)
    return y.astype(h.dtype) @ w_out

def sqrelu_mlp(h, w_up, w_down):
    return jnp.square(jax.nn.relu(h @ w_up)) @ w_down

def setup_inputs(seed: int = 0) -> dict:
    key = jax.random.key(seed)
    ks = jax.random.split(key, 24)
    f32 = jnp.float32

    def nrm(k, shape, scale):
        return scale * jax.random.normal(k, shape, f32)

    na, nb = N_NSA_LAYERS, N_SSD_LAYERS
    x = jax.random.normal(ks[0], (BATCH, SEQ, D_MODEL), f32)
    norm_mix_w = 1.0 + nrm(ks[1], (DEPTH, D_MODEL), 0.02)
    norm_mlp_w = 1.0 + nrm(ks[2], (DEPTH, D_MODEL), 0.02)
    rel_table = nrm(ks[3], (REL_BUCKETS, NSA_HEADS), 0.2)
    nsa_w_in = nrm(ks[4], (na, D_MODEL, NSA_IN_COLS), D_MODEL ** -0.5)
    nsa_q_gain = 1.0 + nrm(ks[5], (na, NSA_HEAD_DIM), 0.02)
    nsa_k_gain = 1.0 + nrm(ks[6], (na, NSA_HEAD_DIM), 0.02)
    cmp_pe_k = nrm(ks[7], (na, CMP_BLOCK, NSA_HEAD_DIM), 0.1)
    cmp_w1_k = nrm(ks[8], (na, CMP_BLOCK, NSA_HEAD_DIM, CMP_HIDDEN), (CMP_BLOCK * NSA_HEAD_DIM) ** -0.5)
    cmp_w2_k = nrm(ks[9], (na, CMP_HIDDEN, NSA_HEAD_DIM), CMP_HIDDEN ** -0.5)
    cmp_pe_v = nrm(ks[10], (na, CMP_BLOCK, NSA_HEAD_DIM), 0.1)
    cmp_w1_v = nrm(ks[11], (na, CMP_BLOCK, NSA_HEAD_DIM, CMP_HIDDEN), (CMP_BLOCK * NSA_HEAD_DIM) ** -0.5)
    cmp_w2_v = nrm(ks[12], (na, CMP_HIDDEN, NSA_HEAD_DIM), CMP_HIDDEN ** -0.5)
    nsa_w_out = nrm(ks[13], (na, NSA_Q_DIM, D_MODEL), NSA_Q_DIM ** -0.5)
    ssd_w_in = nrm(ks[14], (nb, D_MODEL, SSD_IN_COLS), D_MODEL ** -0.5)
    ssd_conv_w = nrm(ks[15], (nb, SSD_CONV, SSD_CONV_DIM), SSD_CONV ** -0.5)
    ssd_conv_b = nrm(ks[16], (nb, SSD_CONV_DIM), 0.02)
    dt0 = jnp.exp(jax.random.uniform(ks[17], (nb, SSD_HEADS), f32)
                  * (math.log(DT_MAX) - math.log(DT_MIN)) + math.log(DT_MIN))
    ssd_dt_bias = dt0 + jnp.log(-jnp.expm1(-dt0))
    ssd_a_log = jnp.log(jax.random.uniform(ks[18], (nb, SSD_HEADS), f32, 1.0, 16.0))
    ssd_d = 1.0 + nrm(ks[19], (nb, SSD_HEADS), 0.1)
    ssd_norm_w = 1.0 + nrm(ks[20], (nb, SSD_D_INNER), 0.02)
    ssd_w_out = nrm(ks[21], (nb, SSD_D_INNER, D_MODEL), SSD_D_INNER ** -0.5)
    mlp_w_up = nrm(ks[22], (DEPTH, D_MODEL, MLP_HIDDEN), D_MODEL ** -0.5)
    mlp_w_down = nrm(ks[23], (DEPTH, MLP_HIDDEN, D_MODEL), MLP_HIDDEN ** -0.5)
    return {'x': x, 'norm_mix_w': norm_mix_w, 'norm_mlp_w': norm_mlp_w, 'rel_table': rel_table,
            'nsa_w_in': nsa_w_in, 'nsa_q_gain': nsa_q_gain, 'nsa_k_gain': nsa_k_gain,
            'cmp_pe_k': cmp_pe_k, 'cmp_w1_k': cmp_w1_k, 'cmp_w2_k': cmp_w2_k,
            'cmp_pe_v': cmp_pe_v, 'cmp_w1_v': cmp_w1_v, 'cmp_w2_v': cmp_w2_v,
            'nsa_w_out': nsa_w_out, 'ssd_w_in': ssd_w_in, 'ssd_conv_w': ssd_conv_w,
            'ssd_conv_b': ssd_conv_b, 'ssd_dt_bias': ssd_dt_bias, 'ssd_a_log': ssd_a_log,
            'ssd_d': ssd_d, 'ssd_norm_w': ssd_norm_w, 'ssd_w_out': ssd_w_out,
            'mlp_w_up': mlp_w_up, 'mlp_w_down': mlp_w_down}

def reference(x, norm_mix_w, norm_mlp_w, rel_table, nsa_w_in, nsa_q_gain, nsa_k_gain,
              cmp_pe_k, cmp_w1_k, cmp_w2_k, cmp_pe_v, cmp_w1_v, cmp_w2_v, nsa_w_out,
              ssd_w_in, ssd_conv_w, ssd_conv_b, ssd_dt_bias, ssd_a_log, ssd_d, ssd_norm_w,
              ssd_w_out, mlp_w_up, mlp_w_down):
    for i in range(DEPTH):
        hn = rmsnorm(x, norm_mix_w[i])
        li = i // N_MIXERS
        if i % N_MIXERS == 0:
            x = x + nsa_mixer(hn, nsa_w_in[li], nsa_q_gain[li], nsa_k_gain[li],
                              cmp_pe_k[li], cmp_w1_k[li], cmp_w2_k[li],
                              cmp_pe_v[li], cmp_w1_v[li], cmp_w2_v[li],
                              rel_table, nsa_w_out[li])
        else:
            x = x + ssd_mixer(hn, ssd_w_in[li], ssd_conv_w[li], ssd_conv_b[li],
                              ssd_dt_bias[li], ssd_a_log[li], ssd_d[li], ssd_norm_w[li],
                              ssd_w_out[li])
        x = x + sqrelu_mlp(rmsnorm(x, norm_mlp_w[i]), mlp_w_up[i], mlp_w_down[i])
    return x


_drawn_inputs = setup_inputs


def setup_inputs(seed=0):
    import zlib

    import numpy as np

    out = dict(_drawn_inputs(seed))
    spreads = {}
    factors = {'norm_mix_w': 2.782,
     'nsa_q_gain': 8.0,
     'nsa_k_gain': 8.0,
     'cmp_pe_k': 6.604,
     'ssd_conv_b': 3.935,
     'ssd_norm_w': 17.099,
     'norm_mlp_w': 3.017,
     'ssd_d': 8.0}
    for name, (base, spread) in spreads.items():
        noise = np.random.default_rng([zlib.crc32(name.encode()), seed]).standard_normal(out[name].shape)
        drawn = base * np.exp(spread * noise) if base else spread * noise
        out[name] = __import__('jax').numpy.asarray(drawn.astype(out[name].dtype))
    for name, factor in factors.items():
        out[name] = (out[name] * factor).astype(out[name].dtype)
    return out
```

```python
from contextlib import ExitStack

import concourse.bass as bass
import concourse.mybir as mybir
import numpy as np

F32 = mybir.dt.float32
F32R = mybir.dt.float32r
ACT = mybir.ActivationFunctionType
ALU = mybir.AluOpType
AX = mybir.AxisListType

P = 128
S = 256
D = 1024
TT = S // P
KD = D // P
H = 16
G = 4
DH = 64
QKV = 640
NCMP = 15
CB, CS = 32, 16
HID = 256
QC = 1024
GATE0 = QC + 6 * 256
NB = 3 * H
DI = 2048
SG = 8
SH = 32
XBC0 = DI
DT0 = DI + DI + 2 * SG * 128
MH = 4096
MJ = MH // 512
EPS = 1e-6
NEG = -1e30
TW = 384
BUCKETS = 32

PW = 2048
RAW = 4
HL = 4
PER = 16

N_KVC = 0
N_W1 = 2
N_ATT = 6
N_WO = N_ATT + 2 * G
N_MLP0 = N_WO + 4
N_SSD = N_MLP0 + 4 * MJ
N_MLP1 = N_SSD + 4 * SG
N_END = N_MLP1 + 4 * MJ

C_MIX, C_MLP, C_SSDN, C_CB, C_PE, C_QG, C_KG = 0, 16, 32, 48, 80, 112, 113
NPCOL = 114
PAR_W = NPCOL + 128 + 3 * P
W2_0, DW_0, GW_0, FLIP_0 = 0, 256, 512, 896


class At:

    def __init__(self, s, it=None, step=0):
        self.s, self.it, self.step = s, it, step

    def __add__(self, k):
        return At(self.s + k, self.it, self.step)

    def n(self, mult=1, add=0):
        if self.it is None:
            return self.s * mult + add
        return self.it * (self.step * mult) + (self.s * mult + add)


class Steps:

    def __init__(self, sem):
        self.sem, self.base, self.k = sem, At(0), 0

    def enter(self, base):
        self.base, self.k = base, 0

    def mark(self, ins):
        ins.then_inc(self.sem, 1)
        self.k += 1
        return self.k

    def wait(self, eng, k=None):
        eng.wait_ge(self.sem, self.base.n(1, self.k if k is None else k))


def raw_round(n):
    v = PER * (n.s // RAW + 1)
    return v if n.it is None else n.it * (PER * n.step // RAW) + v


def view(ap, off, dims):
    return bass.AP(ap.tensor, ap.offset + off, [list(ap.ap[0])] + dims)


def rows(t, off, dims):
    return bass.AP(t.tensor, off, dims)


def build(nc, a):
    ctx = ExitStack()
    with ctx:
        def sb(name, shape, dt=F32, stack=ctx):
            return stack.enter_context(nc.sbuf_tensor(name, shape, dt))

        def sem(name):
            return ctx.enter_context(nc.semaphore(name))

        bank = [ctx.enter_context(nc.psum_tensor(f"bank{i}", [P, 512], F32)) for i in range(8)]
        strip_dram = nc.dram_tensor("strip_dram", (H, 512), F32, kind="Internal").ap()
        acs_dram = nc.dram_tensor("acs_dram", (SH, S), F32, kind="Internal").ap()

        raw = sb("raw", [P, RAW, PW])
        whi = sb("whi", [P, HL, PW], F32R)
        wlo = sb("wlo", [P, HL, PW], F32R)
        x = sb("x", [P, TT, D])
        xn = sb("xn", [P, TT, D])
        xth = sb("xth", [P, KD, S], F32R)
        xtl = sb("xtl", [P, KD, S], F32R)
        hth = sb("hth", [P, 2, 4, S], F32R)
        htl = sb("htl", [P, 2, 4, S], F32R)
        rbuf = sb("rbuf", [P, 2, 512])
        par = sb("par", [P, PAR_W])
        ones = sb("ones", [P, P])
        pcol, ccol = par[:, 0:NPCOL], par[:, NPCOL:NPCOL + 128]
        ident, tri, segmask = (par[:, NPCOL + 128 + i * P:NPCOL + 128 + (i + 1) * P] for i in range(3))
        table = sb("table", [BUCKETS + 1, H])
        small = sb("small", [P, 80])
        mhalf = sb("mhalf", [P, 16])
        epst = sb("epst", [P, 2])
        gq = sb("gq", [P, 1])
        dwh = sb("dwh", [P, KD, SH], F32R)
        dwl = sb("dwl", [P, KD, SH], F32R)
        w2 = sb("w2", [P, 2, 2, DH])
        gate = sb("gate", [P, TT, NB])
        dtb = sb("dtb", [P, SH])
        alog = sb("alog", [P, SH])
        dskip = sb("dskip", [P, SH])

        ssq, vsum, rstd = small[:, 0:2], small[:, 2:4], small[:, 4:6]

        att = ExitStack()
        bias = sb("bias", [P, H, TW], F32, att)
        scratch = sb("scratch", [P, 2048], F32, att)
        qt, kt = rbuf[:, 0, :], rbuf[:, 1, :].rearrange("p (b n) -> p b n", b=2)
        pct = xn[:, 0, 0:S]
        tc = sb("tc", [P, TT, 4, 16], F32, att)
        pc = sb("pc", [P, TT, 4, 32], F32, att)
        cst = sb("cst", [P, 4, 8], F32, att)
        qst = sb("qst", [P, 4, 16], F32, att)
        hst = sb("hst", [P, 2, 8], F32, att)
        hidk = sb("hidk", [P, 2, G, 32], F32, att)
        vcmp = xn[:, 0, S:2 * S].rearrange("p (g d) -> p g d", g=G)
        kst = sb("kst", [32, 3, G], F32, att)
        kbd = sb("kbd", [P, G, 2, 16], F32, att)
        onehot, strip = scratch[0:BUCKETS + 1, 0:512], scratch[0:H, 512:1024]
        gw = scratch[:, 1024:1024 + KD * NB].rearrange("p (k n) -> p k n", k=KD)
        flip = scratch[:, 1408:1536]
        gx = view(tc[:, 0, 0, 0:1], 0, [[NB, TT], [1, NB]])
        dw = scratch[:, 1664:1664 + KD * SH].rearrange("p (k n) -> p k n", k=KD)
        kc = scratch[0:32, 0:2 * G * DH].rearrange("p (i g d) -> p i g d", i=2, g=G)
        kcn = scratch[0:32, 512:1024].rearrange("p (g b d) -> p g b d", g=G, b=2)
        hidv = scratch[:, 1024:2048].rearrange("p (m g n) -> p m g n", m=2, g=G)
        gates = ExitStack()
        gwh = sb("gwh", [P, KD, NB], F32R, gates)
        gwl = sb("gwl", [P, KD, NB], F32R, gates)
        gates.close()
        qkv = sb("qkv", [P, 2, TT, QKV], F32, att)
        pt = sb("pt", [P, 2, 2, TW], F32, att)
        att.close()

        xb = sb("xb", [P, 4, 3 + S])
        cacc = sb("cacc", [P, 4, S])
        xc = sb("xc", [P, 2, 4, S])
        sz = sb("sz", [P, 512])
        xsn = sb("xsn", [P, TT, S])
        bn = sb("bn", [P, P])
        eb = sb("eb", [P, TT, 4, P])
        acb = sb("acb", [P, 2, 4, TT, P])
        xw = sb("xw", [P, S])
        sk = sb("sk", [P, TT, S])
        prev = sb("prev", [P, S])
        y = sb("y", [P, TT, S])
        sst = sb("sst", [P, 6])
        yth = sb("yth", [P, 2, S], F32R)
        ytl = sb("ytl", [P, 2, S], F32R)
        dt = sb("dt", [P, TT, SH])
        dta = sb("dta", [P, TT, SH])
        dtt = sb("dtt", [P, 4, TT, SH])
        acs = sb("acs", [P, TT, SH])
        nacs = sb("nacs", [P, TT, SH])
        eacs = sb("eacs", [P, SH])
        wend = sb("wend", [P, SH])
        ealog = sb("ealog", [P, SH])
        acst = sb("acst", [SH, S])
        probs = scratch[:, 1024:2048].rearrange("p (b n) -> p b n", b=2)
        tsc = scratch[:, 0:1024].rearrange("p (b n) -> p b n", b=2)
        blk = view(scratch[:, 0:1], 0, [[60, 16], [1, 60]])
        blkh = view(hth[:, 0, 0, 0:1], 0, [[960, 2], [60, 16], [1, 60]])
        blkl = view(htl[:, 0, 0, 0:1], 0, [[960, 2], [60, 16], [1, 60]])
        oth = hth[:, :, :, :].rearrange("p a b n -> p (a b) n")
        otl = htl[:, :, :, :].rearrange("p a b n -> p (a b) n")

        def in_order(p):
            return view(bank[7][:, p * S + P - 1:p * S + P], 0, [[P, 2], [-1, P]])

        piece_in = [sem(f"piece_in{i}") for i in range(RAW)]
        high_ready, low_ready, piece_used = sem("high_ready"), sem("low_ready"), sem("piece_used")
        x_in, params_in, rows_in, w_small_in = sem("x_in"), sem("params_in"), sem("rows_in"), sem("w_small_in")
        strip_in, bias_in, out_done = sem("strip_in"), sem("bias_in"), sem("out_done")
        acs_out, acs_in = sem("acs_out"), [sem("acs_in0"), sem("acs_in1")]
        strip_ps, strip_ready = sem("strip_ps"), sem("strip_ready")
        pool_set, gq_ready, small_hi, small_lo = sem("pool_set"), sem("gq_ready"), sem("small_hi"), sem("small_lo")
        sumsq_ready, rstd_ready, xn_ready = sem("sumsq_ready"), sem("rstd_ready"), sem("xn_ready")
        xt_ps, xt_hi, xt_lo, x_ready = sem("xt_ps"), sem("xt_hi"), sem("xt_lo"), sem("x_ready")
        y_ps = sem("y_ps")
        relu_ready, sq_ready, hid_hi, hid_lo = sem("relu_ready"), sem("sq_ready"), sem("hid_hi"), sem("hid_lo")
        gate_ps, gate_exp, gate_ready, gate_flip = sem("gate_ps"), sem("gate_exp"), sem("gate_ready"), sem("gate_flip")
        kvc_ready, kvt_ps, blk_ready, blk_hi, blk_lo = sem("kvc_ready"), sem("kvt_ps"), sem("blk_ready"), sem("blk_hi"), sem("blk_lo")
        hid_ready, cmp_ps, vcmp_ready = sem("hid_ready"), sem("cmp_ps"), sem("vcmp_ready")
        kc_sq, kc_rstd, kcn_ready, kct_ps, kbd_ready = sem("kc_sq"), sem("kc_rstd"), sem("kcn_ready"), sem("kct_ps"), sem("kbd_ready")
        qkv_sq, qkv_ssq, qkv_rstd, qkv_ready = sem("qkv_sq"), sem("qkv_ssq"), sem("qkv_rstd"), sem("qkv_ready")
        qkt_ps, qt_ready, kt_ready = sem("qkt_ps"), sem("qt_ready"), sem("kt_ready")
        sc_ps, sm_max, sm_exp, p_ready = sem("sc_ps"), sem("sm_max"), sem("sm_exp"), sem("p_ready")
        pt_ps, pt_sel, pt_win = sem("pt_ps"), sem("pt_sel"), sem("pt_win")
        csc_ps, csc_ready, csc_exp, pc_ready, pct_ps, pct_ready = (
            sem("csc_ps"), sem("csc_ready"), sem("csc_exp"), sem("pc_ready"), sem("pct_ps"), sem("pct_ready"))
        pv_done, ot_hi, ot_lo = sem("pv_done"), sem("ot_hi"), sem("ot_lo")
        dve_step, act_step, pool_step = sem("dve_step"), sem("act_step"), sem("pool_step")
        dt_ps, dt_neg, dt_exp, dt_one, dt_ln, dt_ready = (
            sem("dt_ps"), sem("dt_neg"), sem("dt_exp"), sem("dt_one"), sem("dt_ln"), sem("dt_ready"))
        acs_ps, acs_ready, acst_ps, acst_ready, decay_ready, wend_ready = (
            sem("acs_ps"), sem("acs_ready"), sem("acst_ps"), sem("acst_ready"), sem("decay_ready"), sem("wend_ready"))
        masked, e_ready, m_ready = sem("masked"), sem("e_ready"), sem("m_ready")
        conv_in, conv_done, xc_ready, z_ready = sem("conv_in"), sem("conv_done"), sem("xc_ready"), sem("z_ready")
        t_ps, bn_ready, xsn_ready, xw_ready, sk_ready = sem("t_ps"), sem("bn_ready"), sem("xsn_ready"), sem("xw_ready"), sem("sk_ready")
        s_ps, prev_ready, ys_ps, y_ready, ysq_ready, yrstd_ready = (
            sem("s_ps"), sem("prev_ready"), sem("ys_ps"), sem("y_ready"), sem("ysq_ready"), sem("yrstd_ready"))
        yn_ready, yt_ps, yt_hi, yt_lo = sem("yn_ready"), sem("yt_ps"), sem("yt_hi"), sem("yt_lo")

        block = ctx.enter_context(nc.Block())

        @block.sync
        def _(sp):
            def piece(n):
                if n.s >= RAW:
                    sp.wait_ge(low_ready, n.n(1, 1 - RAW))
                src = a["stream"][bass.ds(n.n(), 1), :, :].rearrange("a p n -> (a p) n")
                sp.dma_start(raw[:, n.s % RAW, :], src).then_inc(piece_in[n.s % RAW], PER)

            for c in range(TT):
                sp.dma_start(x[:, c, :], a["x"][0, c * P:(c + 1) * P, :]).then_inc(x_in, 16)
            sp.dma_start(par[:, :], a["params"]).then_inc(params_in, 16)
            first = RAW + (N_END - RAW) % 4
            for i in range(first):
                piece(At(i))
            with sp.Fori(0, (N_END - first) // 4) as it:
                for u in range(4):
                    piece(At(first + u, it, 4))
            for c in range(TT):
                sp.wait_ge(x_ready, 12 + 2 * (c + 1))
                sp.dma_start(a["out"][0, c * P:(c + 1) * P, :], x[:, c, :]).then_inc(out_done, 16)
            sp.wait_ge(out_done, 16 * TT)

        @block.scalar
        def _(act):
            step = Steps(act_step)
            copy = ACT.Copy

            def load(dst, src, s):
                act.dma_start(dst, src).then_inc(s, 16)

            def split(n):
                act.wait_ge(piece_in[n.s % RAW], raw_round(n))
                if n.s >= HL:
                    act.wait_ge(piece_used, n.n(1, 1 - HL))
                nc.scalar.activation(whi[:, n.s % HL, :], raw[:, n.s % RAW, :], copy).then_inc(high_ready, 1)

            load(table[0:BUCKETS, :], a["rel_table"], rows_in)
            load(onehot, a["onehot"], rows_in)

            def sumsq(q):
                for c in range(TT):
                    act.wait_ge(*((x_in, 16 * TT) if q == 0 else (x_ready, 4 * (q - 1) + 2 * (c + 1))))
                    if q:
                        act.wait_ge(xt_ps, 4 * q)
                    nc.scalar.activation(xn[:, c, :], x[:, c, :], ACT.Square,
                                         accum_out=small[:, c:c + 1]).then_inc(sumsq_ready, 1)

            def norm_t(q):
                for b in range(4):
                    act.wait_ge(xt_ps, 4 * q + b + 1)
                    for k in (2 * b, 2 * b + 1):
                        col = (q // 2) * 8 + (q % 2) * 16 + k
                        nc.scalar.activation(xth[:, k, :], bank[4 + b][:, (k % 2) * S:(k % 2 + 1) * S], copy,
                                             scale=pcol[:, col:col + 1]).then_inc(xt_hi, 1)

            sumsq(0)
            load(scratch[:, 1024:1024 + KD * NB], a["small_w"][:, GW_0:GW_0 + KD * NB], w_small_in)
            load(scratch[:, 1664:1664 + KD * SH], a["small_w"][:, DW_0:DW_0 + KD * SH], w_small_in)
            load(w2[:, :, :, :].rearrange("p i m d -> p (i m d)"), a["small_w"][:, W2_0:W2_0 + 256], w_small_in)
            load(flip, a["small_w"][:, FLIP_0:FLIP_0 + P], w_small_in)
            for t, name in ((dtb, "ssd_dt_bias"), (alog, "ssd_a_log"), (dskip, "ssd_d")):
                load(t[:, :], rows(a[name], 0, [[0, P], [1, SH]]), w_small_in)
            act.wait_ge(strip_ps, 1)
            nc.scalar.activation(strip, bank[2][0:H, :], copy).then_inc(strip_ready, 1)
            act.wait_ge(strip_ready, 1)
            act.dma_start(strip_dram, strip).then_inc(strip_in, 16)
            act.wait_ge(strip_in, 16)
            act.dma_start(bias[:, :, :], rows(strip_dram, 0, [[1, P], [512, H], [1, TW]])).then_inc(bias_in, 16)
            act.wait_ge(params_in, 16)
            nc.scalar.activation(gq[:, :], pcol[:, C_QG:C_QG + 1], copy, scale=float(DH) ** -0.5).then_inc(gq_ready, 1)
            act.wait_ge(w_small_in, 16 * 7)
            nc.scalar.activation(gwh[:, :, :], gw[:, :, :], copy).then_inc(small_hi, 1)
            nc.scalar.activation(dwh[:, :, :], dw[:, :, :], copy).then_inc(small_hi, 1)
            norm_t(0)
            for i in range(4):
                split(At(i))
            for c in range(TT):
                act.wait_ge(piece_used, 2)
                nc.scalar.activation(view(xn[:, c, 0:1], 0, [[128, 8], [64, 2], [1, DH]]),
                                     view(bank[4 + c][:, 0:1], 0, [[64, 8], [0, 2], [1, DH]]), copy).then_inc(kvc_ready, 1)
            act.wait_ge(gate_ps, 1)
            for c in range(TT):
                nc.scalar.activation(view(gx, c * NB, [[1, NB]]), bank[6][:, c * 64:c * 64 + NB], ACT.Exp, scale=-1.0).then_inc(gate_exp, 1)
            split(At(4))
            split(At(5))
            for kv in range(2):
                act.wait_ge(blk_ready, 8 * (kv + 1))
                nc.scalar.activation(blkh[:, kv, :, :], blk, copy).then_inc(blk_hi, 1)
            for kv in range(2):
                act.wait_ge(piece_used, N_W1 + 2 * kv + 2)
                act.wait_ge(pool_set, 8)
                for m in range(2):
                    src = bank[4 + 2 * kv + m][:, 0:1]
                    if kv == 0:
                        dst, src = hidk[:, m, :, 0:NCMP], view(src, 0, [[NCMP, G], [1, NCMP]])
                    else:
                        dst = view(hidv[:, m, 0, 0:1], 0, [[P, G], [32, 4], [1, NCMP]])
                        src = view(src, 0, [[NCMP, G], [0, 4], [1, NCMP]])
                    nc.scalar.activation(dst, src, ACT.Silu).then_inc(hid_ready, 1)
                split(At(N_ATT + 2 * kv))
                split(At(N_ATT + 2 * kv + 1))
            act.wait_ge(cmp_ps, 2)
            nc.scalar.activation(vcmp, bank[1][:, 0:256].rearrange("p (g d) -> p g d", g=G), copy).then_inc(vcmp_ready, 1)

            def qkv_squares(g):
                for c in range(TT):
                    act.wait_ge(piece_used, N_ATT + 2 * g + 2)
                    if g:
                        act.wait_ge(qkv_ssq, g)
                    nc.scalar.activation(xn[:, 1, c * 512:(c + 1) * 512], bank[4 + c][:, :], ACT.Square).then_inc(qkv_sq, 1)

            def selected_t(g, h):
                m = 4 * g + h
                act.wait_ge(pt_ps, 2 * m + 2)
                if m >= 2:
                    act.wait_ge(pv_done, m - 1)
                nc.scalar.activation(pt[:, m % 2, 0, :], bank[2][:, 0:TW], copy).then_inc(pt_sel, 1)

            def out_high(g, p):
                act.wait_ge(pv_done, 4 * g + 2 * p + 2)
                nc.scalar.activation(view(oth[:, 2 * g + p, 0:1], 0, [[P, 2], [1, P]]), in_order(p), copy).then_inc(ot_hi, 1)

            qkv_squares(0)
            for g in range(G):
                act.wait_ge(qkt_ps, 2 * g + 1)
                nc.scalar.activation(view(qt, 0, [[P, 4], [1, P]]), view(bank[6][:, P - 1:P], 0, [[P, 4], [-1, P]]), copy,
                                     scale=gq[:, 0:1]).then_inc(qt_ready, 1)
                for i in range(8):
                    t = i % 2
                    nk = P * (t + 1)
                    n = 8 * g + i
                    act.wait_ge(sm_max, 2 * n + 2)
                    if n >= 2:
                        act.wait_ge(pt_ps, n - 1)
                    for b in range(2):
                        nc.scalar.activation(probs[:, t, b * S:b * S + nk], tsc[:, t, b * S:b * S + nk], ACT.Exp,
                                             bias=hst[:, t, b:b + 1], scale=-1.0,
                                             accum_out=hst[:, t, 2 + b:3 + b]).then_inc(sm_exp, 1)
                    if i == 0:
                        act.wait_ge(csc_ready, g + 1)
                        nc.scalar.activation(tc[:, :, :, 0:NCMP], tc[:, :, :, 0:NCMP], ACT.Exp).then_inc(csc_exp, 1)
                    if i == 2:
                        act.wait_ge(pct_ps, g + 1)
                        if g:
                            act.wait_ge(pv_done, 4 * g)
                        nc.scalar.activation(pct, bank[6][:, 256:512], copy).then_inc(pct_ready, 1)
                    if i in (2, 4, 6):
                        selected_t(g, i // 2 - 1)
                    if i == 5:
                        out_high(g, 0)
                        if g < G - 1:
                            qkv_squares(g + 1)
                    if i >= 6:
                        split(At(N_ATT + 2 * (g + 2) + i - 6))
                selected_t(g, 3)
                out_high(g, 1)

            def mlp(layer, base):
                def relu(j, n, half):
                    act.wait_ge(piece_used, n.n(1, 1))
                    if layer or j.s:
                        act.wait_ge(hid_lo, j.n(2, 2 * MJ * layer + half - 1))
                    nc.scalar.activation(rbuf[:, half, :], bank[4 + 2 * (j.s % 2) + half][:, :], ACT.Relu).then_inc(relu_ready, 1)

                def high(j, half):
                    act.wait_ge(sq_ready, j.n(2, 2 * MJ * layer + half + 1))
                    nc.scalar.activation(hth[:, j.s % 2, 2 * half:2 * half + 2, :],
                                         rbuf[:, half, :].rearrange("p (m n) -> p m n", m=2), copy).then_inc(hid_hi, 1)

                def body(j, n):
                    split(n + 2)
                    relu(j + 1, n, 0)
                    split(n + 3)
                    high(j + 1, 0)
                    relu(j + 1, n + 1, 1)
                    split(n + 4)
                    high(j + 1, 1)
                    split(n + 5)
                relu(At(0), At(base), 0)
                split(At(base + 2))
                high(At(0), 0)
                relu(At(0), At(base + 1), 1)
                split(At(base + 3))
                high(At(0), 1)
                body(At(0), At(base + 2))
                with act.Fori(0, (MJ - 2) // 2) as it:
                    for u in range(2):
                        body(At(1 + u, it, 2), At(base + 6 + 4 * u, it, 8))
                if layer == 0:
                    split(At(base + 4 * MJ))
                    split(At(base + 4 * MJ + 1))

            for i in range(2):
                split(At(N_MLP0 + i))
            sumsq(1)
            norm_t(1)
            mlp(0, N_MLP0)

            sumsq(2)
            norm_t(2)
            split(At(N_SSD + 2))
            act.wait_ge(dt_neg, 1)
            nc.scalar.activation(dtt[:, 1, :, :], dtt[:, 0, :, :], ACT.Exp).then_inc(dt_exp, 1)
            nc.scalar.activation(ealog[:, :], alog[:, :], ACT.Exp).then_inc(dt_exp, 1)
            act.wait_ge(dt_one, 1)
            nc.scalar.activation(dtt[:, 3, :, :], dtt[:, 2, :, :], ACT.Ln).then_inc(dt_ln, 1)
            act.wait_ge(acst_ps, 1)
            nc.scalar.activation(acst[:, :], bank[7][0:SH, 0:S], copy).then_inc(acst_ready, 1)
            act.wait_ge(acs_ready, 2)
            nc.scalar.activation(eacs[:, :], acs[:, 1, :], ACT.Exp).then_inc(decay_ready, 1)
            nc.scalar.activation(wend[:, :], dtt[:, 0, 0, :], ACT.Exp).then_inc(decay_ready, 1)

            def conv_load(g, n, i):
                act.wait_ge(piece_used, n.n(1, 1))
                if g.s:
                    act.wait_ge(conv_done, g.n(2, i - 1))
                nc.scalar.activation(xb[:, 2 * i:2 * i + 2, 3:3 + S],
                                     bank[4 + i][:, :].rearrange("p (q n) -> p q n", q=2), copy).then_inc(conv_in, 1)

            def silus(g, n):
                for i in range(2):
                    act.wait_ge(conv_done, g.n(2, i + 1))
                    if g.s >= 2:
                        act.wait_ge(ys_ps, g.n(1, -1))
                    nc.scalar.activation(xc[:, g.s % 2, 2 * i:2 * i + 2, :], cacc[:, 2 * i:2 * i + 2, :], ACT.Silu).then_inc(xc_ready, 1)
                act.wait_ge(piece_used, n.n(1, 3))
                if g.s:
                    act.wait_ge(y_ready, g.n())
                nc.scalar.activation(sz[:, :], bank[6][:, :], ACT.Silu).then_inc(z_ready, 1)

            conv_load(At(0), At(N_SSD), 0)
            conv_load(At(0), At(N_SSD + 1), 1)
            split(At(N_SSD + 3))
            silus(At(0), At(N_SSD))

            def ssd(g, n, last=False):
                for i in range(8):
                    c, h = i // 4, i % 4
                    act.wait_ge(masked, g.n(1, 1))
                    if g.s:
                        act.wait_ge(ys_ps, g.n())
                    nc.scalar.activation(eb[:, c, h, :], acb[:, g.s % 2, h, c, :], ACT.Exp,
                                         bias=nacs[:, c, bass.ds(g.n(4, h), 1)]).then_inc(e_ready, 1)
                act.wait_ge(t_ps, g.n(2, 2))
                nc.scalar.activation(bn[:, :], bank[6][:, 256:384], copy).then_inc(bn_ready, 1)
                if not last:
                    split(n + 1)
                    split(n + 2)
                    conv_load(g + 1, n, 0)
                act.wait_ge(s_ps, g.n(1, 1))
                nc.scalar.activation(prev[:, :], bank[7][:, 0:S], copy).then_inc(prev_ready, 1)
                for c in range(TT):
                    act.wait_ge(y_ready, g.n(1, 1))
                    nc.scalar.activation(sk[:, c, :], y[:, c, :], ACT.Square, accum_out=sst[:, c:c + 1]).then_inc(ysq_ready, 1)
                if not last:
                    conv_load(g + 1, n + 1, 1)
                    split(n + 3)
                    silus(g + 1, n)
                    split(n + 4)
                for q in range(2):
                    act.wait_ge(yt_ps, g.n(1, 1))
                    if g.s:
                        if last:
                            act.wait_ge(piece_used, N_MLP1 - 1)
                        else:
                            act.wait_ge(piece_used, n.n())
                    nc.scalar.activation(yth[:, q, :], bank[7][:, q * S:(q + 1) * S], copy,
                                         scale=pcol[:, bass.ds(g.n(2, C_SSDN + q), 1)]).then_inc(yt_hi, 1)
            ssd(At(0), At(N_SSD + 3))
            with act.Fori(0, (SG - 2) // 2) as it:
                for u in range(2):
                    ssd(At(1 + u, it, 2), At(N_SSD + 7 + 4 * u, it, 8))
            split(At(N_MLP1))
            split(At(N_MLP1 + 1))
            ssd(At(SG - 1), None, last=True)

            sumsq(3)
            norm_t(3)
            mlp(1, N_MLP1)


        @block.gpsimd
        def _(pool):
            step = Steps(pool_step)
            pool.memset(table[BUCKETS:BUCKETS + 1, :], NEG).then_inc(pool_set, 1)
            pool.wait_ge(pool_set, 1)
            pool.memset(mhalf[:, :], -0.5).then_inc(pool_set, 1)
            pool.memset(epst[:, :], 256 * EPS).then_inc(pool_set, 1)
            pool.memset(ones[:, :], 1.0).then_inc(pool_set, 1)
            pool.memset(hidk[:, :, :, :], 0.0).then_inc(pool_set, 1)
            pool.memset(pc[:, :, :, :], 0.0).then_inc(pool_set, 1)
            pool.memset(kbd[:, :, :, :], 0.0).then_inc(pool_set, 1)
            def rsqrt(dst, tmp, src, width, n, done, part=P):
                step.mark(nc.gpsimd.tensor_scalar(tmp, src, width * EPS, None, ALU.add))
                step.wait(pool)
                return nc.gpsimd.tensor_tensor(dst, tmp, mhalf[0:part, 0:n], ALU.pow).then_inc(done, 1)

            def norm_stat(q):
                pool.wait_ge(sumsq_ready, 2 * (q + 1))
                rsqrt(rstd, vsum, ssq, D, 2, rstd_ready)

            pool.wait_ge(pool_set, 7)
            norm_stat(0)
            pool.wait_ge(gate_flip, 1)
            pool.memset(hidv, 0.0).then_inc(pool_set, 1)
            pool.wait_ge(pool_set, 8)

            pool.wait_ge(kc_sq, 1)
            rsqrt(kst[:, 2, :], kst[:, 1, :], kst[:, 0, :], DH, G, kc_rstd, 32)
            for g in range(G):
                pool.wait_ge(qkv_ssq, g + 1)
                if g:
                    pool.wait_ge(qkv_ready, 8 * g)
                step.mark(nc.gpsimd.tensor_scalar(qst[:, 1, :], qst[:, 0, :], DH * EPS, None, ALU.add))
                step.wait(pool)
                step.mark(nc.gpsimd.tensor_tensor(qst[:, 2, :], qst[:, 1, :], mhalf[:, :], ALU.pow))
                step.wait(pool)
                pool.memset(view(qst[:, 2, 5:6], 0, [[8, 2], [2, 2]]), DH ** -0.5).then_inc(qkv_rstd, 1)
            norm_stat(1)
            norm_stat(2)

            pool.wait_ge(acst_ready, 1)
            pool.dma_start(acs_dram, acst[:, :]).then_inc(acs_out, 16)
            pool.wait_ge(acs_out, 16)

            def load_decay(g):
                src = acs_dram[bass.ds(g.n(4), 4), :]
                src = bass.AP(src.tensor, src.offset, [[0, P], [1, 4 * S]])
                pool.dma_start(acb[:, g.s % 2, :, :, :].rearrange("p h c l -> p (h c l)"), src).then_inc(acs_in[g.s % 2], 16)

            def mask(g):
                pool.wait_ge(acs_in[g.s % 2], 16 * (g.s // 2 + 1) if g.it is None else g.it * 16 + 16 * (g.s // 2 + 1))
                v = acb[:, g.s % 2, :, :, :].rearrange("p h c l -> p (h c) l")
                nc.gpsimd.tensor_tensor(v, v, view(segmask[:, 0:1], 0, [[0, 8], [1, P]]), ALU.add).then_inc(masked, 1)

            def heads(t, g, dims):
                return view(t[:, bass.ds(g.n(4), 4)], 0, dims)

            def ssd(g, last=False):
                if not last:
                    if g.s:
                        pool.wait_ge(e_ready, g.n(8))
                    load_decay(g + 1)
                pool.wait_ge(xsn_ready, g.n(1, 1))
                if g.s:
                    pool.wait_ge(s_ps, g.n())
                nc.gpsimd.tensor_tensor(xw[:, :].rearrange("p (h d) -> p h d", h=4),
                                        xsn[:, 0, :].rearrange("p (h d) -> p h d", h=4),
                                        heads(wend, g, [[1, 4], [0, DH]]), ALU.mult).then_inc(xw_ready, 1)
                if g.s:
                    pool.wait_ge(ysq_ready, g.n(2))
                for c in range(TT):
                    nc.gpsimd.tensor_tensor(sk[:, c, :].rearrange("p (h d) -> p h d", h=4),
                                            xsn[:, c, :].rearrange("p (h d) -> p h d", h=4),
                                            heads(dskip, g, [[1, 4], [0, DH]]), ALU.mult).then_inc(sk_ready, 1)
                if not last:
                    mask(g + 1)
                pool.wait_ge(ysq_ready, g.n(2, 2))
                step.mark(nc.gpsimd.tensor_tensor(sst[:, 2:4], sst[:, 0:2], epst[:, :], ALU.add))
                step.wait(pool)
                nc.gpsimd.tensor_tensor(sst[:, 4:6], sst[:, 2:4], mhalf[:, 0:2], ALU.pow).then_inc(yrstd_ready, 1)

            pool.wait_ge(wend_ready, 1)
            load_decay(At(0))
            mask(At(0))
            before = step.base.s + step.k
            step.enter(At(before))
            ssd(At(0))
            with pool.Fori(0, (SG - 2) // 2) as it:
                for u in range(2):
                    step.enter(At(before + 1 + u, it, 2))
                    ssd(At(1 + u, it, 2))
            step.enter(At(before + SG - 1))
            ssd(At(SG - 1), last=True)
            norm_stat(3)

        @block.vector
        def _(dve):
            step = Steps(dve_step)
            V = nc.vector

            def low(n):
                dve.wait_ge(high_ready, n.n(1, 1))
                V.tensor_tensor(wlo[:, n.s % HL, :], raw[:, n.s % RAW, :], whi[:, n.s % HL, :].bitcast(F32),
                                ALU.subtract).then_inc(low_ready, 1)

            def norm(q):
                dve.wait_ge(rstd_ready, q + 1)
                for c in range(TT):
                    V.tensor_scalar(xn[:, c, :], x[:, c, :], small[:, 4 + c:5 + c], float(D) ** 0.5,
                                    ALU.mult, ALU.mult).then_inc(xn_ready, 1)
                for b in range(4):
                    dve.wait_ge(xt_hi, 8 * q + 2 * b + 2)
                    for k in (2 * b, 2 * b + 1):
                        col = (q // 2) * 8 + (q % 2) * 16 + k
                        V.scalar_tensor_tensor(xtl[:, k, :], bank[4 + b][:, (k % 2) * S:(k % 2 + 1) * S],
                                               pcol[:, col:col + 1], xth[:, k, :].bitcast(F32),
                                               ALU.mult, ALU.subtract).then_inc(xt_lo, 1)

            def residual(r, last_piece):
                for c in range(TT):
                    for nh in range(2):
                        i = 2 * c + nh
                        dve.wait_ge(*((piece_used, last_piece + 1) if i == 3 else (y_ps, 3 * r + i + 1)))
                        V.tensor_tensor(x[:, c, nh * 512:(nh + 1) * 512], x[:, c, nh * 512:(nh + 1) * 512],
                                        bank[i][:, :], ALU.add).then_inc(x_ready, 1)

            dve.wait_ge(params_in, 16)
            norm(0)
            for i, (h, l, t) in enumerate(((gwh, gwl, gw), (dwh, dwl, dw))):
                dve.wait_ge(small_hi, i + 1)
                V.tensor_tensor(l[:, :, :], t[:, :, :], h[:, :, :].bitcast(F32), ALU.subtract).then_inc(small_lo, 1)
            for i in range(4):
                low(At(i))
            dve.wait_ge(gate_exp, 2)
            step.mark(V.tensor_scalar_add(gx, gx, 1.0))
            step.wait(dve)
            V.reciprocal(gx, gx).then_inc(gate_ready, 1)
            dve.wait_ge(gate_flip, 1)
            V.tensor_copy(gate[:, :, :], view(bank[7][:, 0:1], 0, [[64, 2], [1, NB]])).then_inc(gate_ready, 1)
            low(At(4))
            low(At(5))
            for kv in range(2):
                dve.wait_ge(kvt_ps, 2 * kv + 2)
                if kv:
                    dve.wait_ge(blk_hi, 1)
                    dve.wait_ge(blk_lo, 1)
                for g in range(G):
                    for b in range(2):
                        part = slice(b * DH, (b + 1) * DH)
                        i = 4 * kv + g
                        src = view(bank[i // 2][part, 0:1], (i % 2) * S + b, [[2, 16], [CS, NCMP]])
                        dst = view(scratch[part, 0:1], g * NCMP, [[60, 16], [1, NCMP]])
                        pe = view(par[part, C_PE + 16 * kv:C_PE + 1 + 16 * kv], 0, [[1, 16], [0, NCMP]])
                        V.tensor_tensor(dst, src, pe, ALU.add).then_inc(blk_ready, 1)
                dve.wait_ge(blk_hi, kv + 1)
                V.tensor_tensor(blkl[:, kv, :, :], blk, blkh[:, kv, :, :].bitcast(F32), ALU.subtract).then_inc(blk_lo, 1)
            for i in range(4):
                low(At(N_ATT + i))
            dve.wait_ge(cmp_ps, 1)
            step.mark(V.tensor_copy(kc[:, 0, :, :], bank[0][0:32, 0:256].rearrange("p (g d) -> p g d", g=G)))
            step.wait(dve)
            step.mark(V.tensor_tensor(kc[:, 1, :, :], kc[:, 0, :, :], kc[:, 0, :, :], ALU.mult))
            step.wait(dve)
            V.tensor_reduce(kst[:, 0, :], kc[:, 1, :, :], AX.X, ALU.add).then_inc(kc_sq, 1)
            dve.wait_ge(kc_rstd, 1)
            for b in range(2):
                V.scalar_tensor_tensor(kcn[:, :, b, :], kc[:, 0, :, :], float(DH) ** 0.5,
                                       view(kst[:, 2, 0:1], 0, [[1, G], [0, DH]]), ALU.mult, ALU.mult).then_inc(kcn_ready, 1)
            dve.wait_ge(kct_ps, 1)
            dve.wait_ge(pool_set, 7)
            for b in range(2):
                part = slice(b * DH, (b + 1) * DH)
                V.tensor_scalar(kbd[part, :, b, 0:NCMP], view(bank[2][part, 0:1], 0, [[32, G], [1, NCMP]]),
                                par[part, C_KG:C_KG + 1], None, ALU.mult).then_inc(kbd_ready, 1)

            def qkv_sums(g):
                dve.wait_ge(qkv_sq, 2 * g + 2)
                if g:
                    dve.wait_ge(qkv_rstd, g)
                V.tensor_reduce(qst[:, 0, :], xn[:, 1, :].rearrange("p (n d) -> p n d", d=DH), AX.X, ALU.add).then_inc(qkv_ssq, 1)

            def qkv_norm(g):
                dve.wait_ge(qkv_rstd, g + 1)
                if g >= 2:
                    dve.wait_ge(pv_done, 4 * (g - 1))
                for to, of, st in (([0, DH, 4], [0, DH], [0, 1]), ([256, 192, 2], [256, 128], [4, 2]),
                                   ([320, 192, 2], [256, 128], [4, 2]), ([384, 192, 2], [320, 128], [5, 2])):
                    for c in range(TT):
                        V.scalar_tensor_tensor(view(qkv[:, g % 2, c, 0:1], to[0], [[to[1], to[2]], [1, DH]]),
                                               view(bank[4 + c][:, 0:1], of[0], [[of[1], to[2]], [1, DH]]), float(DH) ** 0.5,
                                               view(qst[:, 2, 8 * c:8 * c + 1], st[0], [[st[1], to[2]], [0, DH]]),
                                               ALU.mult, ALU.mult).then_inc(qkv_ready, 1)

            def score_max(g, i):
                h, t, n = i // 2, i % 2, 8 * g + i
                nk = P * (t + 1)
                dve.wait_ge(sc_ps, n + 1)
                if n >= 2:
                    dve.wait_ge(sm_exp, 2 * n - 2)
                for b in range(2):
                    V.tensor_tensor_reduce(out=tsc[:, t, b * S:b * S + nk], in0=bank[t][:, b * nk:(b + 1) * nk],
                                           in1=bias[:, 4 * g + h, P * (1 - t):P * (1 - t) + nk], scale=-1.0,
                                           scalar=3e38, op0=ALU.add, op1=ALU.min,
                                           accum_out=hst[:, t, b:b + 1]).then_inc(sm_max, 1)

            def score_scale(g, i):
                h, t, n = i // 2, i % 2, 8 * g + i
                nk = P * (t + 1)
                dve.wait_ge(sm_exp, 2 * n + 2)
                step.mark(V.reciprocal(hst[:, t, 4:6], hst[:, t, 2:4]))
                step.wait(dve)
                for b in range(2):
                    col = (1 + b) * H + 4 * g + h
                    V.tensor_scalar(probs[:, t, b * S:b * S + nk], probs[:, t, b * S:b * S + nk],
                                    hst[:, t, 4 + b:5 + b], gate[:, 1 - t, col:col + 1],
                                    ALU.mult, ALU.mult).then_inc(p_ready, 1)

            def window_t(g, h):
                m = 4 * g + h
                dve.wait_ge(pt_ps, 2 * m + 2)
                if m >= 2:
                    dve.wait_ge(pv_done, m - 1)
                V.tensor_copy(pt[:, m % 2, 1, :], bank[3][:, 0:TW]).then_inc(pt_win, 1)

            def out_low(g, p):
                dve.wait_ge(ot_hi, 2 * g + p + 1)
                V.tensor_tensor(view(otl[:, 2 * g + p, 0:1], 0, [[P, 2], [1, P]]), in_order(p),
                                view(oth[:, 2 * g + p, 0:1].bitcast(F32), 0, [[P, 2], [1, P]]), ALU.subtract).then_inc(ot_lo, 1)

            tcv = tc[:, :, :, 0:NCMP]

            def over_heads(i):
                return view(cst[:, i, 0:1], 0, [[4, 2], [1, 4], [0, NCMP]])

            def cmp_max(g):
                dve.wait_ge(csc_ps, g + 1)
                src = view(bank[6][:, 0:1], 0, [[64, 2], [16, 4], [1, NCMP]])
                bs = view(bias[:, 4 * g, 0:1], CB - 1, [[P, 2], [TW, 4], [CS, NCMP]])
                step.mark(V.tensor_tensor(tcv, src, bs, ALU.add))
                step.wait(dve)
                step.mark(V.tensor_reduce(cst[:, 0, :], tcv, AX.X, ALU.max))
                step.wait(dve)
                step.mark(V.tensor_scalar_max(cst[:, 1, :], cst[:, 0, :], -1e20))
                step.wait(dve)
                V.tensor_tensor(tcv, tcv, over_heads(1), ALU.subtract).then_inc(csc_ready, 1)

            def cmp_scale(g):
                dve.wait_ge(csc_exp, g + 1)
                step.mark(V.tensor_reduce(cst[:, 0, :], tcv, AX.X, ALU.add))
                step.wait(dve)
                step.mark(V.tensor_scalar_max(cst[:, 2, :], cst[:, 0, :], 1e-30))
                step.wait(dve)
                step.mark(V.reciprocal(cst[:, 3, :], cst[:, 2, :]))
                step.wait(dve)
                step.mark(V.tensor_tensor(view(cst[:, 2, 0:1], 0, [[4, 2], [1, 4]]), view(cst[:, 3, 0:1], 0, [[4, 2], [1, 4]]),
                                          gate[:, :, 4 * g:4 * g + 4], ALU.mult))
                step.wait(dve)
                if g:
                    dve.wait_ge(pct_ps, g)
                V.tensor_tensor(pc[:, :, :, 0:NCMP], tcv, over_heads(2), ALU.mult).then_inc(pc_ready, 1)

            dve.wait_ge(gate_ready, 2)
            dve.wait_ge(bias_in, 16)
            qkv_sums(0)
            qkv_norm(0)
            for g in range(G):
                dve.wait_ge(qkt_ps, 2 * g + 2)
                V.tensor_scalar(kt[:, :, :], bank[7][:, :].rearrange("p (b n) -> p b n", b=2), pcol[:, C_KG:C_KG + 1],
                                None, ALU.mult).then_inc(kt_ready, 1)
                score_max(g, 0)
                cmp_max(g)
                for i in range(8):
                    if i < 7:
                        score_max(g, i + 1)
                    score_scale(g, i)
                    if i == 0:
                        cmp_scale(g)
                    if i in (2, 4, 6):
                        window_t(g, i // 2 - 1)
                    if i == 5:
                        out_low(g, 0)
                        if g < G - 1:
                            qkv_sums(g + 1)
                    if i >= 6:
                        low(At(N_ATT + 2 * (g + 2) + i - 6))
                window_t(g, 3)
                out_low(g, 1)
                if g < G - 1:
                    qkv_norm(g + 1)
            for i in range(2):
                low(At(N_MLP0 + i))
            residual(0, N_WO + 3)

            def mlp(layer, base):
                def square(j, half):
                    dve.wait_ge(relu_ready, j.n(2, 2 * MJ * layer + half + 1))
                    V.scalar_tensor_tensor(rbuf[:, half, :], bank[4 + 2 * (j.s % 2) + half][:, :], 0.0,
                                           rbuf[:, half, :], ALU.max, ALU.mult).then_inc(sq_ready, 1)

                def hid_low(j, half):
                    dve.wait_ge(hid_hi, j.n(2, 2 * MJ * layer + half + 1))
                    V.tensor_tensor(htl[:, j.s % 2, 2 * half:2 * half + 2, :],
                                    rbuf[:, half, :].rearrange("p (m n) -> p m n", m=2),
                                    hth[:, j.s % 2, 2 * half:2 * half + 2, :].bitcast(F32), ALU.subtract).then_inc(hid_lo, 1)

                def body(j, n):
                    low(n + 2)
                    square(j + 1, 0)
                    low(n + 3)
                    hid_low(j + 1, 0)
                    square(j + 1, 1)
                    low(n + 4)
                    hid_low(j + 1, 1)
                    low(n + 5)
                square(At(0), 0)
                low(At(base + 2))
                hid_low(At(0), 0)
                square(At(0), 1)
                low(At(base + 3))
                hid_low(At(0), 1)
                body(At(0), At(base + 2))
                with dve.Fori(0, (MJ - 2) // 2) as it:
                    for u in range(2):
                        body(At(1 + u, it, 2), At(base + 6 + 4 * u, it, 8))
                if layer == 0:
                    low(At(base + 4 * MJ))
                    low(At(base + 4 * MJ + 1))

            norm(1)
            mlp(0, N_MLP0)
            residual(1, N_SSD - 1)

            norm(2)
            low(At(N_SSD + 2))
            V.memset(xb[:, :, 0:3], 0.0).then_inc(dve_step, 1)
            step.k += 1
            dve.wait_ge(dt_ps, 1)
            step.mark(V.tensor_tensor(dta[:, :, :], bank[6][:, 0:2 * SH].rearrange("p (c h) -> p c h", c=2),
                                      view(dtb[:, 0:1], 0, [[0, 2], [1, SH]]), ALU.add))
            step.wait(dve)
            step.mark(V.tensor_scalar_mul(dtt[:, 1, :, :], dta[:, :, :], -1.0))
            step.wait(dve)
            V.tensor_tensor(dtt[:, 0, :, :], dta[:, :, :], dtt[:, 1, :, :], ALU.min).then_inc(dt_neg, 1)
            dve.wait_ge(dt_exp, 2)
            V.tensor_scalar_add(dtt[:, 2, :, :], dtt[:, 1, :, :], 1.0).then_inc(dt_one, 1)
            dve.wait_ge(dt_one, 1)
            step.mark(V.tensor_scalar(dtt[:, 0, :, :], dtt[:, 2, :, :], -1.0, 1e-30, ALU.add, ALU.add))
            step.wait(dve)
            step.mark(V.reciprocal(dtt[:, 0, :, :], dtt[:, 0, :, :]))
            step.wait(dve)
            dve.wait_ge(dt_ln, 1)
            step.mark(V.scalar_tensor_tensor(dtt[:, 3, :, :], dtt[:, 3, :, :], 1e-30, dtt[:, 0, :, :], ALU.add, ALU.mult))
            step.wait(dve)
            step.mark(V.tensor_tensor(dtt[:, 3, :, :], dtt[:, 3, :, :], dtt[:, 1, :, :], ALU.mult))
            step.wait(dve)
            step.mark(V.scalar_tensor_tensor(dt[:, :, :], dta[:, :, :], 0.0, dtt[:, 3, :, :], ALU.max, ALU.add))
            step.wait(dve)
            V.scalar_tensor_tensor(dta[:, :, :], dt[:, :, :], -1.0, view(ealog[:, 0:1], 0, [[0, 2], [1, SH]]),
                                   ALU.mult, ALU.mult).then_inc(dt_ready, 1)
            dve.wait_ge(acs_ps, 1)
            V.tensor_copy(acs[:, :, :], bank[6][:, 64:128].rearrange("p (c h) -> p c h", c=2)).then_inc(acs_ready, 1)
            dve.wait_ge(acs_ready, 1)
            step.mark(V.tensor_scalar_mul(nacs[:, :, :], acs[:, :, :], -1.0))
            V.tensor_tensor(dtt[:, 0, 0, :], bank[6][:, 128:160], acs[:, 0, :], ALU.subtract).then_inc(acs_ready, 1)
            dve.wait_ge(decay_ready, 2)
            V.tensor_tensor(wend[:, :], wend[:, :], dt[:, 0, :], ALU.mult).then_inc(wend_ready, 1)

            def conv(g, i):
                dve.wait_ge(conv_in, g.n(2, i + 1))
                if g.s:
                    dve.wait_ge(xc_ready, g.n(2, i - 1))

                def col(q, tap):
                    first = (C_CB if tap == 4 else tap * 32) + (q if q < 2 else 16 + 8 * (q - 2))
                    t = pcol if tap == 4 else ccol
                    return t[:, bass.ds(g.n(2 if q < 2 else 1, first), 1)]
                for tap in (3, 0, 1, 2):
                    for q in (2 * i, 2 * i + 1):
                        if tap != 3:
                            step.wait(dve, step.k - 1)
                        if tap == 3:
                            ins = V.tensor_scalar(cacc[:, q, :], xb[:, q, 3:3 + S], col(q, 3), col(q, 4), ALU.mult, ALU.add)
                        else:
                            ins = V.scalar_tensor_tensor(cacc[:, q, :], xb[:, q, tap:tap + S], col(q, tap), cacc[:, q, :],
                                                         ALU.mult, ALU.add)
                        if tap == 2 and q % 2:
                            ins.then_inc(conv_done, 1)
                        else:
                            step.mark(ins)

            step.wait(dve)
            conv(At(0), 0)
            conv(At(0), 1)
            low(At(N_SSD + 3))

            def ssd(g, n, last=False):
                dve.wait_ge(t_ps, g.n(2, 1))
                if g.s:
                    dve.wait_ge(ys_ps, g.n())
                    dve.wait_ge(sk_ready, g.n(2))
                V.tensor_copy(xsn[:, :, :], bank[7][:, :].rearrange("p (c n) -> p c n", c=2)).then_inc(xsn_ready, 1)
                dve.wait_ge(bn_ready, g.n(1, 1))
                for i in range(8):
                    c, h = i // 4, i % 4
                    dve.wait_ge(e_ready, g.n(8, i + 1))
                    V.scalar_tensor_tensor(eb[:, c, h, :], eb[:, c, h, :], dt[:, c, bass.ds(g.n(4, h), 1)],
                                           bank[6][:, c * P:(c + 1) * P], ALU.mult, ALU.mult).then_inc(m_ready, 1)
                if not last:
                    low(n + 1)
                    low(n + 2)
                    conv(g + 1, 0)
                dve.wait_ge(ys_ps, g.n(1, 1))
                dve.wait_ge(sk_ready, g.n(2, 2))
                if g.s:
                    dve.wait_ge(yt_ps, g.n())
                step.mark(V.tensor_tensor(y[:, 1, :].rearrange("p (h d) -> p h d", h=4),
                                          bank[7][:, S:2 * S].rearrange("p (h d) -> p h d", h=4),
                                          view(eacs[:, bass.ds(g.n(4), 4)], 0, [[1, 4], [0, DH]]), ALU.mult))
                step.mark(V.tensor_tensor(y[:, 0, :], bank[6][:, 0:S], sk[:, 0, :], ALU.add))
                step.wait(dve, step.k - 1)
                step.mark(V.tensor_tensor(y[:, 1, :], y[:, 1, :], sk[:, 1, :], ALU.add))
                step.wait(dve)
                step.mark(V.tensor_tensor(y[:, 1, :], bank[6][:, S:2 * S], y[:, 1, :], ALU.add))
                step.wait(dve)
                dve.wait_ge(z_ready, g.n(1, 1))
                V.tensor_tensor(y[:, :, :].rearrange("p c n -> p (c n)"), y[:, :, :].rearrange("p c n -> p (c n)"),
                                sz[:, :], ALU.mult).then_inc(y_ready, 1)
                dve.wait_ge(yrstd_ready, g.n(1, 1))
                for c in range(TT):
                    V.tensor_scalar(y[:, c, :], y[:, c, :], sst[:, 4 + c:5 + c], 16.0, ALU.mult, ALU.mult).then_inc(yn_ready, 1)
                if not last:
                    conv(g + 1, 1)
                    low(n + 3)
                    low(n + 4)
                dve.wait_ge(yt_hi, g.n(2, 2))
                for q in range(2):
                    V.scalar_tensor_tensor(ytl[:, q, :], bank[7][:, q * S:(q + 1) * S],
                                           pcol[:, bass.ds(g.n(2, C_SSDN + q), 1)], yth[:, q, :].bitcast(F32),
                                           ALU.mult, ALU.subtract).then_inc(yt_lo, 1)

            per = 2 * 7 + 4
            before = step.base.s + step.k
            step.enter(At(before))
            ssd(At(0), At(N_SSD + 3))
            assert step.k == per
            with dve.Fori(0, (SG - 2) // 2) as it:
                for u in range(2):
                    step.enter(At(before + per * (1 + u), it, 2 * per))
                    ssd(At(1 + u, it, 2), At(N_SSD + 7 + 4 * u, it, 8))
            step.enter(At(before + per * (SG - 1)))
            low(At(N_MLP1))
            low(At(N_MLP1 + 1))
            ssd(At(SG - 1), None, last=True)
            residual(2, N_MLP1 - 1)

            norm(3)
            mlp(1, N_MLP1)
            residual(3, N_END - 1)

        @block.tensor
        def _(pe):
            T = nc.tensor

            def mm3(out, st, mv, start, stop):
                T.matmul(out, st[0], mv[0], start=start, stop=False)
                T.matmul(out, st[0], mv[1], start=False, stop=False)
                return T.matmul(out, st[1], mv[0], start=False, stop=stop)

            def ready(n):
                pe.wait_ge(low_ready, n.n(1, 1))

            def w(n, a_, b_, width):
                lo, hi = a_ * width + b_.start, a_ * width + b_.stop
                return whi[:, n.s % HL, lo:hi], wlo[:, n.s % HL, lo:hi]

            def xt(k, c):
                return xth[:, k, c * P:(c + 1) * P], xtl[:, k, c * P:(c + 1) * P]

            def xt_all(k):
                return xth[:, k, :], xtl[:, k, :]

            def wide(n, first, banks):
                ready(n)
                for k in range(4):
                    for c in range(TT):
                        last = mm3(banks[c][:, :], xt(first + k, c), w(n, k, slice(0, 512), 512),
                                   first + k == 0, first + k == KD - 1)
                last.then_inc(piece_used, 1)

            def features(n, out):
                ready(n)
                for m in range(2):
                    for k in range(KD):
                        last = mm3(out[:, m * S:(m + 1) * S], w(n, k, slice(m * P, (m + 1) * P), 256), xt_all(k),
                                   k == 0, k == KD - 1)
                last.then_inc(piece_used, 1)

            def back(n, st, start, stop):
                ready(n)
                if stop:
                    order = [(m, c, nh) for c in range(TT) for nh in range(2) for m in range(2)]
                else:
                    order = [(m, c, nh) for m in range(2) for c in range(TT) for nh in range(2)]
                for m, c, nh in order:
                    h, l = st(m)
                    last = mm3(bank[2 * c + nh][:, :], (h[:, c * P:(c + 1) * P], l[:, c * P:(c + 1) * P]),
                               w(n, m, slice(nh * 512, (nh + 1) * 512), 1024), start and m == 0, stop and m == 1)
                    if stop and m == 1 and (c, nh) != (1, 1):
                        last.then_inc(y_ps, 1)
                last.then_inc(piece_used, 1)

            def norm_t(q):
                pe.wait_ge(xn_ready, 2 * (q + 1))
                for b in range(4):
                    for k in (2 * b, 2 * b + 1):
                        for c in range(TT):
                            o = (k % 2) * S + c * P
                            last = T.transpose(bank[4 + b][:, o:o + P], xn[:, c, k * P:(k + 1) * P], ident)
                    last.then_inc(xt_ps, 1)

            pe.wait_ge(params_in, 16)
            pe.wait_ge(rows_in, 16 * 2)
            pe.wait_ge(pool_set, 7)
            T.matmul(bank[2][0:H, :], table[:, :], onehot, start=True, stop=True).then_inc(strip_ps, 1)

            norm_t(0)
            pe.wait_ge(xt_lo, 8)
            for i in range(2):
                wide(At(N_KVC + i), 4 * i, (bank[4], bank[5]))
            pe.wait_ge(small_lo, 2)
            for c in range(TT):
                for k in range(KD):
                    last = mm3(bank[6][:, c * 64:c * 64 + NB], xt(k, c), (gwh[:, k, :], gwl[:, k, :]), k == 0, k == KD - 1)
            last.then_inc(gate_ps, 1)
            pe.wait_ge(kvc_ready, 2)
            pe.wait_ge(strip_ready, 1)
            for i in range(8):
                for c in range(TT):
                    o = (i % 2) * S + c * P
                    last = T.transpose(bank[i // 2][:, o:o + P], xn[:, c, i * P:(i + 1) * P], ident)
                if i % 2:
                    last.then_inc(kvt_ps, 1)
            pe.wait_ge(gate_ready, 1)
            for c in range(TT):
                last = T.matmul(bank[7][:, (1 - c) * 64:(1 - c) * 64 + NB], flip, view(gx, c * NB, [[1, NB]]), start=True, stop=True)
            last.then_inc(gate_flip, 1)
            for kv in range(2):
                pe.wait_ge(blk_lo, kv + 1)
                if kv:
                    pe.wait_ge(gate_ready, 2)
                for i in range(2):
                    n = At(N_W1 + 2 * kv + i)
                    ready(n)
                    for m in range(2):
                        for j in range(8):
                            jj = 8 * i + j
                            last = mm3(bank[4 + 2 * kv + m][:, 0:60], w(n, j, slice(m * P, (m + 1) * P), HID),
                                       (blkh[:, kv, jj, :], blkl[:, kv, jj, :]), jj == 0, jj == 15)
                    last.then_inc(piece_used, 1)
            pe.wait_ge(blk_ready, 16)
            for kv in range(2):
                pe.wait_ge(hid_ready, 2 * kv + 2)
                for g in range(G):
                    for m in range(2):
                        hid = hidv[:, m, g, :] if kv else hidk[:, m, g, :]
                        last = T.matmul(bank[kv][0:P if kv else 32, g * DH:(g + 1) * DH], hid, w2[:, kv, m, :],
                                        start=m == 0, stop=m == 1)
                last.then_inc(cmp_ps, 1)
            for i in range(2):
                wide(At(N_ATT + i), 4 * i, (bank[4], bank[5]))
            pe.wait_ge(kcn_ready, 2)
            for g in range(G):
                last = T.transpose(bank[2][:, g * 32:(g + 1) * 32], kcn[:, g, :, :].rearrange("p b d -> p (b d)"), par[0:32, NPCOL + 128:NPCOL + 160])
            last.then_inc(kct_ps, 1)

            def scores(g, i):
                h, t, n = i // 2, i % 2, 8 * g + i
                nk = P * (t + 1)
                if n >= 2:
                    pe.wait_ge(sm_max, 2 * n - 2)
                pr, b = h // 2, h % 2
                part = slice(b * DH, (b + 1) * DH)
                T.matmul(bank[t][:, 0:2 * nk], qt[part, pr * S + t * P:pr * S + (t + 1) * P], kt[part, :, 0:nk],
                         start=True, stop=True).then_inc(sc_ps, 1)

            def probs_t(g, i):
                h, t, n = i // 2, i % 2, 8 * g + i
                m = 4 * g + h
                pe.wait_ge(p_ready, 2 * n + 2)
                if t == 0 and m:
                    pe.wait_ge(pt_sel, m)
                    pe.wait_ge(pt_win, m)
                for b in range(2):
                    for kk in range(t + 1):
                        o = (t + kk) * P
                        last = T.transpose(bank[2 + b][:, o:o + P], probs[:, t, b * S + kk * P:b * S + (kk + 1) * P], ident)
                last.then_inc(pt_ps, 1)

            def values(g, h):
                m = 4 * g + h
                pr, b = h // 2, h % 2
                pe.wait_ge(pt_sel, m + 1)
                pe.wait_ge(pt_win, m + 1)
                if h == 0:
                    pe.wait_ge(pct_ready, g + 1)
                if h == 2:
                    pe.wait_ge(ot_lo, 2 * g + 1)
                out = bank[7][b * DH:(b + 1) * DH, pr * S:(pr + 1) * S]
                for s in range(2):
                    v = 384 + 192 * s
                    T.matmul(out, qkv[:, g % 2, 0, v:v + DH], pt[:, m % 2, s, 0:S], start=s == 0, stop=False)
                    T.matmul(out[:, P:S], qkv[:, g % 2, 1, v:v + DH], pt[:, m % 2, s, S:TW], start=False, stop=False)
                T.matmul(out, vcmp[32 * h:32 * h + 32, g, :], pct[32 * h:32 * h + 32, :], start=False, stop=True).then_inc(pv_done, 1)

            for g in range(G):
                pe.wait_ge(qkv_ready, 8 * g + 8)
                if g:
                    pe.wait_ge(pct_ready, g)
                    pe.wait_ge(ot_lo, 2 * g)
                else:
                    pe.wait_ge(hid_ready, 4)
                for pr in range(2):
                    for c in range(TT):
                        o = pr * S + c * P
                        last = T.transpose(bank[6][:, o:o + P], qkv[:, g % 2, c, pr * P:(pr + 1) * P], ident)
                last.then_inc(qkt_ps, 1)
                for s in range(2):
                    for c in range(TT):
                        o = s * S + c * P
                        last = T.transpose(bank[7][:, o:o + P], qkv[:, g % 2, c, 256 + 192 * s:384 + 192 * s], ident)
                last.then_inc(qkt_ps, 1)
                pe.wait_ge(qt_ready, g + 1)
                pe.wait_ge(kbd_ready, 2)
                for c in range(TT):
                    for pr in range(2):
                        o = (1 - c) * 64 + pr * 32
                        last = T.matmul(bank[6][:, o:o + 32], qt[:, pr * S + c * P:pr * S + (c + 1) * P], kbd[:, g, :, :],
                                        start=True, stop=True)
                last.then_inc(csc_ps, 1)
                pe.wait_ge(kt_ready, g + 1)
                if g == 0:
                    pe.wait_ge(vcmp_ready, 1)
                scores(g, 0)
                for i in range(8):
                    if i < 7:
                        scores(g, i + 1)
                    if i == 1:
                        pe.wait_ge(pc_ready, g + 1)
                        for c in range(TT):
                            last = T.transpose(bank[6][:, S + c * P:S + (c + 1) * P],
                                               pc[:, 1 - c, :, :].rearrange("p h n -> p (h n)"), ident)
                        last.then_inc(pct_ps, 1)
                    probs_t(g, i)
                    if i in (2, 4, 6):
                        values(g, i // 2 - 1)
                    if g < G - 1 and i in (1, 3):
                        wide(At(N_ATT + 2 * (g + 1) + i // 2), 4 * (i // 2), (bank[4], bank[5]))
                values(g, 3)
            pe.wait_ge(ot_lo, 2 * G)
            for i in range(4):
                back(At(N_WO + i), lambda m, i=i: (oth[:, 2 * i + m, :], otl[:, 2 * i + m, :]), i == 0, i == 3)

            def mlp(layer, base):
                def up(j, n, half):
                    if layer or j.s >= 2:
                        pe.wait_ge(sq_ready, j.n(2, 2 * MJ * layer + half - 3))
                    features(n + half, bank[4 + 2 * (j.s % 2) + half])

                def down(j, n, start=False, stop=False):
                    for half in range(2):
                        pe.wait_ge(hid_lo, j.n(2, 2 * MJ * layer + half + 1))
                        back(n + half, lambda m, half=half: (hth[:, j.s % 2, 2 * half + m, :], htl[:, j.s % 2, 2 * half + m, :]),
                             start and half == 0, stop and half == 1)
                pe.wait_ge(xt_lo, 16 * (layer + 1))
                for half in range(2):
                    up(At(0), At(base), half)
                for half in range(2):
                    up(At(1), At(base + 2), half)
                down(At(0), At(base + 4), start=True)
                with pe.Fori(0, (MJ - 2) // 2) as it:
                    for u in range(2):
                        j, n = At(1 + u, it, 2), At(base + 6 + 4 * u, it, 8)
                        for half in range(2):
                            up(j + 1, n, half)
                        down(j, n + 2)
                down(At(MJ - 1), At(base + 4 * MJ - 2), stop=True)

            norm_t(1)
            mlp(0, N_MLP0)

            norm_t(2)
            pe.wait_ge(xt_lo, 24)
            for c in range(TT):
                for k in range(KD):
                    last = mm3(bank[6][:, c * SH:(c + 1) * SH], xt(k, c), (dwh[:, k, :], dwl[:, k, :]), k == 0, k == KD - 1)
            last.then_inc(dt_ps, 1)
            features(At(N_SSD), bank[4])
            features(At(N_SSD + 1), bank[5])
            pe.wait_ge(dt_ready, 1)
            for c in range(TT):
                T.matmul(bank[6][:, 64 + c * SH:64 + (c + 1) * SH], tri, dta[:, c, :], start=True, stop=True)
            T.matmul(bank[6][:, 128:160], ones[:, :], dta[:, 0, :], start=True, stop=True).then_inc(acs_ps, 1)
            pe.wait_ge(acs_ready, 1)
            for c in range(TT):
                last = T.transpose(bank[7][0:SH, c * P:(c + 1) * P], acs[:, c, :], ident)
            last.then_inc(acst_ps, 1)
            pe.wait_ge(acs_ready, 2)

            def gate_cols(n):
                ready(n)
                for c in range(TT):
                    for k in range(KD):
                        last = mm3(bank[6][:, c * S:(c + 1) * S], xt(k, c), w(n, k, slice(0, 256), 256), k == 0, k == KD - 1)
                last.then_inc(piece_used, 1)
            gate_cols(At(N_SSD + 2))

            def ssd_back(g, n, start=False, stop=False):
                pe.wait_ge(yt_lo, g.n(2, 2))
                back(n, lambda m: (yth[:, m, :], ytl[:, m, :]), start, stop)

            def ssd(g, n, last_group=False):
                par = g.s % 2
                pe.wait_ge(xc_ready, g.n(2, 1))
                if g.s == 0:
                    pe.wait_ge(acst_ready, 1)
                else:
                    pe.wait_ge(yt_lo, g.n(2))
                for c in range(TT):
                    for q in range(2):
                        last = T.transpose(bank[7][:, c * S + q * P:c * S + (q + 1) * P], xc[:, par, q, c * P:(c + 1) * P], ident)
                last.then_inc(t_ps, 1)
                pe.wait_ge(xc_ready, g.n(2, 2))
                pe.wait_ge(z_ready, g.n(1, 1))
                T.transpose(bank[6][:, 2 * P:3 * P], xc[:, par, 2, 0:P], ident)
                for c in range(TT):
                    last = T.matmul(bank[6][:, c * P:(c + 1) * P], xc[:, par, 2, c * P:(c + 1) * P],
                                    xc[:, par, 3, c * P:(c + 1) * P], start=True, stop=True)
                last.then_inc(t_ps, 1)
                if g.s:
                    ssd_back(g + (-1), At(N_MLP1 - 2) if last_group else n + (-1), start=g.s == 1 and g.it is None)
                if not last_group:
                    pe.wait_ge(conv_in, g.n(2, 1))
                    features(n, bank[4])
                pe.wait_ge(xw_ready, g.n(1, 1))
                pe.wait_ge(bn_ready, g.n(1, 1))
                T.matmul(bank[7][:, 0:S], bn[:, :], xw[:, :], start=True, stop=True).then_inc(s_ps, 1)
                pe.wait_ge(m_ready, g.n(8, 8))
                for c in range(TT):
                    for h in range(4):
                        o = c * S + h * DH
                        T.matmul(bank[6][:, o:o + DH], eb[:, c, h, :], xsn[:, c, h * DH:(h + 1) * DH], start=True, stop=True)
                pe.wait_ge(prev_ready, g.n(1, 1))
                T.matmul(bank[7][:, S:2 * S], xc[:, par, 3, P:2 * P], prev[:, :], start=True, stop=True).then_inc(ys_ps, 1)
                if not last_group:
                    pe.wait_ge(conv_in, g.n(2, 2))
                    features(n + 1, bank[5])
                    pe.wait_ge(y_ready, g.n(1, 1))
                    gate_cols(n + 2)
                pe.wait_ge(yn_ready, g.n(2, 2))
                for q in range(2):
                    for c in range(TT):
                        last = T.transpose(bank[7][:, q * S + c * P:q * S + (c + 1) * P], y[:, c, q * P:(q + 1) * P], ident)
                last.then_inc(yt_ps, 1)

            ssd(At(0), At(N_SSD + 3))
            ssd(At(1), At(N_SSD + 7))
            with pe.Fori(0, (SG - 4) // 2) as it:
                for u in range(2):
                    ssd(At(2 + u, it, 2), At(N_SSD + 11 + 4 * u, it, 8))
            ssd(At(SG - 2), At(N_SSD + 7 + 4 * (SG - 3)))
            ssd(At(SG - 1), None, last_group=True)
            ssd_back(At(SG - 1), At(N_MLP1 - 1), stop=True)

            norm_t(3)
            mlp(1, N_MLP1)


def constants():
    tri = np.triu(np.ones((P, P), np.float32))
    dist = 255 - np.arange(512)
    far = BUCKETS // 2 + (np.log(np.maximum(dist, 1) / (BUCKETS // 2)) / np.log(128 / (BUCKETS // 2))
                          * (BUCKETS - BUCKETS // 2)).astype(np.int64)
    bucket = np.where(dist < BUCKETS // 2, np.maximum(dist, 0), np.minimum(far, BUCKETS - 1))
    bucket[dist < 0] = BUCKETS
    onehot = np.zeros((BUCKETS + 1, 512), np.float32)
    onehot[bucket, np.arange(512)] = 1.0
    return np.eye(P, dtype=np.float32), tri, np.where(tri > 0, 0.0, NEG).astype(np.float32), onehot


def tiles(w):
    return w.reshape(-1, P, w.shape[1]).transpose(1, 0, 2).reshape(P, -1)


def stream(t):
    out = []
    w = t["nsa_w_in"][0]
    for k in range(2):
        out.append(tiles(w[k * 512:(k + 1) * 512, QC:QC + 512]))
    for name in ("cmp_w1_k", "cmp_w1_v"):
        w1 = t[name][0].reshape(CB * DH, HID)
        out += [tiles(w1[:1024]), tiles(w1[1024:])]
    for g in range(G):
        starts = [g * 256] + [QC + 512 + b * 256 + g * DH for b in range(4)]
        cols = np.concatenate([w[:, c:c + n] for c, n in zip(starts, (256, DH, DH, DH, DH))], axis=1)
        out += [tiles(cols[:512]), tiles(cols[512:])]
    out += [tiles(t["nsa_w_out"][0][i * 256:(i + 1) * 256]) for i in range(4)]

    def mlp(layer):
        up, down = t["mlp_w_up"][layer], t["mlp_w_down"][layer]
        ups = [tiles(up[:, i * 256:(i + 1) * 256]) for i in range(2 * MJ)]
        downs = [tiles(down[i * 256:(i + 1) * 256]) for i in range(2 * MJ)]
        seq = ups[:2]
        for j in range(MJ):
            seq += ups[2 * j + 2:2 * j + 4] + downs[2 * j:2 * j + 2]
        return seq

    out += mlp(0)
    w, back = t["ssd_w_in"][0], t["ssd_w_out"][0]
    for g in range(SG + 1):
        if g >= 2:
            out.append(tiles(back[(g - 2) * 256:(g - 1) * 256]))
        if g < SG:
            b0 = XBC0 + DI + g * 128
            bc = np.concatenate([w[:, b0:b0 + 128], w[:, b0 + SG * 128:b0 + SG * 128 + 128]], axis=1)
            out += [tiles(w[:, XBC0 + g * 256:XBC0 + (g + 1) * 256]), tiles(bc), tiles(w[:, g * 256:(g + 1) * 256])]
    out.append(tiles(back[(SG - 1) * 256:]))
    out += mlp(1)
    return np.stack(out)


def kernel(**inputs):
    import concourse.bacc as bacc
    from concourse.bass_utils import run_bass_kernel_spmd

    t = {name: np.asarray(v) for name, v in inputs.items()}
    eye, tri, segmask, onehot = constants()

    def cols(v):
        return v.reshape(-1, P).T

    params = np.concatenate(
        [cols(t["norm_mix_w"]), cols(t["norm_mlp_w"]), cols(t["ssd_norm_w"]), cols(t["ssd_conv_b"]),
         cols(t["cmp_pe_k"]), cols(t["cmp_pe_v"]), cols(np.concatenate([t["nsa_q_gain"]] * 2)),
         cols(np.concatenate([t["nsa_k_gain"]] * 2)), cols(t["ssd_conv_w"]), eye, tri, segmask], axis=1)
    small_w = np.concatenate(
        [tiles(t["cmp_w2_k"][0]), tiles(t["cmp_w2_v"][0]), tiles(t["ssd_w_in"][0][:, DT0:DT0 + SH]),
         tiles(t["nsa_w_in"][0][:, GATE0:GATE0 + NB]), eye[::-1]], axis=1)
    given = {"x": t["x"], "stream": stream(t), "params": params, "small_w": small_w, "rel_table": t["rel_table"],
             "onehot": onehot, "ssd_dt_bias": t["ssd_dt_bias"], "ssd_a_log": t["ssd_a_log"], "ssd_d": t["ssd_d"]}

    nc = bacc.Bacc("TRN2", target_bir_lowering=False, num_devices=1)
    arrays, aps = {}, {}
    for name, v in given.items():
        arrays[f"in_{name}"] = np.ascontiguousarray(v)
        aps[name] = nc.dram_tensor(f"in_{name}", v.shape, mybir.dt.from_np(v.dtype), kind="ExternalInput").ap()
    aps["out"] = nc.dram_tensor("out", (1, S, D), F32, kind="ExternalOutput").ap()
    build(nc, aps)
    r = run_bass_kernel_spmd(nc, [arrays], core_ids=[0])
    return r.results[0]["out"]
```

```python
from contextlib import ExitStack

import concourse.bass as bass
import concourse.mybir as mybir
import numpy as np

F32 = mybir.dt.float32
F32R = mybir.dt.float32r
ACT = mybir.ActivationFunctionType
ALU = mybir.AluOpType
AX = mybir.AxisListType

P = 128
S = 256
D = 1024
TT = S // P
KD = D // P
H = 16
G = 4
DH = 64
QKV = 640
NCMP = 15
CB, CS = 32, 16
HID = 256
QC = 1024
GATE0 = QC + 6 * 256
NB = 3 * H
DI = 2048
SG = 8
SH = 32
XBC0 = DI
DT0 = DI + DI + 2 * SG * 128
MH = 4096
MJ = MH // 512
EPS = 1e-6
NEG = -1e30
TW = 384
BUCKETS = 32

PW = 2048
RAW = 4
HL = 4
PER = 16

N_KVC = 0
N_ATT = (2, 8, 10, 12)
N_W1 = 4
N_WO = 14
N_MLP0 = N_WO + 4
N_SSD = N_MLP0 + 4 * MJ
N_MLP1 = N_SSD + 4 * SG
N_END = N_MLP1 + 4 * MJ

C_MIX, C_MLP, C_SSDN, C_CB, C_PE, C_QG, C_KG = 0, 16, 32, 48, 80, 112, 113
NPCOL = 114
PAR_W = NPCOL + 128 + 3 * P
W2_0, DW_0, GW_0, FLIP_0 = 0, 256, 512, 896


class At:

    def __init__(self, s, it=None, step=0):
        self.s, self.it, self.step = s, it, step

    def __add__(self, k):
        return At(self.s + k, self.it, self.step)

    def n(self, mult=1, add=0):
        if self.it is None:
            return self.s * mult + add
        return self.it * (self.step * mult) + (self.s * mult + add)


class Steps:

    def __init__(self, sem):
        self.sem, self.base, self.k = sem, At(0), 0

    def enter(self, base):
        self.base, self.k = base, 0

    def mark(self, ins):
        ins.then_inc(self.sem, 1)
        self.k += 1
        return self.k

    def wait(self, eng, k=None):
        eng.wait_ge(self.sem, self.base.n(1, self.k if k is None else k))


def raw_round(n):
    v = PER * (n.s // RAW + 1)
    return v if n.it is None else n.it * (PER * n.step // RAW) + v


def view(ap, off, dims):
    return bass.AP(ap.tensor, ap.offset + off, [list(ap.ap[0])] + dims)


def rows(t, off, dims):
    return bass.AP(t.tensor, off, dims)


def build(nc, a):
    ctx = ExitStack()
    with ctx:
        def sb(name, shape, dt=F32, stack=ctx):
            return stack.enter_context(nc.sbuf_tensor(name, shape, dt))

        def sem(name):
            return ctx.enter_context(nc.semaphore(name))

        bank = [ctx.enter_context(nc.psum_tensor(f"bank{i}", [P, 512], F32)) for i in range(8)]
        strip_dram = nc.dram_tensor("strip_dram", (H, 512), F32, kind="Internal").ap()
        acs_dram = nc.dram_tensor("acs_dram", (SH, S), F32, kind="Internal").ap()

        raw = sb("raw", [P, RAW, PW])
        whi = sb("whi", [P, HL, PW], F32R)
        wlo = sb("wlo", [P, HL, PW], F32R)
        x = sb("x", [P, TT, D])
        xn = sb("xn", [P, TT, D])
        xth = sb("xth", [P, KD, S], F32R)
        xtl = sb("xtl", [P, KD, S], F32R)
        hth = sb("hth", [P, 2, 4, S], F32R)
        htl = sb("htl", [P, 2, 4, S], F32R)
        rbuf = sb("rbuf", [P, 2, 512])
        par = sb("par", [P, PAR_W])
        ones = sb("ones", [P, P])
        pcol, ccol = par[:, 0:NPCOL], par[:, NPCOL:NPCOL + 128]
        ident, tri, segmask = (par[:, NPCOL + 128 + i * P:NPCOL + 128 + (i + 1) * P] for i in range(3))
        table = sb("table", [BUCKETS + 1, H])
        small = sb("small", [P, 80])
        mhalf = sb("mhalf", [P, 16])
        epst = sb("epst", [P, 2])
        gq = sb("gq", [P, 1])
        dwh = sb("dwh", [P, KD, SH], F32R)
        dwl = sb("dwl", [P, KD, SH], F32R)
        w2 = sb("w2", [P, 2, 2, DH])
        gate = sb("gate", [P, TT, NB])
        dtb = sb("dtb", [P, SH])
        alog = sb("alog", [P, SH])
        dskip = sb("dskip", [P, SH])

        ssq = small[:, 0:4].rearrange("p (c h) -> p c h", c=TT)
        vsum, rstd = small[:, 4:6], small[:, 6:8]

        att = ExitStack()
        bias = sb("bias", [P, H, TW], F32, att)
        scratch = sb("scratch", [P, 2048], F32, att)
        qt, kt = rbuf[:, 0, :], rbuf[:, 1, :].rearrange("p (b n) -> p b n", b=2)
        pct = xn[:, 0, 0:S]
        tc = sb("tc", [P, TT, 4, 16], F32, att)
        pc = sb("pc", [P, TT, 4, 32], F32, att)
        cst = sb("cst", [P, 4, 8], F32, att)
        qst = sb("qst", [P, 4, 16], F32, att)
        hst = sb("hst", [P, 2, 8], F32, att)
        hidk = sb("hidk", [P, 2, G * NCMP], F32, att)
        hid = view(xn[0:G * NCMP, 0, 512:513], 0, [[HID, 2], [1, HID]])
        vcmp = xn[:, 0, S:2 * S].rearrange("p (g d) -> p g d", g=G)
        kst = sb("kst", [G * NCMP, 4], F32, att)
        kbd = sb("kbd", [P, G, 2, 16], F32, att)
        onehot, strip = scratch[0:BUCKETS + 1, 0:512], scratch[0:H, 512:1024]
        gw = scratch[:, 1024:1024 + KD * NB].rearrange("p (k n) -> p k n", k=KD)
        flip = scratch[:, 1408:1536]
        gx = view(tc[:, 0, 0, 0:1], 0, [[NB, TT], [1, NB]])
        dw = scratch[:, 1664:1664 + KD * SH].rearrange("p (k n) -> p k n", k=KD)
        kc = tc[0:G * NCMP, :, :, :].rearrange("p c h n -> p c (h n)")
        kcn = pc[0:G * NCMP, 0, :, :].rearrange("p (b h) n -> p b (h n)", b=2)
        hidv = scratch[:, 1024:2048].rearrange("p (m g n) -> p m g n", m=2, g=G)
        gates = ExitStack()
        gwh = sb("gwh", [P, KD, NB], F32R, gates)
        gwl = sb("gwl", [P, KD, NB], F32R, gates)
        gates.close()
        qkv = sb("qkv", [P, 2, TT, QKV], F32, att)
        pt = sb("pt", [P, 2, 2, TW], F32, att)
        att.close()

        xb = sb("xb", [P, 4, 3 + S])
        cacc = sb("cacc", [P, 4, S])
        xc = sb("xc", [P, 2, 4, S])
        sz = sb("sz", [P, 512])
        xsn = sb("xsn", [P, TT, S])
        bn = sb("bn", [P, P])
        eb = sb("eb", [P, TT, 4, P])
        acb = sb("acb", [P, 2, 4, TT, P])
        xw = sb("xw", [P, S])
        sk = sb("sk", [P, TT, S])
        prev = sb("prev", [P, S])
        y = sb("y", [P, TT, S])
        sst = sb("sst", [P, 6])
        yth = sb("yth", [P, 2, S], F32R)
        ytl = sb("ytl", [P, 2, S], F32R)
        dt = sb("dt", [P, TT, SH])
        dta = sb("dta", [P, TT, SH])
        dtt = sb("dtt", [P, 4, TT, SH])
        acs = sb("acs", [P, TT, SH])
        nacs = sb("nacs", [P, TT, SH])
        eacs = sb("eacs", [P, SH])
        wend = sb("wend", [P, SH])
        ealog = sb("ealog", [P, SH])
        acst = sb("acst", [SH, S])
        probs = scratch[:, 1024:2048].rearrange("p (b n) -> p b n", b=2)
        tsc = scratch[:, 0:1024].rearrange("p (b n) -> p b n", b=2)
        blk = view(scratch[:, 0:1], 0, [[60, 16], [1, 60]])
        blkh = view(hth[:, 0, 0, 0:1], 0, [[960, 2], [60, 16], [1, 60]])
        blkl = view(htl[:, 0, 0, 0:1], 0, [[960, 2], [60, 16], [1, 60]])
        oth = hth[:, :, :, :].rearrange("p a b n -> p (a b) n")
        otl = htl[:, :, :, :].rearrange("p a b n -> p (a b) n")

        def in_order(p):
            return view(bank[7][:, p * S + P - 1:p * S + P], 0, [[P, 2], [-1, P]])

        piece_in = [sem(f"piece_in{i}") for i in range(RAW)]
        high_ready, low_ready, piece_used = sem("high_ready"), sem("low_ready"), sem("piece_used")
        x_in, params_in, rows_in, w_small_in = sem("x_in"), sem("params_in"), sem("rows_in"), sem("w_small_in")
        rest_in = sem("rest_in")
        strip_in, bias_in, out_done = sem("strip_in"), sem("bias_in"), sem("out_done")
        acs_out, acs_in = sem("acs_out"), [sem("acs_in0"), sem("acs_in1")]
        strip_ps, strip_ready = sem("strip_ps"), sem("strip_ready")
        pool_set, gq_ready, small_hi, small_lo = sem("pool_set"), sem("gq_ready"), sem("small_hi"), sem("small_lo")
        sumsq_ready, rstd_ready, xn_ready = sem("sumsq_ready"), sem("rstd_ready"), sem("xn_ready")
        xt_ps, xt_hi, xt_lo, x_ready = sem("xt_ps"), sem("xt_hi"), sem("xt_lo"), sem("x_ready")
        y_ps = sem("y_ps")
        relu_ready, sq_ready, hid_hi, hid_lo = sem("relu_ready"), sem("sq_ready"), sem("hid_hi"), sem("hid_lo")
        gate_ps, gate_exp, gate_ready, gate_flip = sem("gate_ps"), sem("gate_exp"), sem("gate_ready"), sem("gate_flip")
        kvc_ready, kvt_ps, blk_ready, blk_hi, blk_lo = sem("kvc_ready"), sem("kvt_ps"), sem("blk_ready"), sem("blk_hi"), sem("blk_lo")
        hid_ready, cmp_ps, vcmp_ready = sem("hid_ready"), sem("cmp_ps"), sem("vcmp_ready")
        silu_ready, hid_ps = sem("silu_ready"), sem("hid_ps")
        kc_sq, kc_rstd, kcn_ready, kct_ps, kbd_ready = sem("kc_sq"), sem("kc_rstd"), sem("kcn_ready"), sem("kct_ps"), sem("kbd_ready")
        qkv_sq, qkv_ssq, qkv_rstd, qkv_ready = sem("qkv_sq"), sem("qkv_ssq"), sem("qkv_rstd"), sem("qkv_ready")
        qkt_ps, qt_ready, kt_ready = sem("qkt_ps"), sem("qt_ready"), sem("kt_ready")
        sc_ps, sm_max, sm_exp, p_ready = sem("sc_ps"), sem("sm_max"), sem("sm_exp"), sem("p_ready")
        pt_ps, pt_sel, pt_win = sem("pt_ps"), sem("pt_sel"), sem("pt_win")
        csc_ps, csc_ready, csc_exp, pc_ready, pct_ps, pct_ready = (
            sem("csc_ps"), sem("csc_ready"), sem("csc_exp"), sem("pc_ready"), sem("pct_ps"), sem("pct_ready"))
        pv_done, ot_hi, ot_lo = sem("pv_done"), sem("ot_hi"), sem("ot_lo")
        dve_step, act_step, pool_step = sem("dve_step"), sem("act_step"), sem("pool_step")
        dt_ps, dt_neg, dt_exp, dt_one, dt_ln, dt_ready = (
            sem("dt_ps"), sem("dt_neg"), sem("dt_exp"), sem("dt_one"), sem("dt_ln"), sem("dt_ready"))
        acs_ps, acs_ready, acst_ps, acst_ready, decay_ready, wend_ready = (
            sem("acs_ps"), sem("acs_ready"), sem("acst_ps"), sem("acst_ready"), sem("decay_ready"), sem("wend_ready"))
        masked, e_ready, m_ready = sem("masked"), sem("e_ready"), sem("m_ready")
        conv_in, conv_done, xc_ready, z_ready = sem("conv_in"), sem("conv_done"), sem("xc_ready"), sem("z_ready")
        t_ps, bn_ready, xsn_ready, xw_ready, sk_ready = sem("t_ps"), sem("bn_ready"), sem("xsn_ready"), sem("xw_ready"), sem("sk_ready")
        s_ps, prev_ready, ys_ps, y_ready, ysq_ready, yrstd_ready = (
            sem("s_ps"), sem("prev_ready"), sem("ys_ps"), sem("y_ready"), sem("ysq_ready"), sem("yrstd_ready"))
        yn_ready, yt_ps, yt_hi, yt_lo = sem("yn_ready"), sem("yt_ps"), sem("yt_hi"), sem("yt_lo")

        block = ctx.enter_context(nc.Block())

        @block.sync
        def _(sp):
            def piece(n):
                if n.s >= RAW:
                    sp.wait_ge(low_ready, n.n(1, 1 - RAW))
                src = a["stream"][bass.ds(n.n(), 1), :, :].rearrange("a p n -> (a p) n")
                sp.dma_start(raw[:, n.s % RAW, :], src).then_inc(piece_in[n.s % RAW], PER)

            def small_load(dst, src):
                sp.dma_start(dst, src).then_inc(w_small_in, 16)

            for c in range(TT):
                sp.dma_start(x[:, c, :], a["x"][0, c * P:(c + 1) * P, :]).then_inc(x_in, 16)
            sp.dma_start(par[:, :], a["params"]).then_inc(params_in, 16)
            for i in range(2):
                piece(At(i))
            small_load(scratch[:, 1024:1024 + KD * NB], a["small_w"][:, GW_0:GW_0 + KD * NB])
            small_load(scratch[:, 1664:1664 + KD * SH], a["small_w"][:, DW_0:DW_0 + KD * SH])
            small_load(flip, a["small_w"][:, FLIP_0:FLIP_0 + P])
            sp.wait_ge(strip_ready, 1)
            sp.dma_start(strip_dram, strip).then_inc(strip_in, 16)
            for i in range(2, 4):
                piece(At(i))
            sp.dma_start(w2[:, :, :, :].rearrange("p i m d -> p (i m d)"), a["small_w"][:, W2_0:W2_0 + 256]).then_inc(rest_in, 16)
            for t, name in ((dtb, "ssd_dt_bias"), (alog, "ssd_a_log"), (dskip, "ssd_d")):
                sp.dma_start(t[:, :], rows(a[name], 0, [[0, P], [1, SH]])).then_inc(rest_in, 16)
            sp.wait_ge(strip_in, 16)
            sp.dma_start(bias[:, :, :], rows(strip_dram, 0, [[1, P], [512, H], [1, TW]])).then_inc(bias_in, 16)
            first = RAW + (N_END - RAW) % 4
            for i in range(4, first):
                piece(At(i))
            with sp.Fori(0, (N_END - first) // 4) as it:
                for u in range(4):
                    piece(At(first + u, it, 4))
            for c in range(TT):
                sp.wait_ge(x_ready, 12 + 2 * (c + 1))
                sp.dma_start(a["out"][0, c * P:(c + 1) * P, :], x[:, c, :]).then_inc(out_done, 16)
            sp.wait_ge(out_done, 16 * TT)

        @block.scalar
        def _(act):
            step = Steps(act_step)
            copy = ACT.Copy

            def load(dst, src, s):
                act.dma_start(dst, src).then_inc(s, 16)

            def split(n):
                act.wait_ge(piece_in[n.s % RAW], raw_round(n))
                if n.s >= HL:
                    act.wait_ge(piece_used, n.n(1, 1 - HL))
                nc.scalar.activation(whi[:, n.s % HL, :], raw[:, n.s % RAW, :], copy).then_inc(high_ready, 1)

            load(table[0:BUCKETS, :], a["rel_table"], rows_in)
            load(onehot, a["onehot"], rows_in)

            def sumsq(q):
                for c in range(TT):
                    for h in range(2):
                        act.wait_ge(*((x_in, 16 * TT) if q == 0 else (x_ready, 4 * (q - 1) + 2 * c + h + 1)))
                        if q:
                            act.wait_ge(xt_ps, 4 * q)
                        half = slice(h * 512, (h + 1) * 512)
                        nc.scalar.activation(xn[:, c, half], x[:, c, half], ACT.Square,
                                             accum_out=ssq[:, c, h:h + 1]).then_inc(sumsq_ready, 1)

            def norm_t(q):
                for b in range(4):
                    act.wait_ge(xt_ps, 4 * q + b + 1)
                    for k in (2 * b, 2 * b + 1):
                        col = (q // 2) * 8 + (q % 2) * 16 + k
                        nc.scalar.activation(xth[:, k, :], bank[4 + b][:, (k % 2) * S:(k % 2 + 1) * S], copy,
                                             scale=pcol[:, col:col + 1]).then_inc(xt_hi, 1)

            sumsq(0)
            act.wait_ge(strip_ps, 1)
            nc.scalar.activation(strip, bank[2][0:H, :], copy).then_inc(strip_ready, 1)
            split(At(0))
            act.wait_ge(params_in, 16)
            norm_t(0)
            nc.scalar.activation(gq[:, :], pcol[:, C_QG:C_QG + 1], copy, scale=float(DH) ** -0.5).then_inc(gq_ready, 1)
            split(At(1))
            act.wait_ge(w_small_in, 16 * 3)
            nc.scalar.activation(gwh[:, :, :], gw[:, :, :], copy).then_inc(small_hi, 1)
            nc.scalar.activation(dwh[:, :, :], dw[:, :, :], copy).then_inc(small_hi, 1)
            split(At(2))
            for c in range(TT):
                act.wait_ge(piece_used, 2)
                nc.scalar.activation(view(xn[:, c, 0:1], 0, [[128, 8], [64, 2], [1, DH]]),
                                     view(bank[4 + c][:, 0:1], 0, [[64, 8], [0, 2], [1, DH]]), copy).then_inc(kvc_ready, 1)
            split(At(3))
            act.wait_ge(gate_ps, 1)
            for c in range(TT):
                nc.scalar.activation(view(gx, c * NB, [[1, NB]]), bank[6][:, c * 64:c * 64 + NB], ACT.Exp, scale=-1.0).then_inc(gate_exp, 1)
            split(At(4))
            for kv in range(2):
                act.wait_ge(blk_ready, 8 * (kv + 1))
                nc.scalar.activation(blkh[:, kv, :, :], blk, copy).then_inc(blk_hi, 1)
                if kv == 0:
                    split(At(5))

            def qkv_squares(g):
                for c in range(TT):
                    act.wait_ge(piece_used, N_ATT[g] + 2)
                    act.wait_ge(*((qkv_ssq, 2 * g) if g else (kvt_ps, 4)))
                    nc.scalar.activation(xn[:, 1, c * 512:c * 512 + 384], bank[4 + c][:, 0:384], ACT.Square).then_inc(qkv_sq, 1)

            def query_t(g):
                act.wait_ge(qkt_ps, 2 * g + 1)
                nc.scalar.activation(view(qt, 0, [[P, 4], [1, P]]), view(bank[4][:, P - 1:P], 0, [[P, 4], [-1, P]]), copy,
                                     scale=gq[:, 0:1]).then_inc(qt_ready, 1)

            def hidden(kv):
                act.wait_ge(piece_used, N_W1 + 2 * kv + 2)
                nc.scalar.activation(hid[:, kv, :], bank[6 + kv][0:G * NCMP, 0:HID], ACT.Silu).then_inc(silu_ready, 1)

            def selected_t(m):
                act.wait_ge(pt_ps, 2 * m + 2)
                if m >= 2:
                    act.wait_ge(pv_done, m - 1)
                nc.scalar.activation(pt[:, m % 2, 0, :], bank[2][:, 0:TW], copy).then_inc(pt_sel, 1)

            def out_high(p):
                act.wait_ge(pv_done, 2 * p + 2)
                nc.scalar.activation(view(oth[:, p, 0:1], 0, [[P, 2], [1, P]]), in_order(p % 2), copy).then_inc(ot_hi, 1)

            def cmp_exp(g):
                act.wait_ge(csc_ready, g + 1)
                nc.scalar.activation(tc[:, :, :, 0:NCMP], tc[:, :, :, 0:NCMP], ACT.Exp).then_inc(csc_exp, 1)

            qkv_squares(0)
            split(At(6))
            split(At(7))
            hidden(0)
            query_t(0)
            split(At(8))
            act.wait_ge(hid_ps, 1)
            nc.scalar.activation(hidk[:, :, :], view(bank[6][:, 256:257], 0, [[64, 2], [1, G * NCMP]]), copy).then_inc(hid_ready, 1)
            hidden(1)
            act.wait_ge(hid_ps, 2)
            act.wait_ge(pool_set, 7)
            for m in range(2):
                nc.scalar.activation(view(hidv[:, m, 0, 0:1], 0, [[P, G], [32, 4], [1, NCMP]]),
                                     view(bank[7][:, 256 + 64 * m:257 + 64 * m], 0, [[NCMP, G], [0, 4], [1, NCMP]]),
                                     copy).then_inc(hid_ready, 1)
            split(At(9))
            act.wait_ge(cmp_ps, 2)
            nc.scalar.activation(vcmp, bank[1][:, 0:256].rearrange("p (g d) -> p g d", g=G), copy).then_inc(vcmp_ready, 1)
            cmp_exp(0)
            for g in range(G):
                for i in range(8):
                    t = i % 2
                    nk = P * (t + 1)
                    n = 8 * g + i
                    act.wait_ge(sm_max, 2 * n + 2)
                    if n >= 2:
                        act.wait_ge(pt_ps, n - 1)
                    for b in range(2):
                        nc.scalar.activation(probs[:, t, b * S:b * S + nk], tsc[:, t, b * S:b * S + nk], ACT.Exp,
                                             bias=hst[:, t, b:b + 1], scale=-1.0,
                                             accum_out=hst[:, t, 2 + b:3 + b]).then_inc(sm_exp, 1)
                    if i == 1:
                        act.wait_ge(pct_ps, g + 1)
                        if g:
                            act.wait_ge(pv_done, 4 * g)
                        nc.scalar.activation(pct, bank[6][:, 256:512], copy).then_inc(pct_ready, 1)
                    if n and i % 2 == 0:
                        selected_t(n // 2 - 1)
                    if n > 1 and i in (1, 5):
                        out_high(2 * g - 1 if i == 1 else 2 * g)
                    if i in (0, 1):
                        split(At(10 + 2 * g + i))
                    if i == 2 and g < G - 1:
                        qkv_squares(g + 1)
                    if i == 5 and g < G - 1:
                        query_t(g + 1)
                    if i == 7 and g < G - 1:
                        cmp_exp(g + 1)
            selected_t(4 * G - 1)
            out_high(2 * G - 1)

            def mlp(layer, base):
                def relu(j, n, half):
                    act.wait_ge(piece_used, n.n(1, 1))
                    if layer or j.s:
                        act.wait_ge(hid_lo, j.n(2, 2 * MJ * layer + half - 1))
                    nc.scalar.activation(rbuf[:, half, :], bank[4 + 2 * (j.s % 2) + half][:, :], ACT.Relu).then_inc(relu_ready, 1)

                def high(j, half):
                    act.wait_ge(sq_ready, j.n(2, 2 * MJ * layer + half + 1))
                    nc.scalar.activation(hth[:, j.s % 2, 2 * half:2 * half + 2, :],
                                         rbuf[:, half, :].rearrange("p (m n) -> p m n", m=2), copy).then_inc(hid_hi, 1)

                def body(j, n):
                    split(n + 2)
                    relu(j + 1, n, 0)
                    split(n + 3)
                    high(j + 1, 0)
                    relu(j + 1, n + 1, 1)
                    split(n + 4)
                    high(j + 1, 1)
                    split(n + 5)
                relu(At(0), At(base), 0)
                split(At(base + 2))
                high(At(0), 0)
                relu(At(0), At(base + 1), 1)
                split(At(base + 3))
                high(At(0), 1)
                body(At(0), At(base + 2))
                with act.Fori(0, (MJ - 2) // 2) as it:
                    for u in range(2):
                        body(At(1 + u, it, 2), At(base + 6 + 4 * u, it, 8))
                if layer == 0:
                    split(At(base + 4 * MJ))
                    split(At(base + 4 * MJ + 1))

            for i in range(2):
                split(At(N_MLP0 + i))
            sumsq(1)
            norm_t(1)
            mlp(0, N_MLP0)

            sumsq(2)
            norm_t(2)
            split(At(N_SSD + 2))
            act.wait_ge(rest_in, 16 * 4)
            act.wait_ge(dt_neg, 1)
            nc.scalar.activation(dtt[:, 1, :, :], dtt[:, 0, :, :], ACT.Exp).then_inc(dt_exp, 1)
            nc.scalar.activation(ealog[:, :], alog[:, :], ACT.Exp).then_inc(dt_exp, 1)
            act.wait_ge(dt_one, 1)
            nc.scalar.activation(dtt[:, 3, :, :], dtt[:, 2, :, :], ACT.Ln).then_inc(dt_ln, 1)
            act.wait_ge(acst_ps, 1)
            nc.scalar.activation(acst[:, :], bank[7][0:SH, 0:S], copy).then_inc(acst_ready, 1)
            act.wait_ge(acs_ready, 2)
            nc.scalar.activation(eacs[:, :], acs[:, 1, :], ACT.Exp).then_inc(decay_ready, 1)
            nc.scalar.activation(wend[:, :], dtt[:, 0, 0, :], ACT.Exp).then_inc(decay_ready, 1)

            def conv_load(g, n, i):
                act.wait_ge(piece_used, n.n(1, 1))
                if g.s:
                    act.wait_ge(conv_done, g.n(2, i - 1))
                nc.scalar.activation(xb[:, 2 * i:2 * i + 2, 3:3 + S],
                                     bank[4 + i][:, :].rearrange("p (q n) -> p q n", q=2), copy).then_inc(conv_in, 1)

            def conv_silu(g, i):
                act.wait_ge(conv_done, g.n(2, i + 1))
                if g.s >= 2:
                    act.wait_ge(ys_ps, g.n(1, -1))
                nc.scalar.activation(xc[:, g.s % 2, 2 * i:2 * i + 2, :], cacc[:, 2 * i:2 * i + 2, :], ACT.Silu).then_inc(xc_ready, 1)

            def z_silu(g, n):
                act.wait_ge(piece_used, n.n(1, 3))
                if g.s:
                    act.wait_ge(y_ready, g.n())
                nc.scalar.activation(sz[:, :], bank[6][:, :], ACT.Silu).then_inc(z_ready, 1)

            conv_load(At(0), At(N_SSD), 0)
            conv_load(At(0), At(N_SSD + 1), 1)
            split(At(N_SSD + 3))
            conv_silu(At(0), 0)
            conv_silu(At(0), 1)
            z_silu(At(0), At(N_SSD))

            def ssd(g, n, last=False):
                for i in range(8):
                    c, h = i // 4, i % 4
                    act.wait_ge(masked, g.n(1, 1))
                    if g.s:
                        act.wait_ge(ys_ps, g.n())
                    nc.scalar.activation(eb[:, c, h, :], acb[:, g.s % 2, h, c, :], ACT.Exp,
                                         bias=nacs[:, c, bass.ds(g.n(4, h), 1)]).then_inc(e_ready, 1)
                act.wait_ge(t_ps, g.n(2, 2))
                nc.scalar.activation(bn[:, :], bank[6][:, 256:384], copy).then_inc(bn_ready, 1)
                if not last:
                    split(n + 1)
                    split(n + 2)
                    conv_load(g + 1, n, 0)
                act.wait_ge(s_ps, g.n(1, 1))
                nc.scalar.activation(prev[:, :], bank[7][:, 0:S], copy).then_inc(prev_ready, 1)
                if not last:
                    split(n + 3)
                for c in range(TT):
                    act.wait_ge(y_ready, g.n(1, 1))
                    nc.scalar.activation(sk[:, c, :], y[:, c, :], ACT.Square, accum_out=sst[:, c:c + 1]).then_inc(ysq_ready, 1)
                if not last:
                    conv_load(g + 1, n + 1, 1)
                for q in range(2):
                    act.wait_ge(yt_ps, g.n(1, 1))
                    if g.s:
                        if last:
                            act.wait_ge(piece_used, N_MLP1 - 1)
                        else:
                            act.wait_ge(piece_used, n.n())
                    nc.scalar.activation(yth[:, q, :], bank[7][:, q * S:(q + 1) * S], copy,
                                         scale=pcol[:, bass.ds(g.n(2, C_SSDN + q), 1)]).then_inc(yt_hi, 1)
                if not last:
                    split(n + 4)
                    conv_silu(g + 1, 0)
                    conv_silu(g + 1, 1)
                    z_silu(g + 1, n)
            ssd(At(0), At(N_SSD + 3))
            with act.Fori(0, (SG - 2) // 2) as it:
                for u in range(2):
                    ssd(At(1 + u, it, 2), At(N_SSD + 7 + 4 * u, it, 8))
            split(At(N_MLP1))
            split(At(N_MLP1 + 1))
            ssd(At(SG - 1), None, last=True)

            sumsq(3)
            norm_t(3)
            mlp(1, N_MLP1)


        @block.gpsimd
        def _(pool):
            step = Steps(pool_step)
            pool.memset(table[BUCKETS:BUCKETS + 1, :], NEG).then_inc(pool_set, 1)
            pool.wait_ge(pool_set, 1)
            pool.memset(mhalf[:, :], -0.5).then_inc(pool_set, 1)
            pool.memset(epst[:, :], 256 * EPS).then_inc(pool_set, 1)
            pool.memset(ones[:, :], 1.0).then_inc(pool_set, 1)
            pool.memset(qst[:, 2, :], DH ** -0.5).then_inc(pool_set, 1)
            pool.memset(kbd[:, :, :, :], 0.0).then_inc(pool_set, 1)
            def rsqrt(dst, tmp, src, width, n, done, part=P):
                step.mark(nc.gpsimd.tensor_scalar(tmp, src, width * EPS, None, ALU.add))
                step.wait(pool)
                return nc.gpsimd.tensor_tensor(dst, tmp, mhalf[0:part, 0:n], ALU.pow).then_inc(done, 1)

            def norm_stat(q):
                for c in range(TT):
                    pool.wait_ge(sumsq_ready, 4 * q + 2 * c + 1)
                    step.mark(nc.gpsimd.tensor_scalar(vsum[:, c:c + 1], ssq[:, c, 0:1], D * EPS, None, ALU.add))
                    step.wait(pool)
                    pool.wait_ge(sumsq_ready, 4 * q + 2 * c + 2)
                    step.mark(nc.gpsimd.tensor_tensor(vsum[:, c:c + 1], vsum[:, c:c + 1], ssq[:, c, 1:2], ALU.add))
                    step.wait(pool)
                    nc.gpsimd.tensor_tensor(rstd[:, c:c + 1], vsum[:, c:c + 1], mhalf[:, 0:1], ALU.pow).then_inc(rstd_ready, 1)

            pool.wait_ge(pool_set, 6)
            norm_stat(0)
            pool.wait_ge(gate_flip, 1)
            pool.memset(hidv, 0.0).then_inc(pool_set, 1)
            pool.wait_ge(pool_set, 7)

            def qkv_stat(g):
                for c in range(TT):
                    pool.wait_ge(qkv_ssq, 2 * g + c + 1)
                    if g:
                        pool.wait_ge(qkv_ready, 8 * g)
                    st = slice(8 * c, 8 * c + 6)
                    step.mark(nc.gpsimd.tensor_scalar(qst[:, 1, st], qst[:, 0, st], DH * EPS, None, ALU.add))
                    step.wait(pool)
                    nc.gpsimd.tensor_tensor(qst[:, 2, st], qst[:, 1, st], mhalf[:, 0:6], ALU.pow).then_inc(qkv_rstd, 1)

            qkv_stat(0)
            pool.wait_ge(kc_sq, 1)
            rsqrt(kst[:, 2:3], kst[:, 1:2], kst[:, 0:1], DH, 1, kc_rstd, G * NCMP)
            pool.wait_ge(kct_ps, 1)
            pool.memset(pc[:, :, :, :], 0.0).then_inc(pool_set, 1)
            for g in range(1, G):
                qkv_stat(g)
            norm_stat(1)
            norm_stat(2)

            pool.wait_ge(acst_ready, 1)
            pool.dma_start(acs_dram, acst[:, :]).then_inc(acs_out, 16)
            pool.wait_ge(acs_out, 16)

            def load_decay(g):
                src = acs_dram[bass.ds(g.n(4), 4), :]
                src = bass.AP(src.tensor, src.offset, [[0, P], [1, 4 * S]])
                pool.dma_start(acb[:, g.s % 2, :, :, :].rearrange("p h c l -> p (h c l)"), src).then_inc(acs_in[g.s % 2], 16)

            def mask(g):
                pool.wait_ge(acs_in[g.s % 2], 16 * (g.s // 2 + 1) if g.it is None else g.it * 16 + 16 * (g.s // 2 + 1))
                v = acb[:, g.s % 2, :, :, :].rearrange("p h c l -> p (h c) l")
                nc.gpsimd.tensor_tensor(v, v, view(segmask[:, 0:1], 0, [[0, 8], [1, P]]), ALU.add).then_inc(masked, 1)

            def heads(t, g, dims):
                return view(t[:, bass.ds(g.n(4), 4)], 0, dims)

            def ssd(g, last=False):
                if not last:
                    if g.s:
                        pool.wait_ge(e_ready, g.n(8))
                    load_decay(g + 1)
                pool.wait_ge(xsn_ready, g.n(1, 1))
                if g.s:
                    pool.wait_ge(s_ps, g.n())
                nc.gpsimd.tensor_tensor(xw[:, :].rearrange("p (h d) -> p h d", h=4),
                                        xsn[:, 0, :].rearrange("p (h d) -> p h d", h=4),
                                        heads(wend, g, [[1, 4], [0, DH]]), ALU.mult).then_inc(xw_ready, 1)
                if g.s:
                    pool.wait_ge(ysq_ready, g.n(2))
                for c in range(TT):
                    nc.gpsimd.tensor_tensor(sk[:, c, :].rearrange("p (h d) -> p h d", h=4),
                                            xsn[:, c, :].rearrange("p (h d) -> p h d", h=4),
                                            heads(dskip, g, [[1, 4], [0, DH]]), ALU.mult).then_inc(sk_ready, 1)
                if not last:
                    mask(g + 1)
                pool.wait_ge(ysq_ready, g.n(2, 2))
                step.mark(nc.gpsimd.tensor_tensor(sst[:, 2:4], sst[:, 0:2], epst[:, :], ALU.add))
                step.wait(pool)
                nc.gpsimd.tensor_tensor(sst[:, 4:6], sst[:, 2:4], mhalf[:, 0:2], ALU.pow).then_inc(yrstd_ready, 1)

            pool.wait_ge(rest_in, 16 * 4)
            pool.wait_ge(wend_ready, 1)
            load_decay(At(0))
            mask(At(0))
            before = step.base.s + step.k
            step.enter(At(before))
            ssd(At(0))
            with pool.Fori(0, (SG - 2) // 2) as it:
                for u in range(2):
                    step.enter(At(before + 1 + u, it, 2))
                    ssd(At(1 + u, it, 2))
            step.enter(At(before + SG - 1))
            ssd(At(SG - 1), last=True)
            norm_stat(3)

        @block.vector
        def _(dve):
            step = Steps(dve_step)
            V = nc.vector

            def low(n):
                dve.wait_ge(high_ready, n.n(1, 1))
                V.tensor_tensor(wlo[:, n.s % HL, :], raw[:, n.s % RAW, :], whi[:, n.s % HL, :].bitcast(F32),
                                ALU.subtract).then_inc(low_ready, 1)

            def norm(q):
                for c in range(TT):
                    dve.wait_ge(rstd_ready, TT * q + c + 1)
                    for h in range(2):
                        half = slice(h * 512, (h + 1) * 512)
                        V.tensor_scalar(xn[:, c, half], x[:, c, half], rstd[:, c:c + 1], float(D) ** 0.5,
                                        ALU.mult, ALU.mult).then_inc(xn_ready, 1)
                for b in range(4):
                    dve.wait_ge(xt_hi, 8 * q + 2 * b + 2)
                    for k in (2 * b, 2 * b + 1):
                        col = (q // 2) * 8 + (q % 2) * 16 + k
                        V.scalar_tensor_tensor(xtl[:, k, :], bank[4 + b][:, (k % 2) * S:(k % 2 + 1) * S],
                                               pcol[:, col:col + 1], xth[:, k, :].bitcast(F32),
                                               ALU.mult, ALU.subtract).then_inc(xt_lo, 1)

            def residual(r, last_piece):
                for c in range(TT):
                    for nh in range(2):
                        i = 2 * c + nh
                        if r:
                            dve.wait_ge(*((piece_used, last_piece + 1) if i == 3 else (y_ps, 3 * r + i)))
                        else:
                            dve.wait_ge(*((piece_used, last_piece + 2 * nh - 1) if c else (y_ps, nh + 1)))
                        V.tensor_tensor(x[:, c, nh * 512:(nh + 1) * 512], x[:, c, nh * 512:(nh + 1) * 512],
                                        bank[i if r else 4 * (1 - nh) + c][:, :], ALU.add).then_inc(x_ready, 1)

            low(At(0))
            dve.wait_ge(params_in, 16)
            norm(0)
            low(At(1))
            for i, (h, l, t) in enumerate(((gwh, gwl, gw), (dwh, dwl, dw))):
                dve.wait_ge(small_hi, i + 1)
                V.tensor_tensor(l[:, :, :], t[:, :, :], h[:, :, :].bitcast(F32), ALU.subtract).then_inc(small_lo, 1)
            low(At(2))
            low(At(3))
            dve.wait_ge(gate_exp, 2)
            step.mark(V.tensor_scalar_add(gx, gx, 1.0))
            step.wait(dve)
            V.reciprocal(gx, gx).then_inc(gate_ready, 1)
            dve.wait_ge(gate_flip, 1)
            V.tensor_copy(gate[:, :, :], view(bank[7][:, 0:1], 0, [[64, 2], [1, NB]])).then_inc(gate_ready, 1)
            low(At(4))
            dve.wait_ge(strip_in, 16)
            for kv in range(2):
                dve.wait_ge(kvt_ps, 2 * kv + 2)
                if kv:
                    dve.wait_ge(blk_hi, 1)
                    dve.wait_ge(blk_lo, 1)
                for g in range(G):
                    for b in range(2):
                        part = slice(b * DH, (b + 1) * DH)
                        i = 4 * kv + g
                        src = view(bank[i // 2][part, 0:1], (i % 2) * S + b, [[2, 16], [CS, NCMP]])
                        dst = view(scratch[part, 0:1], g * NCMP, [[60, 16], [1, NCMP]])
                        pe = view(par[part, C_PE + 16 * kv:C_PE + 1 + 16 * kv], 0, [[1, 16], [0, NCMP]])
                        V.tensor_tensor(dst, src, pe, ALU.add).then_inc(blk_ready, 1)
                if kv:
                    low(At(5))
                dve.wait_ge(blk_hi, kv + 1)
                V.tensor_tensor(blkl[:, kv, :, :], blk, blkh[:, kv, :, :].bitcast(F32), ALU.subtract).then_inc(blk_lo, 1)
            def keys():
                dve.wait_ge(cmp_ps, 1)
                step.mark(V.tensor_copy(kc[:, 0, :], bank[0][0:G * NCMP, 0:DH]))
                step.wait(dve)
                step.mark(V.tensor_tensor(kc[:, 1, :], kc[:, 0, :], kc[:, 0, :], ALU.mult))
                step.wait(dve)
                V.tensor_reduce(kst[:, 0:1], kc[:, 1, :], AX.X, ALU.add).then_inc(kc_sq, 1)
                dve.wait_ge(kc_rstd, 1)
                for b in range(2):
                    V.tensor_scalar(kcn[:, b, :], kc[:, 0, :], kst[:, 2:3], float(DH) ** 0.5,
                                    ALU.mult, ALU.mult).then_inc(kcn_ready, 1)

            def keys_block():
                dve.wait_ge(kct_ps, 1)
                dve.wait_ge(pool_set, 6)
                for b in range(2):
                    part = slice(b * DH, (b + 1) * DH)
                    V.tensor_scalar(kbd[part, :, b, 0:NCMP], view(bank[2][part, 0:1], 0, [[NCMP, G], [1, NCMP]]),
                                    par[part, C_KG:C_KG + 1], None, ALU.mult).then_inc(kbd_ready, 1)

            def qkv_sums(g):
                for c in range(TT):
                    dve.wait_ge(qkv_sq, 2 * g + c + 1)
                    if g:
                        dve.wait_ge(qkv_rstd, 2 * g)
                    V.tensor_reduce(qst[:, 0, 8 * c:8 * c + 6], xn[:, 1, c * 512:c * 512 + 384].rearrange("p (n d) -> p n d", d=DH),
                                    AX.X, ALU.add).then_inc(qkv_ssq, 1)

            def qkv_norm(g):
                for c in range(TT):
                    dve.wait_ge(qkv_rstd, 2 * g + c + 1)
                    if g == 0:
                        dve.wait_ge(pool_set, 6)
                    if g >= 2:
                        dve.wait_ge(pv_done, 4 * (g - 1))
                    for to, of, st in (([0, DH, 4], [0, DH], [0, 1]), ([256, 192, 2], [256, DH], [4, 1]),
                                       ([320, 192, 2], [256, DH], [4, 1]), ([384, 192, 2], [384, DH], [6, 1])):
                        V.scalar_tensor_tensor(view(qkv[:, g % 2, c, 0:1], to[0], [[to[1], to[2]], [1, DH]]),
                                               view(bank[4 + c][:, 0:1], of[0], [[of[1], to[2]], [1, DH]]), float(DH) ** 0.5,
                                               view(qst[:, 2, 8 * c:8 * c + 1], st[0], [[st[1], to[2]], [0, DH]]),
                                               ALU.mult, ALU.mult).then_inc(qkv_ready, 1)

            def key_t(g):
                dve.wait_ge(qkt_ps, 2 * g + 2)
                V.tensor_scalar(kt[:, :, :], bank[5][:, :].rearrange("p (b n) -> p b n", b=2), pcol[:, C_KG:C_KG + 1],
                                None, ALU.mult).then_inc(kt_ready, 1)

            def score_max(g, i):
                h, t, n = i // 2, i % 2, 8 * g + i
                nk = P * (t + 1)
                dve.wait_ge(sc_ps, n + 1)
                if n >= 2:
                    dve.wait_ge(sm_exp, 2 * n - 2)
                for b in range(2):
                    V.tensor_tensor_reduce(out=tsc[:, t, b * S:b * S + nk], in0=bank[t][:, b * nk:(b + 1) * nk],
                                           in1=bias[:, 4 * g + h, P * (1 - t):P * (1 - t) + nk], scale=-1.0,
                                           scalar=3e38, op0=ALU.add, op1=ALU.min,
                                           accum_out=hst[:, t, b:b + 1]).then_inc(sm_max, 1)

            def score_scale(g, i):
                h, t, n = i // 2, i % 2, 8 * g + i
                nk = P * (t + 1)
                dve.wait_ge(sm_exp, 2 * n + 2)
                step.mark(V.reciprocal(hst[:, t, 4:6], hst[:, t, 2:4]))
                step.wait(dve)
                for b in range(2):
                    col = (1 + b) * H + 4 * g + h
                    V.tensor_scalar(probs[:, t, b * S:b * S + nk], probs[:, t, b * S:b * S + nk],
                                    hst[:, t, 4 + b:5 + b], gate[:, 1 - t, col:col + 1],
                                    ALU.mult, ALU.mult).then_inc(p_ready, 1)

            def window_t(m):
                dve.wait_ge(pt_ps, 2 * m + 2)
                if m >= 2:
                    dve.wait_ge(pv_done, m - 1)
                V.tensor_copy(pt[:, m % 2, 1, :], bank[3][:, 0:TW]).then_inc(pt_win, 1)

            def out_low(p):
                dve.wait_ge(ot_hi, p + 1)
                V.tensor_tensor(view(otl[:, p, 0:1], 0, [[P, 2], [1, P]]), in_order(p % 2),
                                view(oth[:, p, 0:1].bitcast(F32), 0, [[P, 2], [1, P]]), ALU.subtract).then_inc(ot_lo, 1)

            tcv = tc[:, :, :, 0:NCMP]

            def over_heads(i):
                return view(cst[:, i, 0:1], 0, [[4, 2], [1, 4], [0, NCMP]])

            def cmp_max(g):
                dve.wait_ge(csc_ps, g + 1)
                src = view(bank[6][:, 0:1], 0, [[64, 2], [16, 4], [1, NCMP]])
                bs = view(bias[:, 4 * g, 0:1], CB - 1, [[P, 2], [TW, 4], [CS, NCMP]])
                step.mark(V.tensor_tensor(tcv, src, bs, ALU.add))
                step.wait(dve)
                step.mark(V.tensor_reduce(cst[:, 0, :], tcv, AX.X, ALU.max))
                step.wait(dve)
                step.mark(V.tensor_scalar_max(cst[:, 1, :], cst[:, 0, :], -1e20))
                step.wait(dve)
                V.tensor_tensor(tcv, tcv, over_heads(1), ALU.subtract).then_inc(csc_ready, 1)

            def cmp_scale(g):
                dve.wait_ge(csc_exp, g + 1)
                step.mark(V.tensor_reduce(cst[:, 0, :], tcv, AX.X, ALU.add))
                step.wait(dve)
                step.mark(V.tensor_scalar_max(cst[:, 2, :], cst[:, 0, :], 1e-30))
                step.wait(dve)
                step.mark(V.reciprocal(cst[:, 3, :], cst[:, 2, :]))
                if g == 0:
                    dve.wait_ge(pool_set, 8)
                step.wait(dve)
                step.mark(V.tensor_tensor(view(cst[:, 2, 0:1], 0, [[4, 2], [1, 4]]), view(cst[:, 3, 0:1], 0, [[4, 2], [1, 4]]),
                                          gate[:, :, 4 * g:4 * g + 4], ALU.mult))
                step.wait(dve)
                if g:
                    dve.wait_ge(pct_ps, g)
                V.tensor_tensor(pc[:, :, :, 0:NCMP], tcv, over_heads(2), ALU.mult).then_inc(pc_ready, 1)

            qkv_sums(0)
            low(At(6))
            qkv_norm(0)
            low(At(7))
            key_t(0)
            low(At(8))
            keys()
            keys_block()
            dve.wait_ge(gate_ready, 2)
            dve.wait_ge(bias_in, 16)
            score_max(0, 0)
            score_max(0, 1)
            low(At(9))
            cmp_max(0)
            for g in range(G):
                for i in range(8):
                    n = 8 * g + i
                    score_scale(g, i)
                    if i == 0:
                        cmp_scale(g)
                    if n and i % 2 == 0:
                        window_t(n // 2 - 1)
                    if n + 2 < 8 * G:
                        score_max((n + 2) // 8, (i + 2) % 8)
                    if n > 1 and i in (1, 5):
                        out_low(2 * g - 1 if i == 1 else 2 * g)
                    if i in (0, 1):
                        low(At(10 + 2 * g + i))
                    if g < G - 1:
                        if i == 2:
                            qkv_sums(g + 1)
                        if i == 4:
                            qkv_norm(g + 1)
                        if i == 5:
                            key_t(g + 1)
                        if i == 6:
                            cmp_max(g + 1)
            window_t(4 * G - 1)
            out_low(2 * G - 1)
            for i in range(2):
                low(At(N_MLP0 + i))
            residual(0, N_WO + 3)

            def mlp(layer, base):
                def square(j, half):
                    dve.wait_ge(relu_ready, j.n(2, 2 * MJ * layer + half + 1))
                    V.scalar_tensor_tensor(rbuf[:, half, :], bank[4 + 2 * (j.s % 2) + half][:, :], 0.0,
                                           rbuf[:, half, :], ALU.max, ALU.mult).then_inc(sq_ready, 1)

                def hid_low(j, half):
                    dve.wait_ge(hid_hi, j.n(2, 2 * MJ * layer + half + 1))
                    V.tensor_tensor(htl[:, j.s % 2, 2 * half:2 * half + 2, :],
                                    rbuf[:, half, :].rearrange("p (m n) -> p m n", m=2),
                                    hth[:, j.s % 2, 2 * half:2 * half + 2, :].bitcast(F32), ALU.subtract).then_inc(hid_lo, 1)

                def body(j, n):
                    low(n + 2)
                    square(j + 1, 0)
                    low(n + 3)
                    hid_low(j + 1, 0)
                    square(j + 1, 1)
                    low(n + 4)
                    hid_low(j + 1, 1)
                    low(n + 5)
                square(At(0), 0)
                low(At(base + 2))
                hid_low(At(0), 0)
                square(At(0), 1)
                low(At(base + 3))
                hid_low(At(0), 1)
                body(At(0), At(base + 2))
                with dve.Fori(0, (MJ - 2) // 2) as it:
                    for u in range(2):
                        body(At(1 + u, it, 2), At(base + 6 + 4 * u, it, 8))
                if layer == 0:
                    low(At(base + 4 * MJ))
                    low(At(base + 4 * MJ + 1))

            norm(1)
            mlp(0, N_MLP0)
            residual(1, N_SSD - 1)

            norm(2)
            low(At(N_SSD + 2))
            V.memset(xb[:, :, 0:3], 0.0).then_inc(dve_step, 1)
            step.k += 1
            dve.wait_ge(rest_in, 16 * 4)
            dve.wait_ge(dt_ps, 1)
            step.mark(V.tensor_tensor(dta[:, :, :], bank[6][:, 0:2 * SH].rearrange("p (c h) -> p c h", c=2),
                                      view(dtb[:, 0:1], 0, [[0, 2], [1, SH]]), ALU.add))
            step.wait(dve)
            step.mark(V.tensor_scalar_mul(dtt[:, 1, :, :], dta[:, :, :], -1.0))
            step.wait(dve)
            V.tensor_tensor(dtt[:, 0, :, :], dta[:, :, :], dtt[:, 1, :, :], ALU.min).then_inc(dt_neg, 1)
            dve.wait_ge(dt_exp, 2)
            V.tensor_scalar_add(dtt[:, 2, :, :], dtt[:, 1, :, :], 1.0).then_inc(dt_one, 1)
            dve.wait_ge(dt_one, 1)
            step.mark(V.tensor_scalar(dtt[:, 0, :, :], dtt[:, 2, :, :], -1.0, 1e-30, ALU.add, ALU.add))
            step.wait(dve)
            step.mark(V.reciprocal(dtt[:, 0, :, :], dtt[:, 0, :, :]))
            step.wait(dve)
            dve.wait_ge(dt_ln, 1)
            step.mark(V.scalar_tensor_tensor(dtt[:, 3, :, :], dtt[:, 3, :, :], 1e-30, dtt[:, 0, :, :], ALU.add, ALU.mult))
            step.wait(dve)
            step.mark(V.tensor_tensor(dtt[:, 3, :, :], dtt[:, 3, :, :], dtt[:, 1, :, :], ALU.mult))
            step.wait(dve)
            step.mark(V.scalar_tensor_tensor(dt[:, :, :], dta[:, :, :], 0.0, dtt[:, 3, :, :], ALU.max, ALU.add))
            step.wait(dve)
            V.scalar_tensor_tensor(dta[:, :, :], dt[:, :, :], -1.0, view(ealog[:, 0:1], 0, [[0, 2], [1, SH]]),
                                   ALU.mult, ALU.mult).then_inc(dt_ready, 1)
            dve.wait_ge(acs_ps, 1)
            V.tensor_copy(acs[:, :, :], bank[6][:, 64:128].rearrange("p (c h) -> p c h", c=2)).then_inc(acs_ready, 1)
            dve.wait_ge(acs_ready, 1)
            step.mark(V.tensor_scalar_mul(nacs[:, :, :], acs[:, :, :], -1.0))
            V.tensor_tensor(dtt[:, 0, 0, :], bank[6][:, 128:160], acs[:, 0, :], ALU.subtract).then_inc(acs_ready, 1)
            dve.wait_ge(decay_ready, 2)
            V.tensor_tensor(wend[:, :], wend[:, :], dt[:, 0, :], ALU.mult).then_inc(wend_ready, 1)

            def conv(g, i):
                dve.wait_ge(conv_in, g.n(2, i + 1))
                if g.s:
                    dve.wait_ge(xc_ready, g.n(2, i - 1))

                def col(q, tap):
                    first = (C_CB if tap == 4 else tap * 32) + (q if q < 2 else 16 + 8 * (q - 2))
                    t = pcol if tap == 4 else ccol
                    return t[:, bass.ds(g.n(2 if q < 2 else 1, first), 1)]
                for tap in (3, 0, 1, 2):
                    for q in (2 * i, 2 * i + 1):
                        if tap != 3:
                            step.wait(dve, step.k - 1)
                        if tap == 3:
                            ins = V.tensor_scalar(cacc[:, q, :], xb[:, q, 3:3 + S], col(q, 3), col(q, 4), ALU.mult, ALU.add)
                        else:
                            ins = V.scalar_tensor_tensor(cacc[:, q, :], xb[:, q, tap:tap + S], col(q, tap), cacc[:, q, :],
                                                         ALU.mult, ALU.add)
                        if tap == 2 and q % 2:
                            ins.then_inc(conv_done, 1)
                        else:
                            step.mark(ins)

            step.wait(dve)
            conv(At(0), 0)
            conv(At(0), 1)
            low(At(N_SSD + 3))

            def ssd(g, n, last=False):
                dve.wait_ge(t_ps, g.n(2, 1))
                if g.s:
                    dve.wait_ge(ys_ps, g.n())
                    dve.wait_ge(sk_ready, g.n(2))
                V.tensor_copy(xsn[:, :, :], bank[7][:, :].rearrange("p (c n) -> p c n", c=2)).then_inc(xsn_ready, 1)
                dve.wait_ge(bn_ready, g.n(1, 1))
                for i in range(8):
                    c, h = i // 4, i % 4
                    dve.wait_ge(e_ready, g.n(8, i + 1))
                    V.scalar_tensor_tensor(eb[:, c, h, :], eb[:, c, h, :], dt[:, c, bass.ds(g.n(4, h), 1)],
                                           bank[6][:, c * P:(c + 1) * P], ALU.mult, ALU.mult).then_inc(m_ready, 1)
                if not last:
                    low(n + 1)
                    low(n + 2)
                dve.wait_ge(ys_ps, g.n(1, 1))
                dve.wait_ge(sk_ready, g.n(2, 2))
                if g.s:
                    dve.wait_ge(yt_ps, g.n())
                step.mark(V.tensor_tensor(y[:, 1, :].rearrange("p (h d) -> p h d", h=4),
                                          bank[7][:, S:2 * S].rearrange("p (h d) -> p h d", h=4),
                                          view(eacs[:, bass.ds(g.n(4), 4)], 0, [[1, 4], [0, DH]]), ALU.mult))
                step.mark(V.tensor_tensor(y[:, 0, :], bank[6][:, 0:S], sk[:, 0, :], ALU.add))
                step.wait(dve, step.k - 1)
                step.mark(V.tensor_tensor(y[:, 1, :], y[:, 1, :], sk[:, 1, :], ALU.add))
                step.wait(dve)
                step.mark(V.tensor_tensor(y[:, 1, :], bank[6][:, S:2 * S], y[:, 1, :], ALU.add))
                step.wait(dve)
                dve.wait_ge(z_ready, g.n(1, 1))
                V.tensor_tensor(y[:, :, :].rearrange("p c n -> p (c n)"), y[:, :, :].rearrange("p c n -> p (c n)"),
                                sz[:, :], ALU.mult).then_inc(y_ready, 1)
                if not last:
                    conv(g + 1, 0)
                dve.wait_ge(yrstd_ready, g.n(1, 1))
                for c in range(TT):
                    V.tensor_scalar(y[:, c, :], y[:, c, :], sst[:, 4 + c:5 + c], 16.0, ALU.mult, ALU.mult).then_inc(yn_ready, 1)
                if not last:
                    low(n + 3)
                dve.wait_ge(yt_hi, g.n(2, 2))
                for q in range(2):
                    V.scalar_tensor_tensor(ytl[:, q, :], bank[7][:, q * S:(q + 1) * S],
                                           pcol[:, bass.ds(g.n(2, C_SSDN + q), 1)], yth[:, q, :].bitcast(F32),
                                           ALU.mult, ALU.subtract).then_inc(yt_lo, 1)
                if not last:
                    conv(g + 1, 1)
                    low(n + 4)

            per = 2 * 7 + 4
            before = step.base.s + step.k
            step.enter(At(before))
            ssd(At(0), At(N_SSD + 3))
            assert step.k == per
            with dve.Fori(0, (SG - 2) // 2) as it:
                for u in range(2):
                    step.enter(At(before + per * (1 + u), it, 2 * per))
                    ssd(At(1 + u, it, 2), At(N_SSD + 7 + 4 * u, it, 8))
            step.enter(At(before + per * (SG - 1)))
            low(At(N_MLP1))
            low(At(N_MLP1 + 1))
            ssd(At(SG - 1), None, last=True)
            residual(2, N_MLP1 - 1)

            norm(3)
            mlp(1, N_MLP1)
            residual(3, N_END - 1)

        @block.tensor
        def _(pe):
            T = nc.tensor

            def mm3(out, st, mv, start, stop):
                T.matmul(out, st[0], mv[0], start=start, stop=False)
                T.matmul(out, st[0], mv[1], start=False, stop=False)
                return T.matmul(out, st[1], mv[0], start=False, stop=stop)

            def ready(n):
                pe.wait_ge(low_ready, n.n(1, 1))

            def w(n, a_, b_, width):
                lo, hi = a_ * width + b_.start, a_ * width + b_.stop
                return whi[:, n.s % HL, lo:hi], wlo[:, n.s % HL, lo:hi]

            def xt(k, c):
                return xth[:, k, c * P:(c + 1) * P], xtl[:, k, c * P:(c + 1) * P]

            def xt_all(k):
                return xth[:, k, :], xtl[:, k, :]

            def wide(n, first, banks, q=None, part=range(4)):
                if 0 in part:
                    ready(n)
                for k in part:
                    if q is not None:
                        pe.wait_ge(xt_lo, 8 * q + first + k + 1)
                    for c in range(TT):
                        last = mm3(banks[c][:, :], xt(first + k, c), w(n, k, slice(0, 512), 512),
                                   first + k == 0, first + k == KD - 1)
                if 3 in part:
                    last.then_inc(piece_used, 1)

            def attention_out(nh, half, part=range(4)):
                n = At(N_WO + 2 * nh + half)
                pe.wait_ge(ot_lo, 4 * half + 4)
                if 0 in part:
                    ready(n)
                for c, k in [(c, k) for c in range(TT) for k in part] if half else [(c, k) for k in part for c in range(TT)]:
                    kk = 4 * half + k
                    last = mm3(bank[4 * (1 - nh) + c][:, :], (oth[:, kk, c * P:(c + 1) * P], otl[:, kk, c * P:(c + 1) * P]),
                               w(n, k, slice(0, 512), 512), kk == 0, kk == KD - 1)
                    if kk == KD - 1 and c == 0:
                        last.then_inc(y_ps, 1)
                if 3 in part:
                    last.then_inc(piece_used, 1)

            def qk_transposes(g):
                pe.wait_ge(qkv_ready, 8 * g + 8)
                for pr in range(2):
                    for c in range(TT):
                        o = pr * S + c * P
                        last = T.transpose(bank[4][:, o:o + P], qkv[:, g % 2, c, pr * P:(pr + 1) * P], ident)
                last.then_inc(qkt_ps, 1)
                for s in range(2):
                    for c in range(TT):
                        o = s * S + c * P
                        last = T.transpose(bank[5][:, o:o + P], qkv[:, g % 2, c, 256 + 192 * s:384 + 192 * s], ident)
                last.then_inc(qkt_ps, 1)

            def compressed_scores(g):
                pe.wait_ge(qt_ready, g + 1)
                pe.wait_ge(kbd_ready, 2)
                pe.wait_ge(*((pct_ready, g) if g else (hid_ready, 3)))
                for c in range(TT):
                    for pr in range(2):
                        o = (1 - c) * 64 + pr * 32
                        last = T.matmul(bank[6][:, o:o + 32], qt[:, pr * S + c * P:pr * S + (c + 1) * P], kbd[:, g, :, :],
                                        start=True, stop=True)
                last.then_inc(csc_ps, 1)

            def features(n, out, q=None):
                ready(n)
                for m in range(2):
                    for k in range(KD):
                        if q is not None and m == 0:
                            pe.wait_ge(xt_lo, 8 * q + k + 1)
                        last = mm3(out[:, m * S:(m + 1) * S], w(n, k, slice(m * P, (m + 1) * P), 256), xt_all(k),
                                   k == 0, k == KD - 1)
                last.then_inc(piece_used, 1)

            def back(n, st, start, stop):
                ready(n)
                if stop:
                    order = [(m, c, nh) for c in range(TT) for nh in range(2) for m in range(2)]
                else:
                    order = [(m, c, nh) for m in range(2) for c in range(TT) for nh in range(2)]
                for m, c, nh in order:
                    h, l = st(m)
                    last = mm3(bank[2 * c + nh][:, :], (h[:, c * P:(c + 1) * P], l[:, c * P:(c + 1) * P]),
                               w(n, m, slice(nh * 512, (nh + 1) * 512), 1024), start and m == 0, stop and m == 1)
                    if stop and m == 1 and (c, nh) != (1, 1):
                        last.then_inc(y_ps, 1)
                last.then_inc(piece_used, 1)

            def norm_t(q):
                for c in range(TT):
                    for b in range(4):
                        pe.wait_ge(xn_ready, 4 * q + 2 * c + b // 2 + 1)
                        for k in (2 * b, 2 * b + 1):
                            o = (k % 2) * S + c * P
                            last = T.transpose(bank[4 + b][:, o:o + P], xn[:, c, k * P:(k + 1) * P], ident)
                        if c == TT - 1:
                            last.then_inc(xt_ps, 1)

            pe.wait_ge(params_in, 16)
            pe.wait_ge(rows_in, 16 * 2)
            pe.wait_ge(pool_set, 6)
            T.matmul(bank[2][0:H, :], table[:, :], onehot, start=True, stop=True).then_inc(strip_ps, 1)

            norm_t(0)
            for i in range(2):
                if i == 0:
                    pe.wait_ge(xt_lo, 4)
                wide(At(N_KVC + i), 4 * i, (bank[4], bank[5]), 0)
            pe.wait_ge(small_lo, 2)
            for c in range(TT):
                for k in range(KD):
                    last = mm3(bank[6][:, c * 64:c * 64 + NB], xt(k, c), (gwh[:, k, :], gwl[:, k, :]), k == 0, k == KD - 1)
            last.then_inc(gate_ps, 1)
            pe.wait_ge(kvc_ready, 2)
            pe.wait_ge(strip_ready, 1)
            for i in range(8):
                for c in range(TT):
                    o = (i % 2) * S + c * P
                    last = T.transpose(bank[i // 2][:, o:o + P], xn[:, c, i * P:(i + 1) * P], ident)
                if i % 2:
                    last.then_inc(kvt_ps, 1)
            for i in range(2):
                wide(At(N_ATT[0] + i), 4 * i, (bank[4], bank[5]))
            pe.wait_ge(gate_ready, 1)
            for c in range(TT):
                last = T.matmul(bank[7][:, (1 - c) * 64:(1 - c) * 64 + NB], flip, view(gx, c * NB, [[1, NB]]), start=True, stop=True)
            last.then_inc(gate_flip, 1)

            def hidden_t(kv):
                pe.wait_ge(silu_ready, kv + 1)
                for m in range(2):
                    last = T.transpose(bank[6 + kv][:, 256 + 64 * m:256 + 64 * m + G * NCMP], hid[:, kv, m * P:(m + 1) * P],
                                       par[0:G * NCMP, NPCOL + 128:NPCOL + 128 + G * NCMP])
                last.then_inc(hid_ps, 1)

            for kv in range(2):
                pe.wait_ge(blk_lo, kv + 1)
                if kv:
                    pe.wait_ge(gate_ready, 2)
                for i in range(2):
                    n = At(N_W1 + 2 * kv + i)
                    ready(n)
                    for j in range(8):
                        jj = 8 * i + j
                        last = mm3(bank[6 + kv][0:G * NCMP, 0:HID], (blkh[:, kv, jj, :], blkl[:, kv, jj, :]),
                                   w(n, j, slice(0, HID), HID), jj == 0, jj == 15)
                    last.then_inc(piece_used, 1)
                    if kv and i == 0:
                        hidden_t(0)
                if kv == 0:
                    qk_transposes(0)
            pe.wait_ge(blk_ready, 16)
            pe.wait_ge(hid_ready, 1)
            pe.wait_ge(rest_in, 16 * 4)
            for m in range(2):
                last = T.matmul(bank[0][0:G * NCMP, 0:DH], hidk[:, m, :], w2[:, 0, m, :], start=m == 0, stop=m == 1)
            last.then_inc(cmp_ps, 1)
            hidden_t(1)
            pe.wait_ge(kt_ready, 1)
            pe.wait_ge(qt_ready, 1)
            wide(At(N_ATT[1]), 0, (bank[4], bank[5]), part=range(2))
            pe.wait_ge(hid_ready, 3)
            for g in range(G):
                for m in range(2):
                    last = T.matmul(bank[1][:, g * DH:(g + 1) * DH], hidv[:, m, g, :], w2[:, 1, m, :], start=m == 0, stop=m == 1)
            last.then_inc(cmp_ps, 1)
            pe.wait_ge(kcn_ready, 2)
            T.transpose(bank[2][:, 0:G * NCMP], kcn.rearrange("p b d -> p (b d)"),
                        par[0:G * NCMP, NPCOL + 128:NPCOL + 128 + G * NCMP]).then_inc(kct_ps, 1)

            def scores(g, i):
                h, t, n = i // 2, i % 2, 8 * g + i
                nk = P * (t + 1)
                if n >= 2:
                    pe.wait_ge(sm_max, 2 * n - 2)
                pr, b = h // 2, h % 2
                part = slice(b * DH, (b + 1) * DH)
                T.matmul(bank[t][:, 0:2 * nk], qt[part, pr * S + t * P:pr * S + (t + 1) * P], kt[part, :, 0:nk],
                         start=True, stop=True).then_inc(sc_ps, 1)

            def probs_t(g, i):
                h, t, n = i // 2, i % 2, 8 * g + i
                m = 4 * g + h
                pe.wait_ge(p_ready, 2 * n + 2)
                if t == 0 and m:
                    pe.wait_ge(pt_sel, m)
                    pe.wait_ge(pt_win, m)
                for b in range(2):
                    for kk in range(t + 1):
                        o = (t + kk) * P
                        last = T.transpose(bank[2 + b][:, o:o + P], probs[:, t, b * S + kk * P:b * S + (kk + 1) * P], ident)
                last.then_inc(pt_ps, 1)

            def values(m):
                g, h = m // 4, m % 4
                pr, b = h // 2, h % 2
                pe.wait_ge(pt_sel, m + 1)
                pe.wait_ge(pt_win, m + 1)
                if h == 0:
                    pe.wait_ge(pct_ready, g + 1)
                if m >= 2 and h % 2 == 0:
                    pe.wait_ge(ot_lo, m // 2)
                out = bank[7][b * DH:(b + 1) * DH, pr * S:(pr + 1) * S]
                for s in range(2):
                    v = 384 + 192 * s
                    T.matmul(out, qkv[:, g % 2, 0, v:v + DH], pt[:, m % 2, s, 0:S], start=s == 0, stop=False)
                    T.matmul(out[:, P:S], qkv[:, g % 2, 1, v:v + DH], pt[:, m % 2, s, S:TW], start=False, stop=False)
                T.matmul(out, vcmp[32 * h:32 * h + 32, g, :], pct[32 * h:32 * h + 32, :], start=False, stop=True).then_inc(pv_done, 1)

            pe.wait_ge(kt_ready, 1)
            pe.wait_ge(qt_ready, 1)
            pe.wait_ge(vcmp_ready, 1)
            scores(0, 0)
            scores(0, 1)
            compressed_scores(0)
            for g in range(G):
                for i in range(8):
                    n = 8 * g + i
                    if i in (0, 1):
                        for h, part in (((0, (2, 3)), (1, (0,))), ((1, (1, 2, 3)),))[i]:
                            if g < G - 1:
                                wide(At(N_ATT[g + 1] + h), 4 * h, (bank[4], bank[5]), part=part)
                            elif h == 0:
                                attention_out(0, 0, part)
                    if i == 7 and g < G - 1:
                        pe.wait_ge(kt_ready, g + 2)
                        pe.wait_ge(qt_ready, g + 2)
                        if g < G - 2:
                            wide(At(N_ATT[g + 2]), 0, (bank[4], bank[5]), part=(0, 1))
                        else:
                            attention_out(0, 0, (0, 1))
                    if n + 2 < 8 * G:
                        if i == 6:
                            pe.wait_ge(kt_ready, g + 2)
                            pe.wait_ge(qt_ready, g + 2)
                        scores((n + 2) // 8, (i + 2) % 8)
                    if i == 5 and g < G - 1:
                        qk_transposes(g + 1)
                    if i == 6 and g < G - 1:
                        compressed_scores(g + 1)
                    if i == 0:
                        pe.wait_ge(pc_ready, g + 1)
                        for c in range(TT):
                            last = T.transpose(bank[6][:, S + c * P:S + (c + 1) * P],
                                               pc[:, 1 - c, :, :].rearrange("p h n -> p (h n)"), ident)
                        last.then_inc(pct_ps, 1)
                    probs_t(g, i)
                    if n and i % 2 == 0:
                        values(n // 2 - 1)
            values(4 * G - 1)
            pe.wait_ge(ot_lo, 2 * G)
            attention_out(0, 1)
            attention_out(1, 0)
            attention_out(1, 1)

            def mlp(layer, base):
                def up(j, n, half, q=None):
                    if layer or j.s >= 2:
                        pe.wait_ge(sq_ready, j.n(2, 2 * MJ * layer + half - 3))
                    features(n + half, bank[4 + 2 * (j.s % 2) + half], q)

                def down(j, n, start=False, stop=False):
                    for half in range(2):
                        pe.wait_ge(hid_lo, j.n(2, 2 * MJ * layer + half + 1))
                        back(n + half, lambda m, half=half: (hth[:, j.s % 2, 2 * half + m, :], htl[:, j.s % 2, 2 * half + m, :]),
                             start and half == 0, stop and half == 1)
                pe.wait_ge(xt_lo, 16 * layer + 8 + 2)
                for half in range(2):
                    if half:
                        pe.wait_ge(xt_lo, 16 * layer + 8 + 8)
                    up(At(0), At(base), half, None if half else 2 * layer + 1)
                for half in range(2):
                    up(At(1), At(base + 2), half)
                down(At(0), At(base + 4), start=True)
                with pe.Fori(0, (MJ - 2) // 2) as it:
                    for u in range(2):
                        j, n = At(1 + u, it, 2), At(base + 6 + 4 * u, it, 8)
                        for half in range(2):
                            up(j + 1, n, half)
                        down(j, n + 2)
                down(At(MJ - 1), At(base + 4 * MJ - 2), stop=True)

            norm_t(1)
            mlp(0, N_MLP0)

            norm_t(2)
            pe.wait_ge(xt_lo, 16 + 2)
            features(At(N_SSD), bank[4], 2)
            for c in range(TT):
                for k in range(KD):
                    last = mm3(bank[6][:, c * SH:(c + 1) * SH], xt(k, c), (dwh[:, k, :], dwl[:, k, :]), k == 0, k == KD - 1)
            last.then_inc(dt_ps, 1)
            features(At(N_SSD + 1), bank[5])
            pe.wait_ge(dt_ready, 1)
            for c in range(TT):
                T.matmul(bank[6][:, 64 + c * SH:64 + (c + 1) * SH], tri, dta[:, c, :], start=True, stop=True)
            T.matmul(bank[6][:, 128:160], ones[:, :], dta[:, 0, :], start=True, stop=True).then_inc(acs_ps, 1)
            pe.wait_ge(acs_ready, 1)
            for c in range(TT):
                last = T.transpose(bank[7][0:SH, c * P:(c + 1) * P], acs[:, c, :], ident)
            last.then_inc(acst_ps, 1)
            pe.wait_ge(acs_ready, 2)

            def gate_cols(n):
                ready(n)
                for c in range(TT):
                    for k in range(KD):
                        last = mm3(bank[6][:, c * S:(c + 1) * S], xt(k, c), w(n, k, slice(0, 256), 256), k == 0, k == KD - 1)
                last.then_inc(piece_used, 1)
            gate_cols(At(N_SSD + 2))

            def ssd_back(g, n, start=False, stop=False):
                pe.wait_ge(yt_lo, g.n(2, 2))
                back(n, lambda m: (yth[:, m, :], ytl[:, m, :]), start, stop)

            def ssd(g, n, last_group=False):
                par = g.s % 2
                pe.wait_ge(xc_ready, g.n(2, 1))
                if g.s == 0:
                    pe.wait_ge(acst_ready, 1)
                else:
                    pe.wait_ge(yt_lo, g.n(2))
                for c in range(TT):
                    for q in range(2):
                        last = T.transpose(bank[7][:, c * S + q * P:c * S + (q + 1) * P], xc[:, par, q, c * P:(c + 1) * P], ident)
                last.then_inc(t_ps, 1)
                if g.s:
                    ssd_back(g + (-1), At(N_MLP1 - 2) if last_group else n + (-1), start=g.s == 1 and g.it is None)
                pe.wait_ge(xc_ready, g.n(2, 2))
                pe.wait_ge(z_ready, g.n(1, 1))
                T.transpose(bank[6][:, 2 * P:3 * P], xc[:, par, 2, 0:P], ident)
                for c in range(TT):
                    last = T.matmul(bank[6][:, c * P:(c + 1) * P], xc[:, par, 2, c * P:(c + 1) * P],
                                    xc[:, par, 3, c * P:(c + 1) * P], start=True, stop=True)
                last.then_inc(t_ps, 1)
                if not last_group:
                    pe.wait_ge(conv_in, g.n(2, 1))
                    features(n, bank[4])
                pe.wait_ge(xw_ready, g.n(1, 1))
                pe.wait_ge(bn_ready, g.n(1, 1))
                T.matmul(bank[7][:, 0:S], bn[:, :], xw[:, :], start=True, stop=True).then_inc(s_ps, 1)
                pe.wait_ge(m_ready, g.n(8, 8))
                for c in range(TT):
                    for h in range(4):
                        o = c * S + h * DH
                        T.matmul(bank[6][:, o:o + DH], eb[:, c, h, :], xsn[:, c, h * DH:(h + 1) * DH], start=True, stop=True)
                pe.wait_ge(prev_ready, g.n(1, 1))
                T.matmul(bank[7][:, S:2 * S], xc[:, par, 3, P:2 * P], prev[:, :], start=True, stop=True).then_inc(ys_ps, 1)
                if not last_group:
                    pe.wait_ge(conv_in, g.n(2, 2))
                    features(n + 1, bank[5])
                pe.wait_ge(yn_ready, g.n(2, 2))
                for q in range(2):
                    for c in range(TT):
                        last = T.transpose(bank[7][:, q * S + c * P:q * S + (c + 1) * P], y[:, c, q * P:(q + 1) * P], ident)
                last.then_inc(yt_ps, 1)
                if not last_group:
                    gate_cols(n + 2)

            ssd(At(0), At(N_SSD + 3))
            ssd(At(1), At(N_SSD + 7))
            with pe.Fori(0, (SG - 4) // 2) as it:
                for u in range(2):
                    ssd(At(2 + u, it, 2), At(N_SSD + 11 + 4 * u, it, 8))
            ssd(At(SG - 2), At(N_SSD + 7 + 4 * (SG - 3)))
            ssd(At(SG - 1), None, last_group=True)
            ssd_back(At(SG - 1), At(N_MLP1 - 1), stop=True)

            norm_t(3)
            mlp(1, N_MLP1)


def constants():
    tri = np.triu(np.ones((P, P), np.float32))
    dist = 255 - np.arange(512)
    far = BUCKETS // 2 + (np.log(np.maximum(dist, 1) / (BUCKETS // 2)) / np.log(128 / (BUCKETS // 2))
                          * (BUCKETS - BUCKETS // 2)).astype(np.int64)
    bucket = np.where(dist < BUCKETS // 2, np.maximum(dist, 0), np.minimum(far, BUCKETS - 1))
    bucket[dist < 0] = BUCKETS
    onehot = np.zeros((BUCKETS + 1, 512), np.float32)
    onehot[bucket, np.arange(512)] = 1.0
    return np.eye(P, dtype=np.float32), tri, np.where(tri > 0, 0.0, NEG).astype(np.float32), onehot


def tiles(w):
    return w.reshape(-1, P, w.shape[1]).transpose(1, 0, 2).reshape(P, -1)


def stream(t):
    out = []
    w = t["nsa_w_in"][0]
    for k in range(2):
        out.append(tiles(w[k * 512:(k + 1) * 512, QC:QC + 512]))
    for g in range(G):
        starts = [g * 256] + [QC + 512 + b * 256 + g * DH for b in (0, 2, 1, 3)]
        cols = np.concatenate([w[:, c:c + n] for c, n in zip(starts, (256, DH, DH, DH, DH))], axis=1)
        out += [tiles(cols[:512]), tiles(cols[512:])]
        if g == 0:
            for name in ("cmp_w1_k", "cmp_w1_v"):
                w1 = t[name][0].reshape(CB * DH, HID)
                out += [tiles(w1[:1024]), tiles(w1[1024:])]
    wo = t["nsa_w_out"][0]
    out += [tiles(wo[k * 512:(k + 1) * 512, n * 512:(n + 1) * 512]) for n in range(2) for k in range(2)]

    def mlp(layer):
        up, down = t["mlp_w_up"][layer], t["mlp_w_down"][layer]
        ups = [tiles(up[:, i * 256:(i + 1) * 256]) for i in range(2 * MJ)]
        downs = [tiles(down[i * 256:(i + 1) * 256]) for i in range(2 * MJ)]
        seq = ups[:2]
        for j in range(MJ):
            seq += ups[2 * j + 2:2 * j + 4] + downs[2 * j:2 * j + 2]
        return seq

    out += mlp(0)
    w, back = t["ssd_w_in"][0], t["ssd_w_out"][0]
    for g in range(SG + 1):
        if g >= 2:
            out.append(tiles(back[(g - 2) * 256:(g - 1) * 256]))
        if g < SG:
            b0 = XBC0 + DI + g * 128
            bc = np.concatenate([w[:, b0:b0 + 128], w[:, b0 + SG * 128:b0 + SG * 128 + 128]], axis=1)
            out += [tiles(w[:, XBC0 + g * 256:XBC0 + (g + 1) * 256]), tiles(bc), tiles(w[:, g * 256:(g + 1) * 256])]
    out.append(tiles(back[(SG - 1) * 256:]))
    out += mlp(1)
    return np.stack(out)


def kernel(**inputs):
    import concourse.bacc as bacc
    from concourse.bass_utils import run_bass_kernel_spmd

    t = {name: np.asarray(v) for name, v in inputs.items()}
    eye, tri, segmask, onehot = constants()

    def cols(v):
        return v.reshape(-1, P).T

    params = np.concatenate(
        [cols(t["norm_mix_w"]), cols(t["norm_mlp_w"]), cols(t["ssd_norm_w"]), cols(t["ssd_conv_b"]),
         cols(t["cmp_pe_k"]), cols(t["cmp_pe_v"]), cols(np.concatenate([t["nsa_q_gain"]] * 2)),
         cols(np.concatenate([t["nsa_k_gain"]] * 2)), cols(t["ssd_conv_w"]), eye, tri, segmask], axis=1)
    small_w = np.concatenate(
        [tiles(t["cmp_w2_k"][0]), tiles(t["cmp_w2_v"][0]), tiles(t["ssd_w_in"][0][:, DT0:DT0 + SH]),
         tiles(t["nsa_w_in"][0][:, GATE0:GATE0 + NB]), eye[::-1]], axis=1)
    given = {"x": t["x"], "stream": stream(t), "params": params, "small_w": small_w, "rel_table": t["rel_table"],
             "onehot": onehot, "ssd_dt_bias": t["ssd_dt_bias"], "ssd_a_log": t["ssd_a_log"], "ssd_d": t["ssd_d"]}

    nc = bacc.Bacc("TRN2", target_bir_lowering=False, num_devices=1)
    arrays, aps = {}, {}
    for name, v in given.items():
        arrays[f"in_{name}"] = np.ascontiguousarray(v)
        aps[name] = nc.dram_tensor(f"in_{name}", v.shape, mybir.dt.from_np(v.dtype), kind="ExternalInput").ap()
    aps["out"] = nc.dram_tensor("out", (1, S, D), F32, kind="ExternalOutput").ap()
    build(nc, aps)
    r = run_bass_kernel_spmd(nc, [arrays], core_ids=[0])
    return r.results[0]["out"]
```

```python
from contextlib import ExitStack

import concourse.bass as bass
import concourse.mybir as mybir
import numpy as np

F32 = mybir.dt.float32
F32R = mybir.dt.float32r
ACT = mybir.ActivationFunctionType
ALU = mybir.AluOpType
AX = mybir.AxisListType

P = 128
S = 256
D = 1024
TT = S // P
KD = D // P
H = 16
G = 4
DH = 64
QKV = 640
NCMP = 15
CB, CS = 32, 16
HID = 256
QC = 1024
GATE0 = QC + 6 * 256
NB = 3 * H
DI = 2048
SG = 8
SH = 32
XBC0 = DI
DT0 = DI + DI + 2 * SG * 128
MH = 4096
MJ = MH // 512
EPS = 1e-6
NEG = -1e30
TW = 384
BUCKETS = 32
FILL = {0: (1, 2), 1: (3, 4), 2: (5, 6), 3: (7,)}

PW = 2048
RAW = 4
HL = 4
PER = 16

N_KVC = 0
N_ATT = (2, 8, 10, 12)
N_W1 = 4
N_WO = 14
N_MLP0 = N_WO + 4
N_SSD = N_MLP0 + 4 * MJ
N_MLP1 = N_SSD + 4 * SG
N_END = N_MLP1 + 4 * MJ

C_MIX, C_MLP, C_SSDN, C_CB, C_PE, C_QG, C_KG = 0, 16, 32, 48, 80, 112, 113
NPCOL = 114
PAR_W = NPCOL + 128 + 3 * P
W2_0, DW_0, GW_0 = 0, 256, 512


class At:

    def __init__(self, s, it=None, step=0):
        self.s, self.it, self.step = s, it, step

    def __add__(self, k):
        return At(self.s + k, self.it, self.step)

    def n(self, mult=1, add=0):
        if self.it is None:
            return self.s * mult + add
        return self.it * (self.step * mult) + (self.s * mult + add)


class Steps:

    def __init__(self, sem):
        self.sem, self.base, self.k = sem, At(0), 0

    def enter(self, base):
        self.base, self.k = base, 0

    def mark(self, ins):
        ins.then_inc(self.sem, 1)
        self.k += 1
        return self.k

    def wait(self, eng, k=None):
        eng.wait_ge(self.sem, self.base.n(1, self.k if k is None else k))


def raw_round(n):
    v = PER * (n.s // RAW + 1)
    return v if n.it is None else n.it * (PER * n.step // RAW) + v


def view(ap, off, dims):
    return bass.AP(ap.tensor, ap.offset + off, [list(ap.ap[0])] + dims)


def rows(t, off, dims):
    return bass.AP(t.tensor, off, dims)


def build(nc, a):
    ctx = ExitStack()
    with ctx:
        def sb(name, shape, dt=F32, stack=ctx):
            return stack.enter_context(nc.sbuf_tensor(name, shape, dt))

        def sem(name):
            return ctx.enter_context(nc.semaphore(name))

        bank = [ctx.enter_context(nc.psum_tensor(f"bank{i}", [P, 512], F32)) for i in range(8)]
        strip_dram = nc.dram_tensor("strip_dram", (H, 512), F32, kind="Internal").ap()
        acs_dram = nc.dram_tensor("acs_dram", (SH, S), F32, kind="Internal").ap()

        raw = sb("raw", [P, RAW, PW])
        whi = sb("whi", [P, HL, PW], F32R)
        wlo = sb("wlo", [P, HL, PW], F32R)
        x = sb("x", [P, TT, D])
        xn = sb("xn", [P, TT, D])
        xth = sb("xth", [P, KD, S], F32R)
        xtl = sb("xtl", [P, KD, S], F32R)
        hth = sb("hth", [P, 2, 4, S], F32R)
        htl = sb("htl", [P, 2, 4, S], F32R)
        rbuf = sb("rbuf", [P, 2, 512])
        par = sb("par", [P, PAR_W])
        ones = sb("ones", [P, P])
        pcol, ccol = par[:, 0:NPCOL], par[:, NPCOL:NPCOL + 128]
        ident, tri, segmask = (par[:, NPCOL + 128 + i * P:NPCOL + 128 + (i + 1) * P] for i in range(3))
        table = sb("table", [BUCKETS + 1, H])
        small = sb("small", [P, 80])
        mhalf = sb("mhalf", [P, 16])
        epst = sb("epst", [P, 2])
        gq = sb("gq", [P, 1])
        dwh = sb("dwh", [P, KD, SH], F32R)
        dwl = sb("dwl", [P, KD, SH], F32R)
        w2 = sb("w2", [P, 2, 2, DH])
        gate = sb("gate", [P, TT, NB])
        dtb = sb("dtb", [P, SH])
        alog = sb("alog", [P, SH])
        dskip = sb("dskip", [P, SH])

        ssq = small[:, 0:4].rearrange("p (c h) -> p c h", c=TT)
        vsum, rstd = small[:, 4:6], small[:, 6:8]

        att = ExitStack()
        bias = sb("bias", [P, H, TW], F32, att)
        scratch = sb("scratch", [P, 2048], F32, att)
        qt, kt = rbuf[:, 0, :], rbuf[:, 1, :].rearrange("p (b n) -> p b n", b=2)
        pct = xn[:, 0, 0:S]
        tc = sb("tc", [P, TT, 4, 16], F32, att)
        pc = sb("pc", [P, TT, 4, 32], F32, att)
        cst = sb("cst", [P, 4, 8], F32, att)
        qst = sb("qst", [P, 4, 16], F32, att)
        hst = sb("hst", [P, 2, 8], F32, att)
        hidk = sb("hidk", [P, 2, G * NCMP], F32, att)
        hid = view(xn[0:G * NCMP, 0, 512:513], 0, [[HID, 2], [1, HID]])
        vcmp = xn[:, 0, S:2 * S].rearrange("p (g d) -> p g d", g=G)
        kst = sb("kst", [G * NCMP, 4], F32, att)
        kbd = sb("kbd", [P, G, 2, 16], F32, att)
        onehot, strip = scratch[0:BUCKETS + 1, 0:512], scratch[0:H, 512:1024]
        gw = scratch[:, 1024:1024 + KD * NB].rearrange("p (k n) -> p k n", k=KD)
        dw = scratch[:, 1664:1664 + KD * SH].rearrange("p (k n) -> p k n", k=KD)
        kc = tc[0:G * NCMP, :, :, :].rearrange("p c h n -> p c (h n)")
        kcn = pc[0:G * NCMP, 0, :, :].rearrange("p (b h) n -> p b (h n)", b=2)
        hidv = scratch[:, 1024:2048].rearrange("p (m g n) -> p m g n", m=2, g=G)
        gates = ExitStack()
        gwh = sb("gwh", [P, KD, NB], F32R, gates)
        gwl = sb("gwl", [P, KD, NB], F32R, gates)
        gates.close()
        qkv = sb("qkv", [P, 2, TT, QKV], F32, att)
        pt = sb("pt", [P, 2, 2, TW], F32, att)
        gx = pt[0:NB, 0, 0, 0:S]
        att.close()

        xb = sb("xb", [P, 4, 3 + S])
        cacc = sb("cacc", [P, 4, S])
        xc = sb("xc", [P, 2, 4, S])
        sz = sb("sz", [P, 512])
        xsn = sb("xsn", [P, TT, S])
        bn = sb("bn", [P, P])
        eb = sb("eb", [P, TT, 4, P])
        acb = sb("acb", [P, 2, 4, TT, P])
        xw = sb("xw", [P, S])
        sk = sb("sk", [P, TT, S])
        prev = sb("prev", [P, S])
        y = sb("y", [P, TT, S])
        sst = sb("sst", [P, 6])
        yth = sb("yth", [P, 2, S], F32R)
        ytl = sb("ytl", [P, 2, S], F32R)
        dt = sb("dt", [P, TT, SH])
        dta = sb("dta", [P, TT, SH])
        dtt = sb("dtt", [P, 4, TT, SH])
        acs = sb("acs", [P, TT, SH])
        nacs = sb("nacs", [P, TT, SH])
        eacs = sb("eacs", [P, SH])
        wend = sb("wend", [P, SH])
        ealog = sb("ealog", [P, SH])
        acst = sb("acst", [SH, S])
        probs = scratch[:, 1024:2048].rearrange("p (b n) -> p b n", b=2)
        tsc = scratch[:, 0:1024].rearrange("p (b n) -> p b n", b=2)
        blk = view(scratch[:, 0:1], 0, [[60, 16], [1, 60]])
        blkh = view(hth[:, 0, 0, 0:1], 0, [[960, 2], [60, 16], [1, 60]])
        blkl = view(htl[:, 0, 0, 0:1], 0, [[960, 2], [60, 16], [1, 60]])
        oth = hth[:, :, :, :].rearrange("p a b n -> p (a b) n")
        otl = htl[:, :, :, :].rearrange("p a b n -> p (a b) n")

        def xt_bank(q, k):
            if q == 0:
                return 4 + k // 2, (k % 2) * S, k | 1
            return (0, 1, 2, 3, 6, 6, 7, 7)[k], (k % 2) * S * (k // 4), k if k < 4 else k | 1

        def in_order(p):
            return view(bank[7][:, p * S + P - 1:p * S + P], 0, [[P, 2], [-1, P]])

        piece_in = [sem(f"piece_in{i}") for i in range(RAW)]
        high_ready, low_ready, piece_used = sem("high_ready"), sem("low_ready"), sem("piece_used")
        x_in, params_in, rows_in, w_small_in = sem("x_in"), sem("params_in"), sem("rows_in"), sem("w_small_in")
        rest_in = sem("rest_in")
        strip_in, bias_in, out_done = sem("strip_in"), sem("bias_in"), sem("out_done")
        acs_out, acs_in = sem("acs_out"), [sem("acs_in0"), sem("acs_in1")]
        strip_ps, strip_ready = sem("strip_ps"), sem("strip_ready")
        pool_set, gq_ready, small_hi, small_lo = sem("pool_set"), sem("gq_ready"), sem("small_hi"), sem("small_lo")
        sumsq_ready, rstd_ready, xn_ready = sem("sumsq_ready"), sem("rstd_ready"), sem("xn_ready")
        xt_ps, xt_hi, xt_lo, x_ready = sem("xt_ps"), sem("xt_hi"), sem("xt_lo"), sem("x_ready")
        y_ps = sem("y_ps")
        relu_ready, sq_ready, hid_hi, hid_lo = sem("relu_ready"), sem("sq_ready"), sem("hid_hi"), sem("hid_lo")
        gate_ps, gate_exp, gate_ready, gate_t = sem("gate_ps"), sem("gate_exp"), sem("gate_ready"), sem("gate_t")
        kvc_ready, kvt_ps, blk_ready, blk_hi, blk_lo = sem("kvc_ready"), sem("kvt_ps"), sem("blk_ready"), sem("blk_hi"), sem("blk_lo")
        hid_ready, cmp_ps, vcmp_ready = sem("hid_ready"), sem("cmp_ps"), sem("vcmp_ready")
        silu_ready, hid_ps = sem("silu_ready"), sem("hid_ps")
        kc_sq, kc_rstd, kcn_ready, kct_ps, kbd_ready = sem("kc_sq"), sem("kc_rstd"), sem("kcn_ready"), sem("kct_ps"), sem("kbd_ready")
        qkv_sq, qkv_ssq, qkv_rstd, qkv_ready = sem("qkv_sq"), sem("qkv_ssq"), sem("qkv_rstd"), sem("qkv_ready")
        v_ready = sem("v_ready")
        qkt_ps, qt_ready, kt_ready = sem("qkt_ps"), sem("qt_ready"), sem("kt_ready")
        sc_ps, sm_max, sm_exp, p_ready = sem("sc_ps"), sem("sm_max"), sem("sm_exp"), sem("p_ready")
        pt_ps, pt_ready = sem("pt_ps"), sem("pt_ready")
        csc_ps, csc_ready, csc_exp, pc_ready, pct_ps, pct_ready = (
            sem("csc_ps"), sem("csc_ready"), sem("csc_exp"), sem("pc_ready"), sem("pct_ps"), sem("pct_ready"))
        pv_done, ot_hi, ot_lo = sem("pv_done"), sem("ot_hi"), sem("ot_lo")
        dve_step, act_step, pool_step = sem("dve_step"), sem("act_step"), sem("pool_step")
        dt_raw, dt_raw_out = sem("dt_raw"), sem("dt_raw_out")
        dt_ps, dt_neg, dt_exp, dt_one, dt_ln, dt_ready = (
            sem("dt_ps"), sem("dt_neg"), sem("dt_exp"), sem("dt_one"), sem("dt_ln"), sem("dt_ready"))
        acs_ps, acs_ready, acst_ps, acst_ready, decay_ready, wend_ready = (
            sem("acs_ps"), sem("acs_ready"), sem("acst_ps"), sem("acst_ready"), sem("decay_ready"), sem("wend_ready"))
        masked, e_ready, m_ready = sem("masked"), sem("e_ready"), sem("m_ready")
        conv_in, conv_done, xc_ready, z_ready = sem("conv_in"), sem("conv_done"), sem("xc_ready"), sem("z_ready")
        t_ps, bn_ready, xsn_ready, xw_ready, sk_ready = sem("t_ps"), sem("bn_ready"), sem("xsn_ready"), sem("xw_ready"), sem("sk_ready")
        s_ps, prev_ready, ys_ps, y_ready, ysq_ready, yrstd_ready = (
            sem("s_ps"), sem("prev_ready"), sem("ys_ps"), sem("y_ready"), sem("ysq_ready"), sem("yrstd_ready"))
        yn_ready, yt_ps, yt_hi, yt_lo = sem("yn_ready"), sem("yt_ps"), sem("yt_hi"), sem("yt_lo")

        block = ctx.enter_context(nc.Block())

        @block.sync
        def _(sp):
            def piece(n):
                if n.s >= RAW:
                    sp.wait_ge(low_ready, n.n(1, 1 - RAW))
                src = a["stream"][bass.ds(n.n(), 1), :, :].rearrange("a p n -> (a p) n")
                sp.dma_start(raw[:, n.s % RAW, :], src).then_inc(piece_in[n.s % RAW], PER)

            def small_load(dst, src):
                sp.dma_start(dst, src).then_inc(w_small_in, 16)

            for c in range(TT):
                sp.dma_start(x[:, c, :], a["x"][0, c * P:(c + 1) * P, :]).then_inc(x_in, 16)
            sp.dma_start(par[:, :], a["params"]).then_inc(params_in, 16)
            for i in range(2):
                piece(At(i))
            small_load(scratch[:, 1024:1024 + KD * NB], a["small_w"][:, GW_0:GW_0 + KD * NB])
            small_load(scratch[:, 1664:1664 + KD * SH], a["small_w"][:, DW_0:DW_0 + KD * SH])
            sp.wait_ge(strip_ready, 1)
            sp.dma_start(strip_dram, strip).then_inc(strip_in, 16)
            for i in range(2, 4):
                piece(At(i))
            sp.dma_start(w2[:, :, :, :].rearrange("p i m d -> p (i m d)"), a["small_w"][:, W2_0:W2_0 + 256]).then_inc(rest_in, 16)
            for t, name in ((dtb, "ssd_dt_bias"), (alog, "ssd_a_log"), (dskip, "ssd_d")):
                sp.dma_start(t[:, :], rows(a[name], 0, [[0, P], [1, SH]])).then_inc(rest_in, 16)
            first = RAW + (N_END - RAW) % 4
            for i in range(4, first):
                piece(At(i))
            sp.wait_ge(strip_in, 16)
            sp.dma_start(bias[:, :, :], rows(strip_dram, 0, [[1, P], [512, H], [1, TW]])).then_inc(bias_in, 16)
            with sp.Fori(0, (N_END - first) // 4) as it:
                for u in range(4):
                    piece(At(first + u, it, 4))
            for c in range(TT):
                sp.wait_ge(x_ready, 12 + 2 * (c + 1))
                sp.dma_start(a["out"][0, c * P:(c + 1) * P, :], x[:, c, :]).then_inc(out_done, 16)
            sp.wait_ge(out_done, 16 * TT)

        @block.scalar
        def _(act):
            step = Steps(act_step)
            copy = ACT.Copy

            def load(dst, src, s):
                act.dma_start(dst, src).then_inc(s, 16)

            def split(n):
                act.wait_ge(piece_in[n.s % RAW], raw_round(n))
                if n.s >= HL:
                    act.wait_ge(piece_used, n.n(1, 1 - HL))
                nc.scalar.activation(whi[:, n.s % HL, :], raw[:, n.s % RAW, :], copy).then_inc(high_ready, 1)

            load(table[0:BUCKETS, :], a["rel_table"], rows_in)
            load(onehot, a["onehot"], rows_in)

            def sumsq(q):
                for c in range(TT):
                    for h in range(2):
                        act.wait_ge(*((x_in, 16 * TT) if q == 0 else (x_ready, 4 * (q - 1) + 2 * c + h + 1)))
                        if q:
                            act.wait_ge(xt_ps, 8 * q)
                        half = slice(h * 512, (h + 1) * 512)
                        nc.scalar.activation(xn[:, c, half], x[:, c, half], ACT.Square,
                                             accum_out=ssq[:, c, h:h + 1]).then_inc(sumsq_ready, 1)

            def norm_t(q):
                for k in range(KD):
                    b, o, last = xt_bank(q, k)
                    act.wait_ge(xt_ps, KD * q + last + 1)
                    col = (q // 2) * 8 + (q % 2) * 16 + k
                    nc.scalar.activation(xth[:, k, :], bank[b][:, o:o + S], copy, scale=pcol[:, col:col + 1]).then_inc(xt_hi, 1)

            sumsq(0)
            act.wait_ge(strip_ps, 1)
            nc.scalar.activation(strip, bank[2][0:H, :], copy).then_inc(strip_ready, 1)
            split(At(0))
            act.wait_ge(params_in, 16)
            norm_t(0)
            nc.scalar.activation(gq[:, :], pcol[:, C_QG:C_QG + 1], copy, scale=float(DH) ** -0.5).then_inc(gq_ready, 1)
            split(At(1))
            act.wait_ge(w_small_in, 16 * 2)
            nc.scalar.activation(gwh[:, :, :], gw[:, :, :], copy).then_inc(small_hi, 1)
            nc.scalar.activation(dwh[:, :, :], dw[:, :, :], copy).then_inc(small_hi, 1)
            split(At(2))
            split(At(3))
            for c in range(TT):
                act.wait_ge(piece_used, 2)
                nc.scalar.activation(view(xn[:, c, 0:1], 0, [[128, 8], [64, 2], [1, DH]]),
                                     view(bank[c][:, 0:1], 0, [[64, 8], [0, 2], [1, DH]]), copy).then_inc(kvc_ready, 1)
            act.wait_ge(gate_ps, 1)
            nc.scalar.activation(gx, view(bank[6][0:NB, S - 1:S], 0, [[-1, S]]), ACT.Exp, scale=-1.0).then_inc(gate_exp, 1)
            split(At(4))
            split(At(5))
            for kv in range(2):
                act.wait_ge(blk_ready, 8 * (kv + 1))
                nc.scalar.activation(blkh[:, kv, :, :], blk, copy).then_inc(blk_hi, 1)
                if kv == 0:
                    split(At(6))

            def qkv_squares(g):
                for c in range(TT):
                    act.wait_ge(piece_used, N_ATT[g] + 2)
                    act.wait_ge(*((qkv_ssq, 2 * g) if g else (kvt_ps, 4)))
                    nc.scalar.activation(xn[:, 1, c * 512:c * 512 + 384], bank[4 + c][:, 0:384], ACT.Square).then_inc(qkv_sq, 1)

            def value_copy(g):
                for c in range(TT):
                    if g >= 2:
                        act.wait_ge(pv_done, 4 * (g - 1))
                    nc.scalar.activation(view(qkv[:, g % 2, c, 384:385], 0, [[192, 2], [1, DH]]),
                                         view(bank[4 + c][:, 384:385], 0, [[DH, 2], [1, DH]]), copy).then_inc(v_ready, 1)

            def query_t(g):
                act.wait_ge(gq_ready, 1)
                act.wait_ge(qkt_ps, 2 * g + 1)
                nc.scalar.activation(view(qt, 0, [[P, 4], [1, P]]), view(bank[4][:, P - 1:P], 0, [[P, 4], [-1, P]]), copy,
                                     scale=gq[:, 0:1]).then_inc(qt_ready, 1)
                act.wait_ge(qkt_ps, 2 * g + 2)
                nc.scalar.activation(kt[:, :, :], bank[5][:, :].rearrange("p (b n) -> p b n", b=2), copy,
                                     scale=pcol[:, C_KG:C_KG + 1]).then_inc(kt_ready, 1)

            def hidden(kv):
                act.wait_ge(piece_used, N_W1 + 2 * kv + 2)
                nc.scalar.activation(hid[:, kv, :], bank[6 + kv][0:G * NCMP, 0:HID], ACT.Silu).then_inc(silu_ready, 1)

            def probs_copy(m):
                act.wait_ge(pt_ps, 2 * m + 2)
                if m >= 2:
                    act.wait_ge(pv_done, m - 1)
                for b in range(2):
                    nc.scalar.activation(pt[:, m % 2, b, :], bank[2 + b][:, 0:TW], copy).then_inc(pt_ready, 1)

            def out_high(p):
                act.wait_ge(pv_done, 2 * p + 2)
                nc.scalar.activation(view(oth[:, p, 0:1], 0, [[P, 2], [1, P]]), in_order(p % 2), copy).then_inc(ot_hi, 1)

            def cmp_exp(g):
                act.wait_ge(csc_ready, g + 1)
                nc.scalar.activation(tc[:, :, :, 0:NCMP], tc[:, :, :, 0:NCMP], ACT.Exp).then_inc(csc_exp, 1)

            qkv_squares(0)
            value_copy(0)
            split(At(7))
            hidden(0)
            split(At(8))
            act.wait_ge(hid_ps, 1)
            nc.scalar.activation(hidk[:, :, :], view(bank[6][:, 256:257], 0, [[64, 2], [1, G * NCMP]]), copy).then_inc(hid_ready, 1)
            query_t(0)
            hidden(1)
            act.wait_ge(hid_ps, 2)
            act.wait_ge(pool_set, 6)
            for m in range(2):
                nc.scalar.activation(view(hidv[:, m, 0, 0:1], 0, [[P, G], [32, 4], [1, NCMP]]),
                                     view(bank[7][:, 256 + 64 * m:257 + 64 * m], 0, [[NCMP, G], [0, 4], [1, NCMP]]),
                                     copy).then_inc(hid_ready, 1)
            split(At(9))
            act.wait_ge(cmp_ps, 2)
            nc.scalar.activation(vcmp, bank[1][:, 0:256].rearrange("p (g d) -> p g d", g=G), copy).then_inc(vcmp_ready, 1)
            for g in range(G):
                for i in range(8):
                    t = i % 2
                    nk = P * (t + 1)
                    n = 8 * g + i
                    act.wait_ge(sm_max, 2 * n + 2)
                    if n >= 2:
                        act.wait_ge(pt_ps, n - 1)
                    for b in range(2):
                        nc.scalar.activation(probs[:, t, b * S:b * S + nk], tsc[:, t, b * S:b * S + nk], ACT.Exp,
                                             bias=hst[:, t, b:b + 1], scale=-1.0,
                                             accum_out=hst[:, t, 2 + b:3 + b]).then_inc(sm_exp, 1)
                    if i == 1:
                        act.wait_ge(pct_ps, g + 1)
                        if g:
                            act.wait_ge(pv_done, 4 * g)
                        nc.scalar.activation(pct, bank[6][:, 256:512], copy).then_inc(pct_ready, 1)
                    if n and i % 2 == 0:
                        probs_copy(n // 2 - 1)
                    if n > 1 and i in (1, 5):
                        out_high(2 * g - 1 if i == 1 else 2 * g)
                    if n == 0:
                        cmp_exp(0)
                        split(At(10))
                    if n == 1 or g and i == 0:
                        split(At(11 + 2 * g))
                    if i == 7 and g < G - 1:
                        split(At(12 + 2 * g))
                    if i == 3 and g < G - 1:
                        qkv_squares(g + 1)
                        value_copy(g + 1)
                    if i == 6 and g < G - 1:
                        query_t(g + 1)
                    if i == 7 and g < G - 1:
                        cmp_exp(g + 1)
            probs_copy(4 * G - 1)
            out_high(2 * G - 1)

            def mlp(layer, base):
                def relu(j, n, half):
                    act.wait_ge(piece_used, n.n(1, 1))
                    if layer or j.s:
                        act.wait_ge(hid_lo, j.n(2, 2 * MJ * layer + half - 1))
                    nc.scalar.activation(rbuf[:, half, :], bank[4 + 2 * (j.s % 2) + half][:, :], ACT.Relu).then_inc(relu_ready, 1)

                def high(j, half):
                    act.wait_ge(sq_ready, j.n(2, 2 * MJ * layer + half + 1))
                    nc.scalar.activation(hth[:, j.s % 2, 2 * half:2 * half + 2, :],
                                         rbuf[:, half, :].rearrange("p (m n) -> p m n", m=2), copy).then_inc(hid_hi, 1)

                def body(j, n):
                    split(n + 2)
                    relu(j + 1, n, 0)
                    split(n + 3)
                    high(j + 1, 0)
                    relu(j + 1, n + 1, 1)
                    split(n + 4)
                    high(j + 1, 1)
                    split(n + 5)
                split(At(base + 2))
                split(At(base + 3))
                relu(At(0), At(base), 0)
                high(At(0), 0)
                relu(At(0), At(base + 1), 1)
                high(At(0), 1)
                body(At(0), At(base + 2))
                with act.Fori(0, (MJ - 2) // 2) as it:
                    for u in range(2):
                        body(At(1 + u, it, 2), At(base + 6 + 4 * u, it, 8))
                if layer == 0:
                    split(At(base + 4 * MJ))
                    split(At(base + 4 * MJ + 1))

            for i in range(2):
                split(At(N_MLP0 + i))
            sumsq(1)
            norm_t(1)
            mlp(0, N_MLP0)

            sumsq(2)
            norm_t(2)
            act.wait_ge(dt_raw, 1)
            nc.scalar.activation(acst[:, :], bank[5][0:SH, 0:S], copy).then_inc(dt_raw_out, 1)
            split(At(N_SSD + 2))
            act.wait_ge(rest_in, 16 * 4)
            act.wait_ge(dt_neg, 1)
            nc.scalar.activation(dtt[:, 1, :, :], dtt[:, 0, :, :], ACT.Exp).then_inc(dt_exp, 1)
            nc.scalar.activation(ealog[:, :], alog[:, :], ACT.Exp).then_inc(dt_exp, 1)
            act.wait_ge(dt_one, 1)
            nc.scalar.activation(dtt[:, 3, :, :], dtt[:, 2, :, :], ACT.Ln).then_inc(dt_ln, 1)
            def conv_load(g, n, i):
                act.wait_ge(piece_used, n.n(1, 1))
                if g.s:
                    act.wait_ge(conv_done, g.n(2, i - 1))
                nc.scalar.activation(xb[:, 2 * i:2 * i + 2, 3:3 + S],
                                     bank[4 + i][:, :].rearrange("p (q n) -> p q n", q=2), copy).then_inc(conv_in, 1)

            conv_load(At(0), At(N_SSD), 0)
            act.wait_ge(acst_ps, 1)
            nc.scalar.activation(acst[:, :], bank[7][0:SH, 0:S], copy).then_inc(acst_ready, 1)
            act.wait_ge(acs_ready, 2)
            nc.scalar.activation(eacs[:, :], acs[:, 1, :], ACT.Exp).then_inc(decay_ready, 1)
            nc.scalar.activation(wend[:, :], dtt[:, 0, 0, :], ACT.Exp).then_inc(decay_ready, 1)

            def conv_silu(g, i):
                act.wait_ge(conv_done, g.n(2, i + 1))
                if g.s >= 2:
                    act.wait_ge(ys_ps, g.n(1, -1))
                nc.scalar.activation(xc[:, g.s % 2, 2 * i:2 * i + 2, :], cacc[:, 2 * i:2 * i + 2, :], ACT.Silu).then_inc(xc_ready, 1)

            def z_silu(g, n):
                act.wait_ge(piece_used, n.n(1, 3))
                if g.s:
                    act.wait_ge(y_ready, g.n())
                nc.scalar.activation(sz[:, :], bank[6][:, :], ACT.Silu).then_inc(z_ready, 1)

            conv_load(At(0), At(N_SSD + 1), 1)
            split(At(N_SSD + 3))
            conv_silu(At(0), 0)
            conv_silu(At(0), 1)
            z_silu(At(0), At(N_SSD))

            def decays(g):
                for i in range(8):
                    c, h = i // 4, i % 4
                    act.wait_ge(masked, g.n(1, 1))
                    if g.s:
                        act.wait_ge(ys_ps, g.n())
                    nc.scalar.activation(eb[:, c, h, :], acb[:, g.s % 2, h, c, :], ACT.Exp,
                                         bias=nacs[:, c, bass.ds(g.n(4, h), 1)]).then_inc(e_ready, 1)

            def ssd(g, n, last=False):
                act.wait_ge(t_ps, g.n(2, 2))
                nc.scalar.activation(bn[:, :], bank[6][:, 256:384], copy).then_inc(bn_ready, 1)
                if not last:
                    split(n + 1)
                    split(n + 2)
                    conv_load(g + 1, n, 0)
                act.wait_ge(s_ps, g.n(1, 1))
                nc.scalar.activation(prev[:, :], bank[7][:, 0:S], copy).then_inc(prev_ready, 1)
                if not last:
                    split(n + 3)
                for c in range(TT):
                    act.wait_ge(y_ready, g.n(1, 1))
                    nc.scalar.activation(sk[:, c, :], y[:, c, :], ACT.Square, accum_out=sst[:, c:c + 1]).then_inc(ysq_ready, 1)
                if not last:
                    decays(g + 1)
                    conv_load(g + 1, n + 1, 1)
                for q in range(2):
                    act.wait_ge(yt_ps, g.n(1, 1))
                    if g.s:
                        if last:
                            act.wait_ge(piece_used, N_MLP1 - 1)
                        else:
                            act.wait_ge(piece_used, n.n())
                    nc.scalar.activation(yth[:, q, :], bank[7][:, q * S:(q + 1) * S], copy,
                                         scale=pcol[:, bass.ds(g.n(2, C_SSDN + q), 1)]).then_inc(yt_hi, 1)
                if not last:
                    conv_silu(g + 1, 0)
                    split(n + 4)
                    conv_silu(g + 1, 1)
                    z_silu(g + 1, n)
            decays(At(0))
            ssd(At(0), At(N_SSD + 3))
            with act.Fori(0, (SG - 2) // 2) as it:
                for u in range(2):
                    ssd(At(1 + u, it, 2), At(N_SSD + 7 + 4 * u, it, 8))
            ssd(At(SG - 1), None, last=True)
            split(At(N_MLP1))
            split(At(N_MLP1 + 1))

            sumsq(3)
            norm_t(3)
            mlp(1, N_MLP1)


        @block.gpsimd
        def _(pool):
            step = Steps(pool_step)
            pool.memset(table[BUCKETS:BUCKETS + 1, :], NEG).then_inc(pool_set, 1)
            pool.wait_ge(pool_set, 1)
            pool.memset(mhalf[:, :], -0.5).then_inc(pool_set, 1)
            pool.memset(epst[:, :], 256 * EPS).then_inc(pool_set, 1)
            pool.memset(ones[:, :], 1.0).then_inc(pool_set, 1)
            pool.memset(kbd[:, :, :, :], 0.0).then_inc(pool_set, 1)
            def rsqrt(dst, tmp, src, width, n, done, part=P):
                step.mark(nc.gpsimd.tensor_scalar(tmp, src, width * EPS, None, ALU.add))
                step.wait(pool)
                return nc.gpsimd.tensor_tensor(dst, tmp, mhalf[0:part, 0:n], ALU.pow).then_inc(done, 1)

            def norm_stat(q):
                for c in range(TT):
                    pool.wait_ge(sumsq_ready, 4 * q + 2 * c + 1)
                    step.mark(nc.gpsimd.tensor_scalar(vsum[:, c:c + 1], ssq[:, c, 0:1], D * EPS, None, ALU.add))
                    step.wait(pool)
                    pool.wait_ge(sumsq_ready, 4 * q + 2 * c + 2)
                    step.mark(nc.gpsimd.tensor_tensor(vsum[:, c:c + 1], vsum[:, c:c + 1], ssq[:, c, 1:2], ALU.add))
                    step.wait(pool)
                    nc.gpsimd.tensor_tensor(rstd[:, c:c + 1], vsum[:, c:c + 1], mhalf[:, 0:1], ALU.pow).then_inc(rstd_ready, 1)

            pool.wait_ge(pool_set, 5)
            norm_stat(0)
            pool.wait_ge(gate_t, 1)
            pool.memset(hidv, 0.0).then_inc(pool_set, 1)
            pool.wait_ge(pool_set, 6)

            def low(n):
                pool.wait_ge(high_ready, n.n(1, 1))
                pool.wait_ge(low_ready, n.n())
                nc.gpsimd.tensor_tensor(wlo[:, n.s % HL, :], raw[:, n.s % RAW, :], whi[:, n.s % HL, :].bitcast(F32),
                                        ALU.subtract).then_inc(low_ready, 1)

            def qkv_stat(g):
                for c in range(TT):
                    pool.wait_ge(qkv_ssq, 2 * g + c + 1)
                    if g:
                        pool.wait_ge(qkv_ready, 6 * g)
                    st = slice(8 * c, 8 * c + 6)
                    step.mark(nc.gpsimd.tensor_scalar(qst[:, 1, st], qst[:, 0, st], DH * EPS, None, ALU.add))
                    step.wait(pool)
                    nc.gpsimd.tensor_tensor(qst[:, 2, st], qst[:, 1, st], mhalf[:, 0:6], ALU.pow).then_inc(qkv_rstd, 1)

            qkv_stat(0)
            pool.wait_ge(kc_sq, 1)
            rsqrt(kst[:, 2:3], kst[:, 1:2], kst[:, 0:1], DH, 1, kc_rstd, G * NCMP)
            pool.wait_ge(kct_ps, 1)
            pool.memset(pc[:, :, :, :], 0.0).then_inc(pool_set, 1)
            for g in range(G):
                if g:
                    qkv_stat(g)
                low(At(11 + 2 * g))
            norm_stat(1)
            norm_stat(2)

            pool.wait_ge(acst_ready, 1)
            pool.dma_start(acs_dram, acst[:, :]).then_inc(acs_out, 16)
            pool.wait_ge(acs_out, 16)

            def load_decay(g):
                src = acs_dram[bass.ds(g.n(4), 4), :]
                src = bass.AP(src.tensor, src.offset, [[0, P], [1, 4 * S]])
                pool.dma_start(acb[:, g.s % 2, :, :, :].rearrange("p h c l -> p (h c l)"), src).then_inc(acs_in[g.s % 2], 16)

            def mask(g):
                pool.wait_ge(acs_in[g.s % 2], 16 * (g.s // 2 + 1) if g.it is None else g.it * 16 + 16 * (g.s // 2 + 1))
                v = acb[:, g.s % 2, :, :, :].rearrange("p h c l -> p (h c) l")
                nc.gpsimd.tensor_tensor(v, v, view(segmask[:, 0:1], 0, [[0, 8], [1, P]]), ALU.add).then_inc(masked, 1)

            def heads(t, g, dims):
                return view(t[:, bass.ds(g.n(4), 4)], 0, dims)

            def ssd(g, n, last=False):
                if not last:
                    if g.s:
                        pool.wait_ge(e_ready, g.n(8))
                    load_decay(g + 1)
                pool.wait_ge(xsn_ready, g.n(1, 1))
                if g.s:
                    pool.wait_ge(s_ps, g.n())
                nc.gpsimd.tensor_tensor(xw[:, :].rearrange("p (h d) -> p h d", h=4),
                                        xsn[:, 0, :].rearrange("p (h d) -> p h d", h=4),
                                        heads(wend, g, [[1, 4], [0, DH]]), ALU.mult).then_inc(xw_ready, 1)
                if g.s:
                    pool.wait_ge(ysq_ready, g.n(2))
                for c in range(TT):
                    nc.gpsimd.tensor_tensor(sk[:, c, :].rearrange("p (h d) -> p h d", h=4),
                                            xsn[:, c, :].rearrange("p (h d) -> p h d", h=4),
                                            heads(dskip, g, [[1, 4], [0, DH]]), ALU.mult).then_inc(sk_ready, 1)
                if not last:
                    mask(g + 1)
                pool.wait_ge(ysq_ready, g.n(2, 2))
                step.mark(nc.gpsimd.tensor_tensor(sst[:, 2:4], sst[:, 0:2], epst[:, :], ALU.add))
                step.wait(pool)
                nc.gpsimd.tensor_tensor(sst[:, 4:6], sst[:, 2:4], mhalf[:, 0:2], ALU.pow).then_inc(yrstd_ready, 1)
                if not last:
                    low(n + 3)

            pool.wait_ge(rest_in, 16 * 4)
            pool.wait_ge(wend_ready, 1)
            load_decay(At(0))
            mask(At(0))
            before = step.base.s + step.k
            step.enter(At(before))
            ssd(At(0), At(N_SSD + 3))
            with pool.Fori(0, (SG - 2) // 2) as it:
                for u in range(2):
                    step.enter(At(before + 1 + u, it, 2))
                    ssd(At(1 + u, it, 2), At(N_SSD + 7 + 4 * u, it, 8))
            step.enter(At(before + SG - 1))
            ssd(At(SG - 1), None, last=True)
            norm_stat(3)

        @block.vector
        def _(dve):
            step = Steps(dve_step)
            V = nc.vector

            def low(n, after_pool=False):
                dve.wait_ge(high_ready, n.n(1, 1))
                if after_pool:
                    dve.wait_ge(low_ready, n.n())
                V.tensor_tensor(wlo[:, n.s % HL, :], raw[:, n.s % RAW, :], whi[:, n.s % HL, :].bitcast(F32),
                                ALU.subtract).then_inc(low_ready, 1)

            def norm(q):
                norm_x(q)
                norm_low(q)

            def norm_x(q):
                for c in range(TT):
                    dve.wait_ge(rstd_ready, TT * q + c + 1)
                    for h in range(2):
                        half = slice(h * 512, (h + 1) * 512)
                        V.tensor_scalar(xn[:, c, half], x[:, c, half], rstd[:, c:c + 1], float(D) ** 0.5,
                                        ALU.mult, ALU.mult).then_inc(xn_ready, 1)

            def norm_low(q):
                for k in range(KD):
                    b, o, last = xt_bank(q, k)
                    dve.wait_ge(xt_hi, KD * q + last + 1)
                    col = (q // 2) * 8 + (q % 2) * 16 + k
                    V.scalar_tensor_tensor(xtl[:, k, :], bank[b][:, o:o + S], pcol[:, col:col + 1], xth[:, k, :].bitcast(F32),
                                           ALU.mult, ALU.subtract).then_inc(xt_lo, 1)

            def residual(r, last_piece):
                for c in range(TT):
                    for nh in range(2):
                        i = 2 * c + nh
                        if r:
                            dve.wait_ge(*((piece_used, last_piece + 1) if i == 3 else (y_ps, 3 * r + i)))
                        else:
                            dve.wait_ge(*((piece_used, last_piece + 2 * nh - 1) if c else (y_ps, nh + 1)))
                        V.tensor_tensor(x[:, c, nh * 512:(nh + 1) * 512], x[:, c, nh * 512:(nh + 1) * 512],
                                        bank[i if r else 4 * (1 - nh) + c][:, :], ALU.add).then_inc(x_ready, 1)

            norm_x(0)
            low(At(0))
            dve.wait_ge(params_in, 16)
            norm_low(0)
            low(At(1))
            for i, (h, l, t) in enumerate(((gwh, gwl, gw), (dwh, dwl, dw))):
                dve.wait_ge(small_hi, i + 1)
                V.tensor_tensor(l[:, :, :], t[:, :, :], h[:, :, :].bitcast(F32), ALU.subtract).then_inc(small_lo, 1)
            low(At(2))
            low(At(3))
            low(At(4))
            dve.wait_ge(strip_in, 16)
            for kv in range(2):
                dve.wait_ge(kvt_ps, 2 * kv + 2)
                if kv:
                    dve.wait_ge(blk_hi, 1)
                    dve.wait_ge(blk_lo, 1)
                for g in range(G):
                    for b in range(2):
                        part = slice(b * DH, (b + 1) * DH)
                        i = 4 * kv + g
                        src = view(bank[i // 2][part, 0:1], (i % 2) * S + b, [[2, 16], [CS, NCMP]])
                        dst = view(scratch[part, 0:1], g * NCMP, [[60, 16], [1, NCMP]])
                        pe = view(par[part, C_PE + 16 * kv:C_PE + 1 + 16 * kv], 0, [[1, 16], [0, NCMP]])
                        V.tensor_tensor(dst, src, pe, ALU.add).then_inc(blk_ready, 1)
                if kv == 0:
                    dve.wait_ge(gate_t, 1)
                    step.mark(V.tensor_scalar_add(gate[:, :, :], view(bank[7][:, 0:1], 0, [[64, 2], [1, NB]]), 1.0))
                    step.wait(dve)
                    V.reciprocal(gate[:, :, :], gate[:, :, :]).then_inc(gate_ready, 1)
                dve.wait_ge(blk_hi, kv + 1)
                V.tensor_tensor(blkl[:, kv, :, :], blk, blkh[:, kv, :, :].bitcast(F32), ALU.subtract).then_inc(blk_lo, 1)
                if kv == 0:
                    low(At(5))
            def keys():
                dve.wait_ge(cmp_ps, 1)
                step.mark(V.tensor_copy(kc[:, 0, :], bank[0][0:G * NCMP, 0:DH]))
                step.wait(dve)
                step.mark(V.tensor_tensor(kc[:, 1, :], kc[:, 0, :], kc[:, 0, :], ALU.mult))
                step.wait(dve)
                V.tensor_reduce(kst[:, 0:1], kc[:, 1, :], AX.X, ALU.add).then_inc(kc_sq, 1)
                dve.wait_ge(kc_rstd, 1)
                for b in range(2):
                    V.tensor_scalar(kcn[:, b, :], kc[:, 0, :], kst[:, 2:3], float(DH) ** 0.5,
                                    ALU.mult, ALU.mult).then_inc(kcn_ready, 1)

            def keys_block():
                dve.wait_ge(kct_ps, 1)
                dve.wait_ge(pool_set, 5)
                for b in range(2):
                    part = slice(b * DH, (b + 1) * DH)
                    V.tensor_scalar(kbd[part, :, b, 0:NCMP], view(bank[2][part, 0:1], 0, [[NCMP, G], [1, NCMP]]),
                                    par[part, C_KG:C_KG + 1], None, ALU.mult).then_inc(kbd_ready, 1)

            def qkv_sums(g):
                for c in range(TT):
                    dve.wait_ge(qkv_sq, 2 * g + c + 1)
                    if g:
                        dve.wait_ge(qkv_rstd, 2 * g)
                    V.tensor_reduce(qst[:, 0, 8 * c:8 * c + 6], xn[:, 1, c * 512:c * 512 + 384].rearrange("p (n d) -> p n d", d=DH),
                                    AX.X, ALU.add).then_inc(qkv_ssq, 1)

            def qkv_norm(g, tiles=range(TT)):
                for c in tiles:
                    dve.wait_ge(qkv_rstd, 2 * g + c + 1)
                    if g >= 2:
                        dve.wait_ge(pv_done, 4 * (g - 1))
                    dve.wait_ge(v_ready, 2 * (g + 1))
                    for to, of, st in (([0, DH, 4], [0, DH], [0, 1]), ([256, 192, 2], [256, DH], [4, 1]),
                                       ([320, 192, 2], [256, DH], [4, 1])):
                        V.scalar_tensor_tensor(view(qkv[:, g % 2, c, 0:1], to[0], [[to[1], to[2]], [1, DH]]),
                                               view(bank[4 + c][:, 0:1], of[0], [[of[1], to[2]], [1, DH]]), float(DH) ** 0.5,
                                               view(qst[:, 2, 8 * c:8 * c + 1], st[0], [[st[1], to[2]], [0, DH]]),
                                               ALU.mult, ALU.mult).then_inc(qkv_ready, 1)

            def key_t(g):
                dve.wait_ge(qkt_ps, 2 * g + 2)
                V.tensor_scalar(kt[:, :, :], bank[5][:, :].rearrange("p (b n) -> p b n", b=2), pcol[:, C_KG:C_KG + 1],
                                None, ALU.mult).then_inc(kt_ready, 1)

            def score_max(g, i):
                h, t, n = i // 2, i % 2, 8 * g + i
                nk = P * (t + 1)
                dve.wait_ge(sc_ps, n + 1)
                if n >= 2:
                    dve.wait_ge(sm_exp, 2 * n - 2)
                for b in range(2):
                    V.tensor_tensor_reduce(out=tsc[:, t, b * S:b * S + nk], in0=bank[t][:, b * nk:(b + 1) * nk],
                                           in1=bias[:, 4 * g + h, P * (1 - t):P * (1 - t) + nk], scale=-1.0,
                                           scalar=3e38, op0=ALU.add, op1=ALU.min,
                                           accum_out=hst[:, t, b:b + 1]).then_inc(sm_max, 1)

            def score_scale(g, i):
                h, t, n = i // 2, i % 2, 8 * g + i
                nk = P * (t + 1)
                dve.wait_ge(sm_exp, 2 * n + 2)
                step.mark(V.reciprocal(hst[:, t, 4:6], hst[:, t, 2:4]))
                step.wait(dve)
                for b in range(2):
                    col = (1 + b) * H + 4 * g + h
                    V.tensor_scalar(probs[:, t, b * S:b * S + nk], probs[:, t, b * S:b * S + nk],
                                    hst[:, t, 4 + b:5 + b], gate[:, 1 - t, col:col + 1],
                                    ALU.mult, ALU.mult).then_inc(p_ready, 1)

            def out_low(p):
                dve.wait_ge(ot_hi, p + 1)
                V.tensor_tensor(view(otl[:, p, 0:1], 0, [[P, 2], [1, P]]), in_order(p % 2),
                                view(oth[:, p, 0:1].bitcast(F32), 0, [[P, 2], [1, P]]), ALU.subtract).then_inc(ot_lo, 1)

            tcv = tc[:, :, :, 0:NCMP]

            def over_heads(i):
                return view(cst[:, i, 0:1], 0, [[4, 2], [1, 4], [0, NCMP]])

            def cmp_max(g):
                dve.wait_ge(csc_ps, g + 1)
                src = view(bank[6][:, 0:1], 0, [[64, 2], [16, 4], [1, NCMP]])
                bs = view(bias[:, 4 * g, 0:1], CB - 1, [[P, 2], [TW, 4], [CS, NCMP]])
                step.mark(V.tensor_tensor(tcv, src, bs, ALU.add))
                step.wait(dve)
                step.mark(V.tensor_reduce(cst[:, 0, :], tcv, AX.X, ALU.max))
                step.wait(dve)
                step.mark(V.tensor_scalar_max(cst[:, 1, :], cst[:, 0, :], -1e20))
                step.wait(dve)
                V.tensor_tensor(tcv, tcv, over_heads(1), ALU.subtract).then_inc(csc_ready, 1)

            def cmp_scale(g):
                dve.wait_ge(csc_exp, g + 1)
                step.mark(V.tensor_reduce(cst[:, 0, :], tcv, AX.X, ALU.add))
                step.wait(dve)
                step.mark(V.tensor_scalar_max(cst[:, 2, :], cst[:, 0, :], 1e-30))
                step.wait(dve)
                step.mark(V.reciprocal(cst[:, 3, :], cst[:, 2, :]))
                if g == 0:
                    dve.wait_ge(pool_set, 7)
                step.wait(dve)
                step.mark(V.tensor_tensor(view(cst[:, 2, 0:1], 0, [[4, 2], [1, 4]]), view(cst[:, 3, 0:1], 0, [[4, 2], [1, 4]]),
                                          gate[:, :, 4 * g:4 * g + 4], ALU.mult))
                step.wait(dve)
                if g:
                    dve.wait_ge(pct_ps, g)
                V.tensor_tensor(pc[:, :, :, 0:NCMP], tcv, over_heads(2), ALU.mult).then_inc(pc_ready, 1)

            low(At(6))
            qkv_sums(0)
            low(At(7))
            qkv_norm(0)
            low(At(8))
            keys()
            low(At(9))
            keys_block()
            dve.wait_ge(gate_ready, 1)
            dve.wait_ge(bias_in, 16)
            score_max(0, 0)
            score_max(0, 1)
            cmp_max(0)
            for g in range(G):
                for i in range(8):
                    n = 8 * g + i
                    score_scale(g, i)
                    if i == 0:
                        cmp_scale(g)
                    if i == 0:
                        low(At(10 + 2 * g), after_pool=g > 0)
                    if i == 6 and g < G - 1:
                        qkv_norm(g + 1, (1,))
                    if n + 2 < 8 * G:
                        score_max((n + 2) // 8, (i + 2) % 8)
                    if i == 4 and g < G - 1:
                        qkv_sums(g + 1)
                    if n > 1 and i in (1, 5):
                        out_low(2 * g - 1 if i == 1 else 2 * g)
                    if i == 5 and g < G - 1:
                        qkv_norm(g + 1, (0,))
                    if i == 7 and g < G - 1:
                        cmp_max(g + 1)
            out_low(2 * G - 1)
            for i in range(2):
                low(At(N_MLP0 + i), after_pool=i == 0)
            residual(0, N_WO + 3)

            def mlp(layer, base):
                def square(j, half):
                    dve.wait_ge(relu_ready, j.n(2, 2 * MJ * layer + half + 1))
                    V.scalar_tensor_tensor(rbuf[:, half, :], bank[4 + 2 * (j.s % 2) + half][:, :], 0.0,
                                           rbuf[:, half, :], ALU.max, ALU.mult).then_inc(sq_ready, 1)

                def hid_low(j, half):
                    dve.wait_ge(hid_hi, j.n(2, 2 * MJ * layer + half + 1))
                    V.tensor_tensor(htl[:, j.s % 2, 2 * half:2 * half + 2, :],
                                    rbuf[:, half, :].rearrange("p (m n) -> p m n", m=2),
                                    hth[:, j.s % 2, 2 * half:2 * half + 2, :].bitcast(F32), ALU.subtract).then_inc(hid_lo, 1)

                def body(j, n):
                    low(n + 2)
                    square(j + 1, 0)
                    low(n + 3)
                    hid_low(j + 1, 0)
                    square(j + 1, 1)
                    low(n + 4)
                    hid_low(j + 1, 1)
                    low(n + 5)
                low(At(base + 2))
                low(At(base + 3))
                for half in range(2):
                    square(At(0), half)
                    hid_low(At(0), half)
                body(At(0), At(base + 2))
                with dve.Fori(0, (MJ - 2) // 2) as it:
                    for u in range(2):
                        body(At(1 + u, it, 2), At(base + 6 + 4 * u, it, 8))
                if layer == 0:
                    low(At(base + 4 * MJ))
                    low(At(base + 4 * MJ + 1))

            norm(1)
            mlp(0, N_MLP0)
            residual(1, N_SSD - 1)

            norm(2)
            V.memset(xb[:, :, 0:3], 0.0).then_inc(dve_step, 1)
            step.k += 1
            dve.wait_ge(rest_in, 16 * 4)
            dve.wait_ge(dt_ps, 1)
            step.mark(V.tensor_tensor(dta[:, :, :], bank[6][:, S:S + 2 * SH].rearrange("p (c h) -> p c h", c=2),
                                      view(dtb[:, 0:1], 0, [[0, 2], [1, SH]]), ALU.add))
            step.wait(dve)
            step.mark(V.tensor_scalar_mul(dtt[:, 1, :, :], dta[:, :, :], -1.0))
            step.wait(dve)
            V.tensor_tensor(dtt[:, 0, :, :], dta[:, :, :], dtt[:, 1, :, :], ALU.min).then_inc(dt_neg, 1)
            dve.wait_ge(dt_exp, 2)
            V.tensor_scalar_add(dtt[:, 2, :, :], dtt[:, 1, :, :], 1.0).then_inc(dt_one, 1)
            dve.wait_ge(dt_one, 1)
            step.mark(V.tensor_scalar(dtt[:, 0, :, :], dtt[:, 2, :, :], -1.0, 1e-30, ALU.add, ALU.add))
            step.wait(dve)
            step.mark(V.reciprocal(dtt[:, 0, :, :], dtt[:, 0, :, :]))
            step.wait(dve)
            low(At(N_SSD + 2))
            dve.wait_ge(dt_ln, 1)
            step.mark(V.scalar_tensor_tensor(dtt[:, 3, :, :], dtt[:, 3, :, :], 1e-30, dtt[:, 0, :, :], ALU.add, ALU.mult))
            step.wait(dve)
            step.mark(V.tensor_tensor(dtt[:, 3, :, :], dtt[:, 3, :, :], dtt[:, 1, :, :], ALU.mult))
            step.wait(dve)
            step.mark(V.scalar_tensor_tensor(dt[:, :, :], dta[:, :, :], 0.0, dtt[:, 3, :, :], ALU.max, ALU.add))
            step.wait(dve)
            V.scalar_tensor_tensor(dta[:, :, :], dt[:, :, :], -1.0, view(ealog[:, 0:1], 0, [[0, 2], [1, SH]]),
                                   ALU.mult, ALU.mult).then_inc(dt_ready, 1)
            def conv(g, i):
                dve.wait_ge(conv_in, g.n(2, i + 1))
                if g.s:
                    dve.wait_ge(xc_ready, g.n(2, i - 1))

                def col(q, tap):
                    first = (C_CB if tap == 4 else tap * 32) + (q if q < 2 else 16 + 8 * (q - 2))
                    t = pcol if tap == 4 else ccol
                    return t[:, bass.ds(g.n(2 if q < 2 else 1, first), 1)]
                for tap in (3, 0, 1, 2):
                    for q in (2 * i, 2 * i + 1):
                        if tap != 3:
                            step.wait(dve, step.k - 1)
                        if tap == 3:
                            ins = V.tensor_scalar(cacc[:, q, :], xb[:, q, 3:3 + S], col(q, 3), col(q, 4), ALU.mult, ALU.add)
                        else:
                            ins = V.scalar_tensor_tensor(cacc[:, q, :], xb[:, q, tap:tap + S], col(q, tap), cacc[:, q, :],
                                                         ALU.mult, ALU.add)
                        if tap == 2 and q % 2:
                            ins.then_inc(conv_done, 1)
                        else:
                            step.mark(ins)

            dve.wait_ge(acs_ps, 1)
            V.tensor_copy(acs[:, :, :], bank[6][:, 64:128].rearrange("p (c h) -> p c h", c=2)).then_inc(acs_ready, 1)
            dve.wait_ge(acs_ready, 1)
            step.mark(V.tensor_scalar_mul(nacs[:, :, :], acs[:, :, :], -1.0))
            V.tensor_tensor(dtt[:, 0, 0, :], bank[6][:, 128:160], acs[:, 0, :], ALU.subtract).then_inc(acs_ready, 1)
            dve.wait_ge(decay_ready, 2)
            V.tensor_tensor(wend[:, :], wend[:, :], dt[:, 0, :], ALU.mult).then_inc(wend_ready, 1)

            conv(At(0), 0)
            conv(At(0), 1)
            low(At(N_SSD + 3))

            def ssd(g, n, last=False):
                dve.wait_ge(t_ps, g.n(2, 1))
                if g.s:
                    dve.wait_ge(ys_ps, g.n())
                    dve.wait_ge(sk_ready, g.n(2))
                V.tensor_copy(xsn[:, :, :], bank[7][:, :].rearrange("p (c n) -> p c n", c=2)).then_inc(xsn_ready, 1)
                dve.wait_ge(bn_ready, g.n(1, 1))
                for i in range(8):
                    c, h = i // 4, i % 4
                    dve.wait_ge(e_ready, g.n(8, i + 1))
                    V.scalar_tensor_tensor(eb[:, c, h, :], eb[:, c, h, :], dt[:, c, bass.ds(g.n(4, h), 1)],
                                           bank[6][:, c * P:(c + 1) * P], ALU.mult, ALU.mult).then_inc(m_ready, 1)
                if not last:
                    low(n + 1)
                dve.wait_ge(ys_ps, g.n(1, 1))
                dve.wait_ge(sk_ready, g.n(2, 2))
                if g.s:
                    dve.wait_ge(yt_ps, g.n())
                step.mark(V.tensor_tensor(y[:, 1, :].rearrange("p (h d) -> p h d", h=4),
                                          bank[7][:, S:2 * S].rearrange("p (h d) -> p h d", h=4),
                                          view(eacs[:, bass.ds(g.n(4), 4)], 0, [[1, 4], [0, DH]]), ALU.mult))
                step.mark(V.tensor_tensor(y[:, 0, :], bank[6][:, 0:S], sk[:, 0, :], ALU.add))
                step.wait(dve, step.k - 1)
                step.mark(V.tensor_tensor(y[:, 1, :], y[:, 1, :], sk[:, 1, :], ALU.add))
                step.wait(dve)
                step.mark(V.tensor_tensor(y[:, 1, :], bank[6][:, S:2 * S], y[:, 1, :], ALU.add))
                step.wait(dve)
                dve.wait_ge(z_ready, g.n(1, 1))
                V.tensor_tensor(y[:, :, :].rearrange("p c n -> p (c n)"), y[:, :, :].rearrange("p c n -> p (c n)"),
                                sz[:, :], ALU.mult).then_inc(y_ready, 1)
                if not last:
                    low(n + 2)
                dve.wait_ge(yrstd_ready, g.n(1, 1))
                for c in range(TT):
                    V.tensor_scalar(y[:, c, :], y[:, c, :], sst[:, 4 + c:5 + c], 16.0, ALU.mult, ALU.mult).then_inc(yn_ready, 1)
                if not last:
                    conv(g + 1, 0)
                dve.wait_ge(yt_hi, g.n(2, 2))
                for q in range(2):
                    V.scalar_tensor_tensor(ytl[:, q, :], bank[7][:, q * S:(q + 1) * S],
                                           pcol[:, bass.ds(g.n(2, C_SSDN + q), 1)], yth[:, q, :].bitcast(F32),
                                           ALU.mult, ALU.subtract).then_inc(yt_lo, 1)
                if not last:
                    conv(g + 1, 1)
                    low(n + 4, after_pool=True)

            per = 2 * 7 + 4
            before = step.base.s + step.k
            step.enter(At(before))
            ssd(At(0), At(N_SSD + 3))
            assert step.k == per
            with dve.Fori(0, (SG - 2) // 2) as it:
                for u in range(2):
                    step.enter(At(before + per * (1 + u), it, 2 * per))
                    ssd(At(1 + u, it, 2), At(N_SSD + 7 + 4 * u, it, 8))
            step.enter(At(before + per * (SG - 1)))
            ssd(At(SG - 1), None, last=True)
            low(At(N_MLP1))
            low(At(N_MLP1 + 1))
            residual(2, N_MLP1 - 1)

            norm(3)
            mlp(1, N_MLP1)
            residual(3, N_END - 1)

        @block.tensor
        def _(pe):
            T = nc.tensor

            def mm3(out, st, mv, start, stop):
                T.matmul(out, st[0], mv[0], start=start, stop=False)
                T.matmul(out, st[0], mv[1], start=False, stop=False)
                return T.matmul(out, st[1], mv[0], start=False, stop=stop)

            def ready(n):
                pe.wait_ge(low_ready, n.n(1, 1))

            def w(n, a_, b_, width):
                lo, hi = a_ * width + b_.start, a_ * width + b_.stop
                return whi[:, n.s % HL, lo:hi], wlo[:, n.s % HL, lo:hi]

            def xt(k, c):
                return xth[:, k, c * P:(c + 1) * P], xtl[:, k, c * P:(c + 1) * P]

            def xt_all(k):
                return xth[:, k, :], xtl[:, k, :]

            def wide(n, first, banks, q=None, part=range(4)):
                if 0 in part:
                    ready(n)
                for k in part:
                    if q is not None:
                        pe.wait_ge(xt_lo, 8 * q + first + k + 1)
                    for c in range(TT):
                        last = mm3(banks[c][:, :], xt(first + k, c), w(n, k, slice(0, 512), 512),
                                   first + k == 0, first + k == KD - 1)
                if 3 in part:
                    last.then_inc(piece_used, 1)

            def attention_out(nh, half, part=range(4)):
                n = At(N_WO + 2 * nh + half)
                pe.wait_ge(ot_lo, 4 * half + 1 + max(part))
                if 0 in part:
                    ready(n)
                for c, k in [(c, k) for c in range(TT) for k in part]:
                    kk = 4 * half + k
                    last = mm3(bank[4 * (1 - nh) + c][:, :], (oth[:, kk, c * P:(c + 1) * P], otl[:, kk, c * P:(c + 1) * P]),
                               w(n, k, slice(0, 512), 512), kk == 0, kk == KD - 1)
                    if kk == KD - 1 and c == 0:
                        last.then_inc(y_ps, 1)
                if 3 in part:
                    last.then_inc(piece_used, 1)

            def qk_transposes(g):
                pe.wait_ge(qkv_ready, 6 * g + 6)
                for pr in range(2):
                    for c in range(TT):
                        o = pr * S + c * P
                        last = T.transpose(bank[4][:, o:o + P], qkv[:, g % 2, c, pr * P:(pr + 1) * P], ident)
                last.then_inc(qkt_ps, 1)
                for s in range(2):
                    for c in range(TT):
                        o = s * S + c * P
                        last = T.transpose(bank[5][:, o:o + P], qkv[:, g % 2, c, 256 + 192 * s:384 + 192 * s], ident)
                last.then_inc(qkt_ps, 1)

            def compressed_scores(g):
                pe.wait_ge(qt_ready, g + 1)
                pe.wait_ge(kbd_ready, 2)
                pe.wait_ge(*((pct_ready, g) if g else (hid_ready, 3)))
                for c in range(TT):
                    for pr in range(2):
                        o = (1 - c) * 64 + pr * 32
                        last = T.matmul(bank[6][:, o:o + 32], qt[:, pr * S + c * P:pr * S + (c + 1) * P], kbd[:, g, :, :],
                                        start=True, stop=True)
                last.then_inc(csc_ps, 1)

            def feature_product(n, out, m, k):
                return mm3(out[:, m * S:(m + 1) * S], w(n, k, slice(m * P, (m + 1) * P), 256), xt_all(k), k == 0, k == KD - 1)

            def features(n, out, part=range(2)):
                if 0 in part:
                    ready(n)
                for m in part:
                    for k in range(KD):
                        last = feature_product(n, out, m, k)
                if 1 in part:
                    last.then_inc(piece_used, 1)

            def back(n, st, start, stop, part=range(8)):
                if 0 in part:
                    ready(n)
                if stop:
                    order = [(m, c, nh) for c in range(TT) for nh in range(2) for m in range(2)]
                else:
                    order = [(m, c, nh) for m in range(2) for c in range(TT) for nh in range(2)]
                for m, c, nh in (order[i] for i in part):
                    h, l = st(m)
                    last = mm3(bank[2 * c + nh][:, :], (h[:, c * P:(c + 1) * P], l[:, c * P:(c + 1) * P]),
                               w(n, m, slice(nh * 512, (nh + 1) * 512), 1024), start and m == 0, stop and m == 1)
                    if stop and m == 1 and (c, nh) != (1, 1):
                        last.then_inc(y_ps, 1)
                if 7 in part:
                    last.then_inc(piece_used, 1)

            def norm_t(q):
                for c in range(TT):
                    for k in range(KD):
                        pe.wait_ge(xn_ready, 4 * q + 2 * c + k // 4 + 1)
                        b, o, _ = xt_bank(q, k)
                        last = T.transpose(bank[b][:, o + c * P:o + (c + 1) * P], xn[:, c, k * P:(k + 1) * P], ident)
                        if c == TT - 1:
                            last.then_inc(xt_ps, 1)

            pe.wait_ge(params_in, 16)
            pe.wait_ge(rows_in, 16 * 2)
            pe.wait_ge(pool_set, 5)
            T.matmul(bank[2][0:H, :], table[:, :], onehot, start=True, stop=True).then_inc(strip_ps, 1)

            norm_t(0)
            for i in range(2):
                wide(At(N_KVC + i), 4 * i, (bank[0], bank[1]), 0)
            pe.wait_ge(small_lo, 2)
            for k in range(KD):
                last = mm3(bank[6][0:NB, 0:S], (gwh[:, k, :], gwl[:, k, :]), xt_all(k), k == 0, k == KD - 1)
            last.then_inc(gate_ps, 1)
            pe.wait_ge(kvc_ready, 2)
            pe.wait_ge(strip_ready, 1)
            for i in range(8):
                for c in range(TT):
                    o = (i % 2) * S + c * P
                    last = T.transpose(bank[i // 2][:, o:o + P], xn[:, c, i * P:(i + 1) * P], ident)
                if i % 2:
                    last.then_inc(kvt_ps, 1)
            pe.wait_ge(gate_exp, 1)
            for c in range(TT):
                last = T.transpose(bank[7][:, c * 64:c * 64 + NB], gx[:, c * P:(c + 1) * P], par[0:NB, NPCOL + 128:NPCOL + 128 + NB])
            last.then_inc(gate_t, 1)
            for i in range(2):
                wide(At(N_ATT[0] + i), 4 * i, (bank[4], bank[5]))

            def hidden_t(kv):
                pe.wait_ge(silu_ready, kv + 1)
                for m in range(2):
                    last = T.transpose(bank[6 + kv][:, 256 + 64 * m:256 + 64 * m + G * NCMP], hid[:, kv, m * P:(m + 1) * P],
                                       par[0:G * NCMP, NPCOL + 128:NPCOL + 128 + G * NCMP])
                last.then_inc(hid_ps, 1)

            for kv in range(2):
                pe.wait_ge(blk_lo, kv + 1)
                if kv:
                    pe.wait_ge(gate_ready, 1)
                for i in range(2):
                    n = At(N_W1 + 2 * kv + i)
                    ready(n)
                    for j in range(8):
                        jj = 8 * i + j
                        last = mm3(bank[6 + kv][0:G * NCMP, 0:HID], (blkh[:, kv, jj, :], blkl[:, kv, jj, :]),
                                   w(n, j, slice(0, HID), HID), jj == 0, jj == 15)
                    last.then_inc(piece_used, 1)
                    if kv and i == 0:
                        hidden_t(0)
            qk_transposes(0)
            pe.wait_ge(blk_ready, 16)
            pe.wait_ge(hid_ready, 1)
            pe.wait_ge(rest_in, 16 * 4)
            for m in range(2):
                last = T.matmul(bank[0][0:G * NCMP, 0:DH], hidk[:, m, :], w2[:, 0, m, :], start=m == 0, stop=m == 1)
            last.then_inc(cmp_ps, 1)
            hidden_t(1)
            pe.wait_ge(hid_ready, 3)
            for g in range(G):
                for m in range(2):
                    last = T.matmul(bank[1][:, g * DH:(g + 1) * DH], hidv[:, m, g, :], w2[:, 1, m, :], start=m == 0, stop=m == 1)
            last.then_inc(cmp_ps, 1)
            pe.wait_ge(kt_ready, 1)
            pe.wait_ge(qt_ready, 1)
            wide(At(N_ATT[1]), 0, (bank[4], bank[5]), part=range(2))
            pe.wait_ge(kcn_ready, 2)
            T.transpose(bank[2][:, 0:G * NCMP], kcn.rearrange("p b d -> p (b d)"),
                        par[0:G * NCMP, NPCOL + 128:NPCOL + 128 + G * NCMP]).then_inc(kct_ps, 1)

            def scores(g, i):
                h, t, n = i // 2, i % 2, 8 * g + i
                nk = P * (t + 1)
                if n >= 2:
                    pe.wait_ge(sm_max, 2 * n - 2)
                pr, b = h // 2, h % 2
                part = slice(b * DH, (b + 1) * DH)
                T.matmul(bank[t][:, 0:2 * nk], qt[part, pr * S + t * P:pr * S + (t + 1) * P], kt[part, :, 0:nk],
                         start=True, stop=True).then_inc(sc_ps, 1)

            def probs_t(g, i):
                h, t, n = i // 2, i % 2, 8 * g + i
                m = 4 * g + h
                pe.wait_ge(p_ready, 2 * n + 2)
                if t == 0 and m:
                    pe.wait_ge(pt_ready, 2 * m)
                for b in range(2):
                    for kk in range(t + 1):
                        o = (t + kk) * P
                        last = T.transpose(bank[2 + b][:, o:o + P], probs[:, t, b * S + kk * P:b * S + (kk + 1) * P], ident)
                last.then_inc(pt_ps, 1)

            def values(m):
                g, h = m // 4, m % 4
                pr, b = h // 2, h % 2
                pe.wait_ge(pt_ready, 2 * (m + 1))
                if h == 0:
                    pe.wait_ge(v_ready, 2 * (g + 1))
                    pe.wait_ge(pct_ready, g + 1)
                if m >= 2 and h % 2 == 0:
                    pe.wait_ge(ot_lo, m // 2)
                out = bank[7][b * DH:(b + 1) * DH, pr * S:(pr + 1) * S]
                for s in range(2):
                    v = 384 + 192 * s
                    T.matmul(out, qkv[:, g % 2, 0, v:v + DH], pt[:, m % 2, s, 0:S], start=s == 0, stop=False)
                    T.matmul(out[:, P:S], qkv[:, g % 2, 1, v:v + DH], pt[:, m % 2, s, S:TW], start=False, stop=False)
                T.matmul(out, vcmp[32 * h:32 * h + 32, g, :], pct[32 * h:32 * h + 32, :], start=False, stop=True).then_inc(pv_done, 1)

            pe.wait_ge(kt_ready, 1)
            pe.wait_ge(qt_ready, 1)
            pe.wait_ge(vcmp_ready, 1)
            scores(0, 0)
            scores(0, 1)
            compressed_scores(0)
            for g in range(G):
                for i in range(8):
                    n = 8 * g + i
                    if g < G - 1:
                        for k in FILL.get(i, ()):
                            if g or k != 1:
                                wide(At(N_ATT[g + 1] + k // 4), k // 4 * 4, (bank[4], bank[5]), part=(k % 4,))
                    elif i < 3:
                        attention_out(0, 0, (i + 1,))
                    if g == G - 1 and i in (3, 4):
                        attention_out(0, 1, (i - 3,))
                    if i == 7 and g < G - 1:
                        pe.wait_ge(kt_ready, g + 2)
                        pe.wait_ge(qt_ready, g + 2)
                        if g < G - 2:
                            wide(At(N_ATT[g + 2]), 0, (bank[4], bank[5]), part=(0,))
                        else:
                            attention_out(0, 0, (0,))
                    if i == 1:
                        pe.wait_ge(pc_ready, g + 1)
                        for c in range(TT):
                            last = T.transpose(bank[6][:, S + c * P:S + (c + 1) * P],
                                               pc[:, 1 - c, :, :].rearrange("p h n -> p (h n)"), ident)
                        last.then_inc(pct_ps, 1)
                    if i != 6 and n + 2 < 8 * G:
                        scores((n + 2) // 8, (i + 2) % 8)
                    probs_t(g, i)
                    if i == 6 and g < G - 1:
                        qk_transposes(g + 1)
                    if n and i % 2 == 0:
                        values(n // 2 - 1)
                    if i == 6 and g < G - 1:
                        pe.wait_ge(kt_ready, g + 2)
                        pe.wait_ge(qt_ready, g + 2)
                        scores(g + 1, 0)
                    if i == 7 and g < G - 1:
                        compressed_scores(g + 1)
            values(4 * G - 1)
            pe.wait_ge(ot_lo, 2 * G)
            attention_out(0, 1, (2, 3))
            attention_out(1, 0)
            attention_out(1, 1)

            def mlp(layer, base):
                def up(j, n, half, part=range(2)):
                    if layer or j.s >= 2:
                        pe.wait_ge(sq_ready, j.n(2, 2 * MJ * layer + half - 3))
                    features(n + half, bank[4 + 2 * (j.s % 2) + half], part)

                def down(j, n, start=False, stop=False):
                    for half in range(2):
                        pe.wait_ge(hid_lo, j.n(2, 2 * MJ * layer + half + 1))
                        back(n + half, lambda m, half=half: (hth[:, j.s % 2, 2 * half + m, :], htl[:, j.s % 2, 2 * half + m, :]),
                             start and half == 0, stop and half == 1)
                ready(At(base + 1))
                for k in range(KD):
                    pe.wait_ge(xt_lo, 16 * layer + 8 + k + 1)
                    for half in range(2):
                        feature_product(At(base + half), bank[4 + half], 0, k)
                for half in range(2):
                    up(At(0), At(base), half, (1,))
                for half in range(2):
                    up(At(1), At(base + 2), half)
                down(At(0), At(base + 4), start=True)
                with pe.Fori(0, (MJ - 2) // 2) as it:
                    for u in range(2):
                        j, n = At(1 + u, it, 2), At(base + 6 + 4 * u, it, 8)
                        for half in range(2):
                            up(j + 1, n, half)
                        down(j, n + 2)
                down(At(MJ - 1), At(base + 4 * MJ - 2), stop=True)

            norm_t(1)
            mlp(0, N_MLP0)

            norm_t(2)
            ready(At(N_SSD))
            for k in range(KD):
                pe.wait_ge(xt_lo, 16 + k + 1)
                feature_product(At(N_SSD), bank[4], 0, k)
                last = mm3(bank[5][0:SH, 0:S], (dwh[:, k, :], dwl[:, k, :]), xt_all(k), k == 0, k == KD - 1)
            last.then_inc(dt_raw, 1)
            features(At(N_SSD), bank[4], part=(1,))
            pe.wait_ge(dt_raw_out, 1)
            for c in range(TT):
                last = T.transpose(bank[6][:, S + c * SH:S + (c + 1) * SH], acst[:, c * P:(c + 1) * P],
                                   par[0:SH, NPCOL + 128:NPCOL + 128 + SH])
            last.then_inc(dt_ps, 1)
            features(At(N_SSD + 1), bank[5])
            pe.wait_ge(dt_ready, 1)
            for c in range(TT):
                T.matmul(bank[6][:, 64 + c * SH:64 + (c + 1) * SH], tri, dta[:, c, :], start=True, stop=True)
            T.matmul(bank[6][:, 128:160], ones[:, :], dta[:, 0, :], start=True, stop=True).then_inc(acs_ps, 1)
            pe.wait_ge(acs_ready, 1)
            for c in range(TT):
                last = T.transpose(bank[7][0:SH, c * P:(c + 1) * P], acs[:, c, :], ident)
            last.then_inc(acst_ps, 1)
            pe.wait_ge(acs_ready, 2)

            def gate_cols(n):
                ready(n)
                for c in range(TT):
                    for k in range(KD):
                        last = mm3(bank[6][:, c * S:(c + 1) * S], xt(k, c), w(n, k, slice(0, 256), 256), k == 0, k == KD - 1)
                last.then_inc(piece_used, 1)
            gate_cols(At(N_SSD + 2))

            def ssd_back(g, n, start=False, stop=False, part=range(8)):
                pe.wait_ge(yt_lo, g.n(2, 2))
                back(n, lambda m: (yth[:, m, :], ytl[:, m, :]), start, stop, part)

            def ssd(g, n, last_group=False):
                par = g.s % 2
                pe.wait_ge(xc_ready, g.n(2, 1))
                if g.s == 0:
                    pe.wait_ge(acst_ready, 1)
                else:
                    pe.wait_ge(yt_lo, g.n(2))
                for c in range(TT):
                    for q in range(2):
                        last = T.transpose(bank[7][:, c * S + q * P:c * S + (q + 1) * P], xc[:, par, q, c * P:(c + 1) * P], ident)
                last.then_inc(t_ps, 1)
                if last_group:
                    ssd_back(g + (-1), At(N_MLP1 - 2), part=range(2))
                elif g.s:
                    ssd_back(g + (-1), n + (-1), start=g.s == 1 and g.it is None)
                pe.wait_ge(xc_ready, g.n(2, 2))
                pe.wait_ge(z_ready, g.n(1, 1))
                T.transpose(bank[6][:, 2 * P:3 * P], xc[:, par, 2, 0:P], ident)
                for c in range(TT):
                    last = T.matmul(bank[6][:, c * P:(c + 1) * P], xc[:, par, 2, c * P:(c + 1) * P],
                                    xc[:, par, 3, c * P:(c + 1) * P], start=True, stop=True)
                last.then_inc(t_ps, 1)
                if last_group:
                    ssd_back(g + (-1), At(N_MLP1 - 2), part=range(2, 5))
                else:
                    pe.wait_ge(conv_in, g.n(2, 1))
                    features(n, bank[4])
                pe.wait_ge(xw_ready, g.n(1, 1))
                pe.wait_ge(bn_ready, g.n(1, 1))
                T.matmul(bank[7][:, 0:S], bn[:, :], xw[:, :], start=True, stop=True).then_inc(s_ps, 1)
                pe.wait_ge(m_ready, g.n(8, 8))
                for c in range(TT):
                    for h in range(4):
                        o = c * S + h * DH
                        T.matmul(bank[6][:, o:o + DH], eb[:, c, h, :], xsn[:, c, h * DH:(h + 1) * DH], start=True, stop=True)
                pe.wait_ge(prev_ready, g.n(1, 1))
                T.matmul(bank[7][:, S:2 * S], xc[:, par, 3, P:2 * P], prev[:, :], start=True, stop=True).then_inc(ys_ps, 1)
                if not last_group:
                    pe.wait_ge(conv_in, g.n(2, 2))
                    features(n + 1, bank[5])
                else:
                    ssd_back(g + (-1), At(N_MLP1 - 2), part=range(5, 8))
                pe.wait_ge(yn_ready, g.n(2, 2))
                for q in range(2):
                    for c in range(TT):
                        last = T.transpose(bank[7][:, q * S + c * P:q * S + (c + 1) * P], y[:, c, q * P:(q + 1) * P], ident)
                last.then_inc(yt_ps, 1)
                if not last_group:
                    gate_cols(n + 2)

            ssd(At(0), At(N_SSD + 3))
            ssd(At(1), At(N_SSD + 7))
            with pe.Fori(0, (SG - 4) // 2) as it:
                for u in range(2):
                    ssd(At(2 + u, it, 2), At(N_SSD + 11 + 4 * u, it, 8))
            ssd(At(SG - 2), At(N_SSD + 7 + 4 * (SG - 3)))
            ssd(At(SG - 1), None, last_group=True)
            ssd_back(At(SG - 1), At(N_MLP1 - 1), stop=True)

            norm_t(3)
            mlp(1, N_MLP1)


def constants():
    tri = np.triu(np.ones((P, P), np.float32))
    dist = 255 - np.arange(512)
    far = BUCKETS // 2 + (np.log(np.maximum(dist, 1) / (BUCKETS // 2)) / np.log(128 / (BUCKETS // 2))
                          * (BUCKETS - BUCKETS // 2)).astype(np.int64)
    bucket = np.where(dist < BUCKETS // 2, np.maximum(dist, 0), np.minimum(far, BUCKETS - 1))
    bucket[dist < 0] = BUCKETS
    onehot = np.zeros((BUCKETS + 1, 512), np.float32)
    onehot[bucket, np.arange(512)] = 1.0
    return np.eye(P, dtype=np.float32), tri, np.where(tri > 0, 0.0, NEG).astype(np.float32), onehot


def tiles(w):
    return w.reshape(-1, P, w.shape[1]).transpose(1, 0, 2).reshape(P, -1)


def stream(t):
    out = []
    w = t["nsa_w_in"][0]
    for k in range(2):
        out.append(tiles(w[k * 512:(k + 1) * 512, QC:QC + 512]))
    for g in range(G):
        starts = [g * 256] + [QC + 512 + b * 256 + g * DH for b in (0, 2, 1, 3)]
        cols = np.concatenate([w[:, c:c + n] for c, n in zip(starts, (256, DH, DH, DH, DH))], axis=1)
        out += [tiles(cols[:512]), tiles(cols[512:])]
        if g == 0:
            for name in ("cmp_w1_k", "cmp_w1_v"):
                w1 = t[name][0].reshape(CB * DH, HID)
                out += [tiles(w1[:1024]), tiles(w1[1024:])]
    wo = t["nsa_w_out"][0]
    out += [tiles(wo[k * 512:(k + 1) * 512, n * 512:(n + 1) * 512]) for n in range(2) for k in range(2)]

    def mlp(layer):
        up, down = t["mlp_w_up"][layer], t["mlp_w_down"][layer]
        ups = [tiles(up[:, i * 256:(i + 1) * 256]) for i in range(2 * MJ)]
        downs = [tiles(down[i * 256:(i + 1) * 256]) for i in range(2 * MJ)]
        seq = ups[:2]
        for j in range(MJ):
            seq += ups[2 * j + 2:2 * j + 4] + downs[2 * j:2 * j + 2]
        return seq

    out += mlp(0)
    w, back = t["ssd_w_in"][0], t["ssd_w_out"][0]
    for g in range(SG + 1):
        if g >= 2:
            out.append(tiles(back[(g - 2) * 256:(g - 1) * 256]))
        if g < SG:
            b0 = XBC0 + DI + g * 128
            bc = np.concatenate([w[:, b0:b0 + 128], w[:, b0 + SG * 128:b0 + SG * 128 + 128]], axis=1)
            out += [tiles(w[:, XBC0 + g * 256:XBC0 + (g + 1) * 256]), tiles(bc), tiles(w[:, g * 256:(g + 1) * 256])]
    out.append(tiles(back[(SG - 1) * 256:]))
    out += mlp(1)
    return np.stack(out)


def kernel(**inputs):
    import concourse.bacc as bacc
    from concourse.bass_utils import run_bass_kernel_spmd

    t = {name: np.asarray(v) for name, v in inputs.items()}
    eye, tri, segmask, onehot = constants()

    def cols(v):
        return v.reshape(-1, P).T

    params = np.concatenate(
        [cols(t["norm_mix_w"]), cols(t["norm_mlp_w"]), cols(t["ssd_norm_w"]), cols(t["ssd_conv_b"]),
         cols(t["cmp_pe_k"]), cols(t["cmp_pe_v"]), cols(np.concatenate([t["nsa_q_gain"]] * 2)),
         cols(np.concatenate([t["nsa_k_gain"]] * 2)), cols(t["ssd_conv_w"]), eye, tri, segmask], axis=1)
    small_w = np.concatenate(
        [tiles(t["cmp_w2_k"][0]), tiles(t["cmp_w2_v"][0]), tiles(t["ssd_w_in"][0][:, DT0:DT0 + SH]),
         tiles(t["nsa_w_in"][0][:, GATE0:GATE0 + NB])], axis=1)
    given = {"x": t["x"], "stream": stream(t), "params": params, "small_w": small_w, "rel_table": t["rel_table"],
             "onehot": onehot, "ssd_dt_bias": t["ssd_dt_bias"], "ssd_a_log": t["ssd_a_log"], "ssd_d": t["ssd_d"]}

    nc = bacc.Bacc("TRN2", target_bir_lowering=False, num_devices=1)
    arrays, aps = {}, {}
    for name, v in given.items():
        arrays[f"in_{name}"] = np.ascontiguousarray(v)
        aps[name] = nc.dram_tensor(f"in_{name}", v.shape, mybir.dt.from_np(v.dtype), kind="ExternalInput").ap()
    aps["out"] = nc.dram_tensor("out", (1, S, D), F32, kind="ExternalOutput").ap()
    build(nc, aps)
    r = run_bass_kernel_spmd(nc, [arrays], core_ids=[0])
    return r.results[0]["out"]
```
